# Optimizing a Trainium2 kernel written in Bass

```python
import math
import jax
import jax.numpy as jnp
from jax import lax
import numpy as np

D_MODEL = 1024
BATCH = 1
SEQ = 1024
DEPTH = 2
DEC_BATCH = 8
DEC_SEQ = 4
PAST_LEN = 1024
PAGE_SIZE = 128

N_EVEN = (DEPTH + 1) // 2
N_ODD = DEPTH // 2
S5_WIDTH = D_MODEL // 2
S5_GROUP = 16
S5_GROUPS = S5_WIDTH // S5_GROUP
S5_STATE = 64
SWA_WIDTH = D_MODEL // 2
SWA_HEAD_DIM = 64
SWA_HEADS = SWA_WIDTH // SWA_HEAD_DIM
SWA_KV_HEADS = 2
SWA_GROUP = SWA_HEADS // SWA_KV_HEADS
WINDOW = 128
T5_BUCKETS = 32
T5_MAX_DIST = 128
HGRN_HEADS = 8
HGRN_DK = 128
HGRN_DV = D_MODEL // HGRN_HEADS
HGRN_CHUNK = 64
D_FF = 4 * D_MODEL
EVEN_IN = S5_WIDTH + SWA_WIDTH + 2 * SWA_KV_HEADS * SWA_HEAD_DIM
ODD_IN = 2 * HGRN_HEADS * HGRN_DK + 2 * HGRN_HEADS * HGRN_DV
RMS_EPS = 1e-6
NEG_INF = -1e30
LOG_FLOOR = 1e-30

kernel_name = 'hybrid_s5_swa_hgrn2_decode_step'

def rms_norm(x, w):
    xf = x.astype(jnp.float32)
    y = xf * lax.rsqrt(jnp.mean(xf * xf, axis=-1, keepdims=True) + RMS_EPS) * w.astype(jnp.float32)
    return y.astype(x.dtype)

def t5_bias(table, dist):
    n = jnp.maximum(dist, 0)
    max_exact = T5_BUCKETS // 2
    large = max_exact + (jnp.log(jnp.maximum(n, max_exact).astype(jnp.float32) / max_exact)
                         / math.log(T5_MAX_DIST / max_exact) * (T5_BUCKETS - max_exact)).astype(jnp.int32)
    large = jnp.minimum(large, T5_BUCKETS - 1)
    bucket = jnp.where(n < max_exact, n, large)
    bias = table.astype(jnp.float32)[bucket]
    return jnp.moveaxis(bias, -1, 0).reshape(SWA_KV_HEADS, SWA_GROUP, *dist.shape)

def sink_attention(q, k, v, bias, mask, sinks):
    f32 = jnp.float32
    s = jnp.einsum('bnqkgd,bnskd->bnkgqs', q.astype(f32), k.astype(f32)) * (SWA_HEAD_DIM ** -0.5)
    s = jnp.where(mask[None, :, None, None], s + bias[None, None], NEG_INF)
    sink = jnp.broadcast_to(sinks.astype(f32).reshape(SWA_KV_HEADS, SWA_GROUP)[None, None, :, :, None, None],
                            s.shape[:-1] + (1,))
    p = jax.nn.softmax(jnp.concatenate([s, sink], axis=-1), axis=-1)[..., :-1]
    return jnp.einsum('bnkgqs,bnskd->bnqkgd', p, v.astype(f32))

def swa_prompt(q, k, v, sinks, table):
    bt, L, _ = q.shape
    nb = L // WINDOW
    qb = q.reshape(bt, nb, WINDOW, SWA_KV_HEADS, SWA_GROUP, SWA_HEAD_DIM)
    kb = k.reshape(bt, nb, WINDOW, SWA_KV_HEADS, SWA_HEAD_DIM)
    vb = v.reshape(bt, nb, WINDOW, SWA_KV_HEADS, SWA_HEAD_DIM)

    def band(t):
        prev = jnp.concatenate([jnp.zeros_like(t[:, :1]), t[:, :-1]], axis=1)
        return jnp.concatenate([prev, t], axis=2)

    t_idx = jnp.arange(WINDOW)[:, None]
    m_idx = jnp.arange(2 * WINDOW)[None, :]
    dist = WINDOW + t_idx - m_idx
    in_win = (dist >= 0) & (dist < WINDOW)
    blk = jnp.arange(nb)[:, None, None]
    mask = in_win[None] & ((blk > 0) | (m_idx[None] >= WINDOW))
    o = sink_attention(qb, band(kb), band(vb), t5_bias(table, dist), mask, sinks)
    w = min(WINDOW, L)
    return o.reshape(bt, L, SWA_HEADS * SWA_HEAD_DIM), k[:, L - w:], v[:, L - w:]

def swa_sample(q, k, v, cache_k, cache_v, sinks, table):
    bt, L, _ = q.shape
    wc = cache_k.shape[1]
    kk = jnp.concatenate([cache_k, k.astype(cache_k.dtype)], axis=1)
    vv = jnp.concatenate([cache_v, v.astype(cache_v.dtype)], axis=1)
    dist = wc + jnp.arange(L)[:, None] - jnp.arange(wc + L)[None, :]
    mask = ((dist >= 0) & (dist < WINDOW))[None]
    qb = q.reshape(bt, 1, L, SWA_KV_HEADS, SWA_GROUP, SWA_HEAD_DIM)
    o = sink_attention(qb, kk[:, None], vv[:, None], t5_bias(table, dist), mask, sinks)
    return o.reshape(bt, L, SWA_HEADS * SWA_HEAD_DIM), kk[:, L:], vv[:, L:]

def s5_mixer(u, h0_re, h0_im, lam_re, lam_im, log_step, b_re, b_im, c_re, c_im, d_skip, w_glu):
    f32 = jnp.float32
    bt, L, _ = u.shape
    uf = u.astype(f32)
    ug = uf.reshape(bt, L, S5_GROUPS, S5_GROUP)
    lam_re = lam_re.astype(f32)
    lam_im = lam_im.astype(f32)
    dt = jnp.exp(log_step.astype(f32))[:, None]
    mag = jnp.exp(lam_re * dt)
    ang = lam_im * dt
    abar_re = mag * jnp.cos(ang)
    abar_im = mag * jnp.sin(ang)
    den = lam_re * lam_re + lam_im * lam_im
    nr = abar_re - 1.0
    coef_re = ((nr * lam_re + abar_im * lam_im) / den)[..., None]
    coef_im = ((abar_im * lam_re - nr * lam_im) / den)[..., None]
    b_re = b_re.astype(f32)
    b_im = b_im.astype(f32)
    bb_re = coef_re * b_re - coef_im * b_im
    bb_im = coef_re * b_im + coef_im * b_re
    bu_re = jnp.einsum('blgc,gpc->blgp', ug, bb_re)
    bu_im = jnp.einsum('blgc,gpc->blgp', ug, bb_im)
    h0_re = h0_re.astype(f32)
    h0_im = h0_im.astype(f32)
    bu_re = bu_re.at[:, 0].add(abar_re * h0_re - abar_im * h0_im)
    bu_im = bu_im.at[:, 0].add(abar_re * h0_im + abar_im * h0_re)
    a_re = jnp.broadcast_to(abar_re, bu_re.shape)
    a_im = jnp.broadcast_to(abar_im, bu_im.shape)

    def combine(e1, e2):
        a1r, a1i, b1r, b1i = e1
        a2r, a2i, b2r, b2i = e2
        return (a1r * a2r - a1i * a2i, a1r * a2i + a1i * a2r,
                a2r * b1r - a2i * b1i + b2r, a2r * b1i + a2i * b1r + b2i)

    _, _, h_re, h_im = lax.associative_scan(combine, (a_re, a_im, bu_re, bu_im), axis=1)
    y = (jnp.einsum('gcp,blgp->blgc', c_re.astype(f32), h_re)
         - jnp.einsum('gcp,blgp->blgc', c_im.astype(f32), h_im)).reshape(bt, L, S5_WIDTH)
    y = y + d_skip.astype(f32) * uf
    g = jax.nn.gelu(y)
    out = g * jax.nn.sigmoid(g @ w_glu.astype(f32))
    return out.astype(u.dtype), h_re[:, -1], h_im[:, -1]

def hgrn2_mixer(q, fz, iv, gz, lb, s0, gnorm_w):
    f32 = jnp.float32
    bt, L, _ = q.shape
    lb = lb.astype(f32)
    fzf = fz.astype(f32)
    qf = jax.nn.silu(q.astype(f32))
    log_f = jnp.logaddexp(jnp.log(jnp.maximum(lb, LOG_FLOOR)), jnp.log1p(-lb) + jax.nn.log_sigmoid(fzf))
    kf = (1.0 - lb) * jax.nn.sigmoid(-fzf)
    vf = iv.astype(f32)
    c = min(HGRN_CHUNK, L)
    nc = -(-L // c)
    pad = nc * c - L

    def chunked(t, dim):
        t = t.reshape(bt, L, HGRN_HEADS, dim)
        t = jnp.pad(t, ((0, 0), (0, pad), (0, 0), (0, 0)))
        return jnp.moveaxis(t.reshape(bt, nc, c, HGRN_HEADS, dim), 1, 0)

    xs = (chunked(qf, HGRN_DK), chunked(kf, HGRN_DK), chunked(log_f, HGRN_DK), chunked(vf, HGRN_DV))
    causal = jnp.tril(jnp.ones((c, c), dtype=bool))[None, :, :, None, None]

    def step(S, inp):
        qc, kc, gc, vc = inp
        b = jnp.cumsum(gc, axis=1)
        diff = b[:, :, None] - b[:, None, :]
        decay = jnp.exp(jnp.where(causal, diff, NEG_INF))
        scores = jnp.einsum('bthd,bshd,btshd->bhts', qc, kc, decay)
        o = (jnp.einsum('bhts,bshv->bthv', scores, vc)
             + jnp.einsum('bthd,bhdv->bthv', qc * jnp.exp(b), S))
        b_last = b[:, -1]
        S = (jnp.exp(b_last)[..., None] * S
             + jnp.einsum('bshd,bshv->bhdv', kc * jnp.exp(b_last[:, None] - b), vc))
        return S, o

    s_fin, o = lax.scan(step, s0.astype(f32), xs)
    o = jnp.moveaxis(o, 0, 1).reshape(bt, nc * c, HGRN_HEADS, HGRN_DV)[:, :L]
    o = o * lax.rsqrt(jnp.mean(o * o, axis=-1, keepdims=True) + RMS_EPS) * gnorm_w.astype(f32)
    o = o * jax.nn.silu(gz.astype(f32).reshape(bt, L, HGRN_HEADS, HGRN_DV))
    return o.reshape(bt, L, HGRN_HEADS * HGRN_DV).astype(q.dtype), s_fin

def trunk(x, cache_k, cache_v, st_re, st_im, st_h, p):
    prompt = cache_k is None
    bt, L, _ = x.shape
    sm = jax.nn.softmax(p['hgrn_lb_param'].astype(jnp.float32), axis=0)
    lower_bounds = jnp.cumsum(sm, axis=0) - sm[0]
    k_out, v_out, re_out, im_out, h_out = [], [], [], [], []
    split_even = [S5_WIDTH, S5_WIDTH + SWA_WIDTH, S5_WIDTH + SWA_WIDTH + SWA_KV_HEADS * SWA_HEAD_DIM]
    qk_w = HGRN_HEADS * HGRN_DK
    split_odd = [qk_w, 2 * qk_w, 2 * qk_w + HGRN_HEADS * HGRN_DV]
    for layer in range(DEPTH):
        idx = layer // 2
        h = rms_norm(x, p['norm_mix_pre'][layer])
        if layer % 2 == 0:
            proj = h @ p['w_in_even'][idx]
            u, q, k, v = jnp.split(proj, split_even, axis=-1)
            if prompt:
                h0_re = jnp.zeros((bt, S5_GROUPS, S5_STATE), jnp.float32)
                h0_im = jnp.zeros((bt, S5_GROUPS, S5_STATE), jnp.float32)
            else:
                h0_re, h0_im = st_re[idx], st_im[idx]
            a_out, h_re, h_im = s5_mixer(u, h0_re, h0_im, p['s5_lambda_re'][idx], p['s5_lambda_im'][idx],
                                         p['s5_log_step'][idx], p['s5_b_re'][idx], p['s5_b_im'][idx],
                                         p['s5_c_re'][idx], p['s5_c_im'][idx], p['s5_d'][idx],
                                         p['s5_w_glu'][idx])
            k = k.reshape(bt, L, SWA_KV_HEADS, SWA_HEAD_DIM)
            v = v.reshape(bt, L, SWA_KV_HEADS, SWA_HEAD_DIM)
            if prompt:
                b_out, kw, vw = swa_prompt(q, k, v, p['swa_sinks'][idx], p['t5_bias_table'])
            else:
                b_out, kw, vw = swa_sample(q, k, v, cache_k[idx], cache_v[idx],
                                           p['swa_sinks'][idx], p['t5_bias_table'])
            mix = jnp.concatenate([a_out, b_out.astype(a_out.dtype)], axis=-1) @ p['w_out_even'][idx]
            k_out.append(kw)
            v_out.append(vw)
            re_out.append(h_re.astype(x.dtype))
            im_out.append(h_im.astype(x.dtype))
        else:
            proj = h @ p['w_in_odd'][idx]
            q, fz, iv, gz = jnp.split(proj, split_odd, axis=-1)
            if prompt:
                s0 = jnp.zeros((bt, HGRN_HEADS, HGRN_DK, HGRN_DV), jnp.float32)
            else:
                s0 = st_h[idx]
            c_out, s_new = hgrn2_mixer(q, fz, iv, gz, lower_bounds[idx], s0, p['hgrn_gnorm'][idx])
            mix = c_out @ p['w_out_odd'][idx]
            h_out.append(s_new.astype(x.dtype))
        x = x + rms_norm(mix, p['norm_mix_post'][layer])
        h = rms_norm(x, p['norm_mlp_pre'][layer])
        h = jnp.square(jax.nn.relu(h @ p['w_up'][layer])) @ p['w_down'][layer]
        x = x + rms_norm(h, p['norm_mlp_post'][layer])
    return x, jnp.stack(k_out), jnp.stack(v_out), jnp.stack(re_out), jnp.stack(im_out), jnp.stack(h_out)

def setup_inputs(seed: int = 0) -> dict:
    key = jax.random.key(seed)
    keys = iter(jax.random.split(key, 40))
    f32 = jnp.float32

    def normal(shape, scale):
        return jax.random.normal(next(keys), shape, f32) * scale

    def gain(shape):
        return 1.0 + normal(shape, 0.02)

    sw = min(WINDOW, PAST_LEN)
    n_idx = jnp.arange(S5_STATE, dtype=f32)
    mix_w = S5_WIDTH + SWA_WIDTH
    return {
        'x_prompt': normal((BATCH, SEQ, D_MODEL), 1.0),
        'x_sample': normal((DEC_BATCH, DEC_SEQ, D_MODEL), 1.0),
        'cache_swa_k': normal((N_EVEN, DEC_BATCH, sw, SWA_KV_HEADS, SWA_HEAD_DIM), 1.0),
        'cache_swa_v': normal((N_EVEN, DEC_BATCH, sw, SWA_KV_HEADS, SWA_HEAD_DIM), 1.0),
        'state_s5_re': normal((N_EVEN, DEC_BATCH, S5_GROUPS, S5_STATE), 0.5),
        'state_s5_im': normal((N_EVEN, DEC_BATCH, S5_GROUPS, S5_STATE), 0.5),
        'state_hgrn': normal((N_ODD, DEC_BATCH, HGRN_HEADS, HGRN_DK, HGRN_DV), 0.5),
        't5_bias_table': normal((T5_BUCKETS, SWA_HEADS), 0.5),
        'norm_mix_pre': gain((DEPTH, D_MODEL)),
        'norm_mix_post': gain((DEPTH, D_MODEL)),
        'norm_mlp_pre': gain((DEPTH, D_MODEL)),
        'norm_mlp_post': gain((DEPTH, D_MODEL)),
        'w_in_even': normal((N_EVEN, D_MODEL, EVEN_IN), D_MODEL ** -0.5),
        'w_out_even': normal((N_EVEN, mix_w, D_MODEL), mix_w ** -0.5),
        's5_lambda_re': -0.5 + normal((N_EVEN, S5_GROUPS, S5_STATE), 0.01),
        's5_lambda_im': math.pi * n_idx + normal((N_EVEN, S5_GROUPS, S5_STATE), 0.01),
        's5_log_step': jax.random.uniform(next(keys), (N_EVEN, S5_GROUPS), f32,
                                          math.log(1e-3), math.log(1e-1)),
        's5_b_re': normal((N_EVEN, S5_GROUPS, S5_STATE, S5_GROUP), (2 * S5_GROUP) ** -0.5),
        's5_b_im': normal((N_EVEN, S5_GROUPS, S5_STATE, S5_GROUP), (2 * S5_GROUP) ** -0.5),
        's5_c_re': normal((N_EVEN, S5_GROUPS, S5_GROUP, S5_STATE), (2 * S5_STATE) ** -0.5),
        's5_c_im': normal((N_EVEN, S5_GROUPS, S5_GROUP, S5_STATE), (2 * S5_STATE) ** -0.5),
        's5_d': normal((N_EVEN, S5_WIDTH), 1.0),
        's5_w_glu': normal((N_EVEN, S5_WIDTH, S5_WIDTH), S5_WIDTH ** -0.5),
        'swa_sinks': normal((N_EVEN, SWA_HEADS), 0.5),
        'w_in_odd': normal((N_ODD, D_MODEL, ODD_IN), D_MODEL ** -0.5),
        'w_out_odd': normal((N_ODD, HGRN_HEADS * HGRN_DV, D_MODEL), (HGRN_HEADS * HGRN_DV) ** -0.5),
        'hgrn_lb_param': normal((N_ODD, HGRN_HEADS * HGRN_DK), 1.0),
        'hgrn_gnorm': gain((N_ODD, HGRN_DV)),
        'w_up': normal((DEPTH, D_MODEL, D_FF), D_MODEL ** -0.5),
        'w_down': normal((DEPTH, D_FF, D_MODEL), D_FF ** -0.5),
    }

def reference(x_prompt, x_sample, cache_swa_k, cache_swa_v, state_s5_re, state_s5_im, state_hgrn,
              t5_bias_table, norm_mix_pre, norm_mix_post, norm_mlp_pre, norm_mlp_post,
              w_in_even, w_out_even, s5_lambda_re, s5_lambda_im, s5_log_step, s5_b_re, s5_b_im,
              s5_c_re, s5_c_im, s5_d, s5_w_glu, swa_sinks, w_in_odd, w_out_odd, hgrn_lb_param,
              hgrn_gnorm, w_up, w_down):
    params = dict(t5_bias_table=t5_bias_table, norm_mix_pre=norm_mix_pre, norm_mix_post=norm_mix_post,
                  norm_mlp_pre=norm_mlp_pre, norm_mlp_post=norm_mlp_post, w_in_even=w_in_even,
                  w_out_even=w_out_even, s5_lambda_re=s5_lambda_re, s5_lambda_im=s5_lambda_im,
                  s5_log_step=s5_log_step, s5_b_re=s5_b_re, s5_b_im=s5_b_im, s5_c_re=s5_c_re,
                  s5_c_im=s5_c_im, s5_d=s5_d, s5_w_glu=s5_w_glu, swa_sinks=swa_sinks,
                  w_in_odd=w_in_odd, w_out_odd=w_out_odd, hgrn_lb_param=hgrn_lb_param,
                  hgrn_gnorm=hgrn_gnorm, w_up=w_up, w_down=w_down)
    y_prompt, k_p, v_p, re_p, im_p, hg_p = trunk(x_prompt, None, None, None, None, None, params)
    y_sample, k_s, v_s, re_s, im_s, hg_s = trunk(x_sample, cache_swa_k, cache_swa_v, state_s5_re,
                                                 state_s5_im, state_hgrn, params)
    return (y_prompt, y_sample, k_p, v_p, k_s, v_s, re_p, im_p, re_s, im_s, hg_p, hg_s)


_drawn_inputs = setup_inputs


def setup_inputs(seed=0):
    import zlib

    import numpy as np

    out = dict(_drawn_inputs(seed))
    spreads = {}
    factors = {'norm_mix_post': 2.759,
     'norm_mlp_pre': 3.109,
     'norm_mlp_post': 9.662,
     's5_lambda_re': 15.566,
     'swa_sinks': 6.008,
     'hgrn_gnorm': 34.912}
    for name, (base, spread) in spreads.items():
        noise = np.random.default_rng([zlib.crc32(name.encode()), seed]).standard_normal(out[name].shape)
        drawn = base * np.exp(spread * noise) if base else spread * noise
        out[name] = jnp.asarray(drawn.astype(out[name].dtype))
    for name, factor in factors.items():
        out[name] = (out[name] * factor).astype(out[name].dtype)
    return out
```

```python
import math
from contextlib import ExitStack

import numpy as np

import concourse.bass as bass
from concourse import mybir

F32 = mybir.dt.float32
F32R = mybir.dt.float32r
I32 = mybir.dt.int32
U8 = mybir.dt.uint8
ALU = mybir.AluOpType
ACT = mybir.ActivationFunctionType
AX_X = mybir.AxisListType.X

P = 128
D = 1024
KC = D // P
SEQ = 1024
DB, DS = 8, 4
NS = DB * DS
T = SEQ + NS
TT = T // 3
FF = 4 * D
EPS = 1e-6
HID = 4
GROUPS = FF // (HID * P)
LOOKBACK = 2

STREAM = [("in_even", 10, 10), ("glu", 2, 4), ("out_even", 8, 8), ("mlp0", 64, 96),
          ("in_odd", 32, 32), ("out_odd", 8, 8), ("mlp1", 64, 96)]
FIRST_BLOCK, FIRST_UNIT = {}, {}
LOG_FLOOR = 1e-30
ROUND = 1.5 * 2.0 ** 23
TWO_PI = (6.28125, 0.0019350051879882812, 3.0199159819567e-07)
PI_BELOW = 3.14159250259
_b = _u = 0
for _name, _nb, _nu in STREAM:
    FIRST_BLOCK[_name], FIRST_UNIT[_name] = _b, _u
    _b, _u = _b + _nb, _u + _nu
BLOCKS = _b


class Steps:

    def __init__(self, sem, names):
        self.sem, self.names, self.next = sem, list(names), 0
        self.index = {n: i for i, n in enumerate(self.names)}
        assert len(self.index) == len(self.names)

    def prime(self, eng):
        eng.sem_inc(self.sem, len(self.names))

    def at(self, name, turn=0):
        return turn * len(self.names) + (len(self.names) + self.index[name] + 1)

    def done(self, ins, name):
        assert self.names[self.next] == name, (self.names[self.next], name)
        self.next = (self.next + 1) % len(self.names)
        return ins.then_inc(self.sem, 1)

    def wait(self, eng, name, turn=0):
        eng.wait_ge(self.sem, self.at(name, turn))

    def wait_last(self, eng, turn=0):
        eng.wait_ge(self.sem, turn * len(self.names) + (len(self.names) + self.next))


def t3(ap):
    return ap.rearrange("p (a t) -> p a t", a=3)


def build_trunk(nc, io):
    with ExitStack() as ctx:
        BASE = 16512
        W_RAW, W_HI, W_LO = BASE, BASE + 8192, BASE + 16384
        A_HI = BASE + 24576
        A_LO = A_HI + KC * T * 4
        R1 = A_LO + KC * T * 4

        def at(name, shape, offset, dt=F32):
            return nc.alloc_sbuf_tensor_at(name, shape, dt, offset=offset)

        w_raw = at("w_raw", [P, 2, KC * P], W_RAW)
        w_hi = at("w_hi", [P, 2, KC, P], W_HI, F32R)
        w_lo = at("w_lo", [P, 2, KC, P], W_LO, F32R)
        a_hi = at("a_hi", [P, KC, T], A_HI, F32R)
        a_lo = at("a_lo", [P, KC, T], A_LO, F32R)
        h_hi = at("h_hi", [P, HID, T], R1, F32R)
        h_lo = at("h_lo", [P, HID, T], R1 + 16896, F32R)
        y = at("y", [P, KC, T], R1 + 33792)
        x = at("x", [P, KC, T], R1 + 67584)
        rstd = at("rstd", [P, T], R1 + 101376)
        ssq = at("ssq", [P, T], R1 + 105600)
        sq = at("sq", [P, 2, T], R1 + 109824)
        gains = at("gains", [P, 8, KC], R1 + 118272)
        ones = at("ones", [P, P], R1 + 118528)
        CONST_END = R1 + 119040
        assert CONST_END <= nc.sbuf_usable_end

        ps = ctx.enter_context(nc.psum_tensor("ps", [P, 8, 512], F32))

        def sem(name):
            return ctx.enter_context(nc.semaphore(name))

        w_loaded = [sem("w_loaded0"), sem("w_loaded1")]
        hi_made = sem("w_hi_made")
        w_ready = sem("w_ready")
        unit_done = sem("unit_done")
        consts_in = sem("consts_in")
        x_in = [sem(f"x_in{k}") for k in range(KC)]
        x_saved = sem("x_saved")
        y_out = sem("y_out")

        def unit(slot):
            return ps[:, 3 * slot:3 * slot + 3, 0:TT]

        def sp_weights(sp):
            with sp.Fori(0, BLOCKS // 2) as i:
                for b in range(2):
                    sp.wait_ge(w_ready, i * 2 + b + 1)
                    sp.dma_start(w_raw[:, b, :], io["w"][bass.ds(i * 2 + b, 1)].rearrange("a p n -> p (a n)")
                                 ).then_inc(w_loaded[b], 16)

        def pool_split(pool, count, b, turn_of_slot, free_at):
            pool.wait_ge(w_loaded[b], turn_of_slot)
            pool.wait_ge(unit_done, free_at)
            pool.wait_ge(w_ready, count + LOOKBACK)
            hi, lo = (w[:, b].rearrange("p k m -> p (k m)") for w in (w_hi, w_lo))
            pool.tensor_tensor(hi, w_raw[:, b, :], ones[:, 0:1].broadcast_to([P, KC * P]), ALU.mult).then_inc(hi_made, 1)
            pool.wait_ge(hi_made, count + 1)
            pool.tensor_tensor(lo, w_raw[:, b, :], hi.bitcast(F32), ALU.subtract).then_inc(w_ready, 1)

        def pool_weights(pool):
            pool.sem_inc(w_ready, LOOKBACK)
            for name, nb, nu in STREAM:
                n0, u0 = FIRST_BLOCK[name], FIRST_UNIT[name]
                if name.startswith("mlp"):
                    ahead = [-1, 0, 1, 2, 3, 4, 6, 8]
                    with pool.Fori(0, GROUPS) as g:
                        for j in range(8):
                            pool_split(pool, g * 8 + (n0 + j), j % 2, g * 64 + 16 * (n0 // 2 + j // 2 + 1),
                                       g * 12 + (LOOKBACK + u0 + ahead[j]))
                else:
                    per = nu // nb
                    with pool.Fori(0, nb // 2) as i:
                        for b in range(2):
                            pool_split(pool, i * 2 + (n0 + b), b, i * 16 + 16 * (n0 // 2 + 1),
                                       i * (2 * per) + (LOOKBACK + u0 - 1 + b))

        def pe_unit(pe, b, slot, ks, act, ready=None, wk=None):
            tiles = unit(slot)
            for n, k in enumerate(ks):
                if ready:
                    ready(k)
                w = n if wk is None else wk + n
                for t in range(3):
                    cols = slice(t * TT, (t + 1) * TT)
                    for i, (wt, at_) in enumerate(((w_hi, act[0]), (w_hi, act[1]), (w_lo, act[0]))):
                        mm = pe.matmul(tiles[:, t], wt[:, b, w], at_[:, k, cols],
                                       start=(n == 0 and i == 0), stop=(n == len(ks) - 1 and i == 2))
            mm.then_inc(unit_done, 1)

        def pe_projection(pe, name, evacuated, nb=None):
            n0, nb = FIRST_BLOCK[name], nb or dict((s[0], s[1]) for s in STREAM)[name]
            with pe.Fori(0, nb // 2) as i:
                for b in range(2):
                    pe.wait_ge(w_ready, i * 2 + (n0 + b + 1 + LOOKBACK))
                    pe.wait_ge(evacuated, i * 2 + (b + 1))
                    pe_unit(pe, b, b, range(KC), (a_hi, a_lo))

        class Boundary:

            def __init__(self, tag, post, pre):
                self.tag, self.post, self.pre = tag, post, pre
                vec, act = [], []
                if post is not None:
                    vec.append("mean_y")
                    act += ["ln_y", "rstd_y"]
                for k in range(KC):
                    if post is not None:
                        vec += [f"scaled{k}", f"x{k}"]
                    if pre is not None:
                        if k > 0:
                            vec.append(f"lo{k - 1}")
                        act += [f"hi{k}", f"sq{k}"]
                if pre is not None:
                    vec += [f"lo{KC - 1}", "mean_x"]
                    act += ["ln_x", "rstd_x"]
                self.vec = Steps(sem(f"{tag}_vec"), vec)
                self.act = Steps(sem(f"{tag}_act"), act)
                if pre is not None:
                    self.stat_x = sem(f"{tag}_stat_x")
                if post is not None:
                    self.ssq_ready = sem(f"{tag}_ssq_ready")
                    self.stat_y = sem(f"{tag}_stat_y")

            def tensor(self, pe):
                if self.post is not None:
                    pe.wait_ge(self.ssq_ready, 1)
                    for t in range(3):
                        mm = pe.matmul(unit(0)[:, t], ones[:], ssq[:, t * TT:(t + 1) * TT], start=True, stop=True)
                    mm.then_inc(self.stat_y, 1)
                if self.pre is not None:
                    for k in range(KC):
                        self.act.wait(pe, f"sq{k}")
                        for t in range(3):
                            mm = pe.matmul(unit(1)[:, t], ones[:], sq[:, k % 2, t * TT:(t + 1) * TT],
                                           start=(k == 0), stop=(k == KC - 1))
                        mm.then_inc(self.stat_x, 1)
                    self.vec.wait(pe, f"lo{KC - 1}")
                    self.vec.wait(pe, "mean_x")

            def vector(self, dve, x_ready=None):
                v = self.vec
                v.prime(dve)
                if self.post is not None:
                    dve.wait_ge(self.stat_y, 1)
                    v.done(dve.tensor_scalar(t3(ssq[:]), unit(0), 1.0 / D, EPS, ALU.mult, ALU.add), "mean_y")
                    self.act.wait(dve, "rstd_y")
                for k in range(KC):
                    if x_ready:
                        x_ready(dve, k)
                    if self.post is not None:
                        v.done(dve.tensor_tensor(y[:, k], y[:, k], rstd[:], ALU.mult), f"scaled{k}")
                        v.wait(dve, f"scaled{k}")
                        v.done(dve.scalar_tensor_tensor(x[:, k], y[:, k], gains[:, self.post, k:k + 1], x[:, k],
                                                        ALU.mult, ALU.add), f"x{k}")
                    if self.pre is not None and k > 0:
                        self.lo(dve, k - 1)
                if self.pre is not None:
                    self.lo(dve, KC - 1)
                    dve.wait_ge(self.stat_x, KC)
                    v.done(dve.tensor_scalar(t3(ssq[:]), unit(1), 1.0 / D, EPS, ALU.mult, ALU.add), "mean_x")

            def lo(self, dve, k):
                self.act.wait(dve, f"hi{k}")
                self.vec.done(dve.scalar_tensor_tensor(a_lo[:, k], x[:, k], gains[:, self.pre, k:k + 1],
                                                       a_hi[:, k].bitcast(F32), ALU.mult, ALU.subtract), f"lo{k}")

            def scalar(self, act, x_ready=None, on_x=None):
                a = self.act
                a.prime(act)
                if self.post is not None:
                    self.vec.wait(act, "mean_y")
                    self.rsqrt(act, "y")
                for k in range(KC):
                    if x_ready:
                        x_ready(act, k)
                    if self.post is not None:
                        self.vec.wait(act, f"x{k}")
                    if on_x:
                        on_x(act, k)
                    if self.pre is not None:
                        a.done(act.activation(a_hi[:, k], x[:, k], ACT.Copy, scale=gains[:, self.pre, k:k + 1]),
                               f"hi{k}")
                        if k >= 2:
                            act.wait_ge(self.stat_x, k - 1)
                        else:
                            a.wait_last(act)
                        a.done(act.activation(sq[:, k % 2], x[:, k], ACT.Square), f"sq{k}")
                if self.pre is not None:
                    self.vec.wait(act, "mean_x")
                    self.rsqrt(act, "x")

            def rsqrt(self, act, which):
                a = self.act
                a.wait_last(act)
                a.done(act.activation(sq[:, 0], ssq[:], ACT.Ln), f"ln_{which}")
                a.wait_last(act)
                a.done(act.activation(rstd[:], sq[:, 0], ACT.Exp, scale=-0.5), f"rstd_{which}")

        class Mlp:
            def __init__(self, name, before, after):
                self.name, self.before, self.after = name, before, after
                vec = []
                for j in range(HID):
                    vec += [f"scaled{j}", f"squared{j}"] + ([f"lo{j - 1}"] if j else [])
                vec += [f"lo{HID - 1}"] + [f"sum{m}" for m in range(KC)]
                self.vec = Steps(sem(f"{name}_vec"), vec)
                self.act = Steps(sem(f"{name}_act"), [f"hi{j}" for j in range(HID)])
                self.sq_done = sem(f"{name}_squares")
                self.sums = sem(f"{name}_sums")
                self.u0, self.n0 = FIRST_UNIT[name], FIRST_BLOCK[name]

            def tensor(self, pe):
                v = self.vec
                with pe.Fori(0, GROUPS) as g:
                    for j in range(HID):
                        pe.wait_ge(w_ready, g * 8 + (self.n0 + j + 1 + LOOKBACK))
                        if j < 2:
                            v.wait(pe, f"sum{KC - 2 + j}", g - 1)
                        else:
                            v.wait(pe, f"scaled{j - 2}", g)
                        pe_unit(pe, j % 2, j % 2, range(KC), (a_hi, a_lo))
                    for m in range(KC):
                        if m % 2 == 0:
                            pe.wait_ge(w_ready, g * 8 + (self.n0 + 4 + m // 2 + 1 + LOOKBACK))
                        v.wait(pe, f"scaled{m + 2}" if m < 2 else f"sum{m - 2}", g)
                        pe_unit(pe, (m // 2) % 2, m % 2, range(HID), (h_hi, h_lo), wk=4 * (m % 2),
                                ready=(lambda k: v.wait(pe, f"lo{k}", g)) if m == 0 else None)

            def units(self, n, g):
                return g * 12 + (LOOKBACK + self.u0 + n + 1)

            def vec_group(self, dve, g, first, last):
                v, a = self.vec, self.act
                for j in range(HID):
                    dve.wait_ge(unit_done, self.units(j, g))
                    v.wait_last(dve, g)
                    v.done(dve.tensor_tensor(t3(ssq[:]), unit(j % 2), t3(rstd[:]), ALU.mult), f"scaled{j}")
                    v.wait_last(dve, g)
                    v.done(dve.scalar_tensor_tensor(sq[:, j % 2], ssq[:], 0.0, ssq[:], ALU.max, ALU.mult),
                           f"squared{j}")
                    if j:
                        self.lo(dve, g, j - 1)
                self.lo(dve, g, HID - 1)
                for m in range(KC):
                    dve.wait_ge(unit_done, self.units(HID + m, g))
                    v.wait_last(dve, g)
                    if first:
                        ins = dve.tensor_copy(t3(y[:, m]), unit(m % 2))
                    else:
                        ins = dve.tensor_tensor(t3(y[:, m]), unit(m % 2), t3(y[:, m]), ALU.add)
                    v.done(ins, f"sum{m}")
                    if last:
                        sum_squares(dve, m, self.sq_done, self.sums, self.after)

            def lo(self, dve, g, j):
                self.act.wait(dve, f"hi{j}", g)
                self.vec.done(dve.tensor_tensor(h_lo[:, j], sq[:, j % 2], h_hi[:, j].bitcast(F32), ALU.subtract),
                              f"lo{j}")

            def vector(self, dve):
                self.vec.prime(dve)
                self.before.act.wait(dve, "rstd_x")
                self.vec_group(dve, 0, True, False)
                with dve.Fori(1, GROUPS - 1) as g:
                    self.vec_group(dve, g, False, False)
                self.vec_group(dve, GROUPS - 1, False, True)

            def scalar(self, act):
                self.act.prime(act)
                with act.Fori(0, GROUPS) as g:
                    for j in range(HID):
                        self.vec.wait(act, f"squared{j}", g)
                        self.act.done(act.activation(h_hi[:, j], sq[:, j % 2], ACT.Copy), f"hi{j}")
                for m in range(KC):
                    self.vec.wait(act, f"sum{m}", GROUPS - 1)
                    square_y(act, m, self.sq_done, self.sums)

        def square_y(act, m, sq_done, sums):
            if m >= 2:
                act.wait_ge(sums, m - 1)
            act.activation(sq[:, m % 2], y[:, m], ACT.Square).then_inc(sq_done, 1)

        def sum_squares(dve, m, sq_done, sums, after):
            dve.wait_ge(sq_done, m + 1)
            if m == 0:
                ins = dve.tensor_copy(ssq[:], sq[:, 0])
            else:
                dve.wait_ge(sums, m)
                ins = dve.tensor_tensor(ssq[:], ssq[:], sq[:, m % 2], ALU.add)
            ins.then_inc(after.ssq_ready if m == KC - 1 else sums, 1)

        class OutProjection:

            def __init__(self, name, after):
                self.name, self.after = name, after
                self.evacuated = sem(f"{name}_evacuated")
                self.sq_done, self.sums = sem(f"{name}_squares"), sem(f"{name}_sums")

            def tensor(self, pe):
                pe.sem_inc(self.evacuated, LOOKBACK)
                pe_projection(pe, self.name, self.evacuated)

            def vector(self, dve):
                for m in range(KC):
                    dve.wait_ge(unit_done, LOOKBACK + FIRST_UNIT[self.name] + m + 1)
                    dve.tensor_copy(t3(y[:, m]), unit(m % 2)).then_inc(self.evacuated, 1)
                    sum_squares(dve, m, self.sq_done, self.sums, self.after)

            def scalar(self, act):
                for m in range(KC):
                    act.wait_ge(self.evacuated, LOOKBACK + m + 1)
                    square_y(act, m, self.sq_done, self.sums)

        CH = 8
        NCH = SEQ // CH
        SP_, SC, SG = 64, 16, 32
        GP = SG // 2
        L = CH + 1
        NU = NCH + DB
        NPOW = L + CH

        u_p = at("u_p", [P, 4, T], R1)
        q_t = at("q_t", [P, 4, T], R1 + 16896)
        k_t = at("k_t", [P, T], R1 + 33792)
        v_t = at("v_t", [P, T], R1 + 38016)
        in_st = at("in_st", [P, 2, GP, CH, SC], R1 + 42240)
        out_st = at("out_st", [P, 2, GP, L, SC], R1 + 58624)
        turn = at("turn", [P, 2, GP, NCH], R1 + 77056)
        prod = at("prod", [P, GP * L * SC], R1 + 77056)
        s0 = R1 + 93440
        bb = at("bb", [P, 2, GP, SC], s0)
        d_diag = at("d_diag", [SC, SG, SC], s0 + 2048)
        h0 = at("h0", [P, 2, GP, DB], s0 + 4096)
        pw = at("pw", [P, 2, NPOW, GP], s0 + 5120)
        mag8 = at("mag8", [P, GP], s0 + 7296)
        s1 = R1 + 105600
        lam = at("lam", [P, 3, GP], s1)
        b_in = at("b_in", [P, 2, GP, SC], s1 + 192)
        c_in = at("c_in", [P, 2, GP, SC], s1 + 2240)
        kvec = at("kvec", [P, NPOW], s1 + 4288)
        ang = at("ang", [P, NPOW, GP], s1 + 4416)
        rho = at("rho", [P, NPOW, GP], s1 + 5504)
        rnd = at("rnd", [P, NPOW, GP], s1 + 6592)
        sin_ = at("sin_", [P, NPOW, GP], s1 + 7680)
        cos_ = at("cos_", [P, NPOW, GP], s1 + 8768)
        sm = at("sm", [P, 12, GP], s1 + 9856)
        assert s1 + 9856 + 768 <= R1 + 118272
        rest = at("rest", [P, GP * NCH // 2], s1 + 192)
        assert 192 + GP * NCH * 2 <= 4288 + 192
        toep = at("toep", [P, 2, GP, P], R1 + 101376)
        A0 = A_HI
        u_c = at("u_c", [P, SG, NU], A0)
        h_st = at("h_st", [P, 2, GP, NCH + 1], A0 + 17408)
        lags = at("lags", [SC, 2, GP, P], A0 + 17408)
        g_st = at("g_st", [P, 2, 4, NCH], A0 + 33920)
        g_tmp = at("g_tmp", [P, 4, NCH], A0 + 38016)
        in_ch = at("in_ch", [P, 2, GP, P], A0 + 40064)
        h_s = at("h_s", [P, 2, GP, DB], A0 + 56448)
        h_s2 = at("h_s2", [P, 2, GP, DB], A0 + 62464)
        h_end = at("h_end", [P, 2, GP], A0 + 63488)
        g_hi = at("g_hi", [P, 4, T], R1 + 42240, F32R)
        g_lo = at("g_lo", [P, 4, T], R1 + 59136, F32R)
        ident = at("ident", [P, P], CONST_END)
        C2_END = CONST_END + 512
        assert C2_END <= nc.sbuf_usable_end

        s5_in, in_evac = sem("s5_in"), sem("in_even_evacuated")
        s5_vec, s5_act = sem("s5_vec"), sem("s5_act")
        u_out, g_out = sem("u_out"), sem("g_out")
        turned_out_a = sem("in_ch_out_act")
        s5_act2, lags_ready = sem("s5_act2"), sem("lags_ready")
        dt_ready, rates_ready, sines_ready = sem("dt_ready"), sem("rates_ready"), sem("sines_ready")
        prepared = sem("s5_prepared")
        lags_done, lags_out = sem("lags_done"), sem("lags_out")
        turned, turned_out = sem("in_ch_turned"), sem("in_ch_out")
        toep_zero, toep_in, u_in = sem("toep_zero"), sem("toep_in"), sem("u_in")
        v_done, v_read, h_ready, y_done, y_read = (sem(n) for n in ("v_done", "v_read", "h_ready", "y_done", "y_read"))
        g_in, s5_out, hs_ready = sem("g_in"), sem("s5_out"), sem("hs_ready")
        const_set, cin = sem("const_set"), sem("cin")

        class Chain:

            def __init__(self, eng, sem):
                self.eng, self.sem, self.count, self.tail = eng, sem, {}, None

            def __call__(self, ins, signal=None):
                s = signal or self.sem
                ins.then_inc(s, 1)
                self.count[id(s)] = self.count.get(id(s), 0) + 1
                self.tail = (s, self.count[id(s)])

            def after(self):
                if self.tail:
                    self.eng.wait_ge(*self.tail)
                return self.eng

        def bc(ap, axis, n):
            ap = ap.unsqueeze(axis)
            shape = list(ap.shape)
            shape[axis] = n
            return ap.broadcast_to(shape)

        def s5_prepare(dve, c):
            TT_, TS, STT = dve.tensor_tensor, dve.tensor_scalar, dve.scalar_tensor_tensor
            lr, li = lam[:, 0], lam[:, 1]

            def tt(out, a, b, op, signal=None):
                c.after()
                c(TT_(out, a, b, op), signal)

            dve.wait_ge(s5_in, 16 * 6)
            dve.wait_ge(dt_ready, 1)
            tt(sm[:, 1], lr, sm[:, 0], ALU.mult)
            tt(sm[:, 2], li, sm[:, 0], ALU.mult)
            tt(rho[:], bc(sm[:, 1], 1, NPOW), bc(kvec[:], 2, GP), ALU.mult)
            tt(ang[:], bc(sm[:, 2], 1, NPOW), bc(kvec[:], 2, GP), ALU.mult)
            c.after(); c(TS(rnd[:], ang[:], 1 / (2 * math.pi), ROUND, ALU.mult, ALU.add))
            c.after(); c(TS(rnd[:], rnd[:], -ROUND, None, ALU.add))
            for part in TWO_PI:
                c.after(); c(STT(ang[:], rnd[:], -part, ang[:], ALU.mult, ALU.add))
            c.after(); c(TS(ang[:], ang[:], PI_BELOW, -PI_BELOW, ALU.min, ALU.max), rates_ready)
            tt(sm[:, 3], lr, lr, ALU.mult)
            tt(sm[:, 4], li, li, ALU.mult)
            tt(sm[:, 3], sm[:, 3], sm[:, 4], ALU.add)
            c.after(); c(dve.reciprocal(sm[:, 3], sm[:, 3]))
            dve.wait_ge(sines_ready, 1)
            tt(cos_[:], cos_[:], cos_[:], ALU.mult)
            c.after(); c(TS(cos_[:], cos_[:], -2.0, 1.0, ALU.mult, ALU.add))
            tt(pw[:, 0], rho[:], cos_[:], ALU.mult)
            tt(pw[:, 1], rho[:], sin_[:], ALU.mult)
            c.after(); c(dve.tensor_copy(mag8[:], rho[:, CH]))
            c.after(); c(TS(sm[:, 4], pw[:, 0, 1], -1.0, None, ALU.add))
            tt(sm[:, 5], sm[:, 4], lr, ALU.mult)
            tt(sm[:, 6], pw[:, 1, 1], li, ALU.mult)
            tt(sm[:, 5], sm[:, 5], sm[:, 6], ALU.add)
            tt(sm[:, 5], sm[:, 5], sm[:, 3], ALU.mult)
            tt(sm[:, 6], pw[:, 1, 1], lr, ALU.mult)
            tt(sm[:, 7], sm[:, 4], li, ALU.mult)
            tt(sm[:, 6], sm[:, 6], sm[:, 7], ALU.subtract)
            tt(sm[:, 6], sm[:, 6], sm[:, 3], ALU.mult)
            cre, cim = bc(sm[:, 5], 2, SC), bc(sm[:, 6], 2, SC)
            pb = prod[:, 0:GP * SC].rearrange("p (i c) -> p i c", c=SC)
            tt(bb[:, 0], cre, b_in[:, 0], ALU.mult)
            tt(pb, cim, b_in[:, 1], ALU.mult)
            tt(bb[:, 0], bb[:, 0], pb, ALU.subtract)
            tt(bb[:, 1], cre, b_in[:, 1], ALU.mult)
            tt(pb, cim, b_in[:, 0], ALU.mult)
            tt(bb[:, 1], bb[:, 1], pb, ALU.add)
            yield
            pr, pi = (bc(pw[:, r, 0:L].rearrange("p k i -> p i k"), 3, SC) for r in range(2))
            cr, ci = (bc(c_in[:, r], 2, L) for r in range(2))
            po = prod[:].rearrange("p (i k c) -> p i k c", k=L, c=SC)
            tt(out_st[:, 0], cr, pr, ALU.mult)
            tt(po, ci, pi, ALU.mult)
            tt(out_st[:, 0], out_st[:, 0], po, ALU.subtract)
            yield
            tt(out_st[:, 1], cr, pi, ALU.mult)
            tt(po, ci, pr, ALU.mult)
            c.after(); c(STT(out_st[:, 1].rearrange("p i k c -> p (i k c)"),
                             out_st[:, 1].rearrange("p i k c -> p (i k c)"), -1.0, prod[:], ALU.mult, ALU.subtract))
            yield
            pr, pi = (bc(pw[:, r, L:NPOW].rearrange("p k i -> p i k"), 3, SC) for r in range(2))
            br, bi = (bc(bb[:, r], 2, CH) for r in range(2))
            pn = prod[:, 0:GP * CH * SC].rearrange("p (i k c) -> p i k c", k=CH, c=SC)
            tt(in_st[:, 0], br, pr, ALU.mult)
            tt(pn, bi, pi, ALU.mult)
            tt(in_st[:, 0], in_st[:, 0], pn, ALU.subtract)
            yield
            tt(in_st[:, 1], br, pi, ALU.mult)
            tt(pn, bi, pr, ALU.mult)
            tt(in_st[:, 1], in_st[:, 1], pn, ALU.add)
            yield
            c.after(); c(dve.memset(turn[:, 0, :, 0:1], 1.0))
            c.after(); c(dve.memset(turn[:, 1, :, 0:1], 0.0))
            c.after(); c(dve.tensor_copy(sm[:, 8], cos_[:, CH]))
            c.after(); c(dve.tensor_copy(sm[:, 9], sin_[:, CH]))
            n = 1
            while n < NCH:
                wr, wi = bc(sm[:, 8], 2, n), bc(sm[:, 9], 2, n)
                old = [turn[:, r, :, 0:n] for r in range(2)]
                new = [turn[:, r, :, n:2 * n] for r in range(2)]
                tp = rest[:, 0:GP * n].rearrange("p (i j) -> p i j", i=GP)
                tt(new[0], old[0], wr, ALU.mult)
                tt(tp, old[1], wi, ALU.mult)
                tt(new[0], new[0], tp, ALU.subtract)
                tt(new[1], old[0], wi, ALU.mult)
                tt(tp, old[1], wr, ALU.mult)
                tt(new[1], new[1], tp, ALU.add, prepared if 2 * n == NCH else None)
                if 2 * n < NCH:
                    tt(sm[:, 10], sm[:, 8], sm[:, 8], ALU.mult)
                    tt(sm[:, 11], sm[:, 9], sm[:, 9], ALU.mult)
                    tt(sm[:, 9], sm[:, 8], sm[:, 9], ALU.mult)
                    c.after(); c(TS(sm[:, 9], sm[:, 9], 2.0, None, ALU.mult))
                    tt(sm[:, 8], sm[:, 10], sm[:, 11], ALU.subtract)
                n *= 2
                if n in (32, 64):
                    yield

        def chunked(ap):
            return ap[:, 0:SEQ].rearrange("p (s j) -> p j s", s=CH)

        def stepped(ap):
            return ap[:, SEQ:T].rearrange("p (s b) -> p b s", s=DS)

        def vec_in_even(dve):
            c = Chain(dve, s5_vec)
            pieces = s5_prepare(dve, c)
            next(pieces)
            dve.wait_ge(load.act.sem, load.act.at("rstd_x"))
            u0 = LOOKBACK + FIRST_UNIT["in_even"] + 1
            JT = TT // CH
            for u in range(10):
                dve.wait_ge(unit_done, u0 + u)
                un = unit(u % 2)
                if u < 4:
                    for t in range(3):
                        n = JT if t < 2 else NCH - 2 * JT
                        dve.tensor_tensor(chunked(u_p[:, u])[:, t * JT:t * JT + n],
                                          un[:, t, 0:n * CH].rearrange("p (j s) -> p j s", s=CH),
                                          rstd[:, t * TT:t * TT + n * CH].rearrange("p (j s) -> p j s", s=CH), ALU.mult)
                    dve.tensor_tensor(stepped(u_p[:, u]), un[:, 2, TT - NS:TT].rearrange("p (b s) -> p b s", s=DS),
                                      rstd[:, SEQ:T].rearrange("p (b s) -> p b s", s=DS), ALU.mult).then_inc(in_evac, 1)
                elif u < 8:
                    dve.scalar_tensor_tensor(t3(q_t[:, u - 4]), un, 0.125, t3(rstd[:]), ALU.mult, ALU.mult
                                             ).then_inc(in_evac, 1)
                else:
                    dve.wait_ge(rel_out, 16)
                    dve.tensor_tensor(t3((k_t, v_t)[u - 8][:]), un, t3(rstd[:]), ALU.mult).then_inc(in_evac, 1)
                next(pieces, None)
            for _ in pieces:
                pass
            dve.wait_ge(in_evac, LOOKBACK + 10)
            return c

        def act_prepare(act):
            act.wait_ge(s5_in, 16 * 6)
            act.activation(sm[:, 0], lam[:, 2], ACT.Exp).then_inc(dt_ready, 1)
            act.wait_ge(rates_ready, 1)
            act.activation(sin_[:], ang[:], ACT.Sin).then_inc(s5_act, 1)
            act.activation(cos_[:], ang[:], ACT.Sin, scale=0.5).then_inc(s5_act, 1)
            act.wait_ge(s5_act, 2)
            act.activation(rho[:], rho[:], ACT.Exp).then_inc(sines_ready, 1)

        def pe_s5(pe):
            pe.wait_ge(prepared, 1)
            pe.wait_ge(in_evac, LOOKBACK + 10)
            for i in range(GP):
                for par in range(2):
                    rows = slice(par * 64, par * 64 + 64)
                    out = ps[0:SC, par * 4 + i // 4, (i % 4) * P:(i % 4 + 1) * P]
                    for r in range(2):
                        mm = pe.matmul(out, bb[rows, r, i], out_st[rows, r, i, 0:CH].rearrange("p k c -> p (k c)"),
                                       start=(r == 0), stop=(r == 1))
            mm.then_inc(lags_done, 1)
            pe.wait_ge(lags_ready, 1)
            for r in range(2):
                for i in range(GP):
                    mm = pe.transpose(ps[:, r * 4 + i // 4, (i % 4) * P:(i % 4 + 1) * P],
                                      in_st[:, r, i].rearrange("p s c -> p (s c)"), ident[:])
                mm.then_inc(turned, 1)
            pe.wait_ge(turned_out, 1)
            pe.wait_ge(turned_out_a, 1)
            pe.wait_ge(u_in, 16 * 16)
            def state_in(bank, r, i0, n, rows, cols, w, width):
                for i in range(i0, i0 + n):
                    for par in range(2):
                        out = ps[par * 64:par * 64 + 64, bank, w + (i - i0) * width:w + (i - i0 + 1) * width]
                        mm = pe.matmul(out, in_ch[rows, r, i, par * 64:par * 64 + 64], u_c[rows, 2 * i + par, cols],
                                       start=True, stop=True)
                return mm
            for r in range(2):
                mm = state_in(4, r, 0, GP, slice(64, P), slice(NCH, NU), r * P, DB)
            mm.then_inc(v_done, 1)
            for q in range(4):
                if q >= 2:
                    pe.wait_ge(v_read, q)
                for r in range(2):
                    mm = state_in(2 * (q % 2) + r, r, 4 * q, 4, slice(0, P), slice(0, NCH), 0, NCH)
                mm.then_inc(v_done, 1)
            pe.wait_ge(toep_in, 16 * CH)
            pe.wait_ge(v_read, 5)
            def y_of(out, i, par, m, urhs, hr, hi):
                rows = slice(par * 64, par * 64 + 64)
                pe.matmul(out, toep[:, par, i, 0:m], urhs, start=True, stop=False)
                pe.matmul(out, out_st[rows, 0, i, 1:L].rearrange("p k c -> p (k c)")[:, 0:m], hr[rows], start=False, stop=False)
                return pe.matmul(out, out_st[rows, 1, i, 1:L].rearrange("p k c -> p (k c)")[:, 0:m], hi[rows],
                                 start=False, stop=True)
            for q in range(4):
                pe.wait_ge(h_ready, q + 1)
                if q >= 2:
                    pe.wait_ge(y_read, 2 * (q - 1))
                for n in range(4):
                    for par in range(2):
                        i = 4 * q + n
                        mm = y_of(ps[:, 4 + 2 * (q % 2) + par, n * NCH:(n + 1) * NCH], i, par, P,
                                  u_c[:, 2 * i + par, 0:NCH], h_st[:, 0, i, 0:NCH], h_st[:, 1, i, 0:NCH])
                mm.then_inc(y_done, 1)
            for i in range(GP):
                for par in range(2):
                    mm = y_of(ps[0:64, par, i * DB:(i + 1) * DB], i, par, 64, u_c[:, 2 * i + par, NCH:NU],
                              h0[:, 0, i], h0[:, 1, i])
            mm.then_inc(y_done, 1)

        def vec_s5(dve, c):
            TT_ = dve.tensor_tensor

            def tt(out, a, b, op, signal=None):
                c.after()
                c(TT_(out, a, b, op), signal)

            c.after(); c(dve.memset(toep[:], 0.0), toep_zero)
            dve.wait_ge(lags_done, 1)
            c.after(); c(dve.tensor_copy(lags[:, 0].rearrange("p (a b) n -> p a (b n)", a=4), ps[0:SC, 0:4]))
            tt(lags[:, 0, :, 0:SC], lags[:, 0, :, 0:SC], d_diag[:, 0:GP], ALU.add)
            dve.wait_ge(lags_out, 1)
            tt(lags[:, 1, :, 0:SC], lags[:, 1, :, 0:SC], d_diag[:, GP:SG], ALU.add, lags_ready)
            dve.wait_ge(turned, 1)
            c.after(); c(dve.tensor_copy(in_ch[:, 0].rearrange("p (a b) n -> p a (b n)", a=4), ps[:, 0:4]), turned_out)
            dve.wait_ge(v_done, 1)
            p4 = [bc(pw[:, r, DS], 2, DB) for r in range(2)]
            add = ps[:, 4, 0:2 * P].rearrange("p (r i b) -> p r i b", r=2, b=DB)
            tt(h_s[:, 0], h0[:, 0], p4[0], ALU.mult)
            tt(h_s2[:, 0], h0[:, 1], p4[1], ALU.mult)
            tt(h_s[:, 1], h0[:, 0], p4[1], ALU.mult)
            tt(h_s2[:, 1], h0[:, 1], p4[0], ALU.mult)
            tt(h_s[:, 0], h_s[:, 0], h_s2[:, 0], ALU.subtract)
            tt(h_s[:, 1], h_s[:, 1], h_s2[:, 1], ALU.add)
            tt(h_s[:], h_s[:], add, ALU.add, v_read)
            dve.wait_ge(toep_in, 16 * CH)
            c.after(); c(dve.memset(h_st[:, :, :, 0:1], 0.0))
            for q in range(4):
                i = slice(4 * q, 4 * q + 4)
                wr, wi = turn[:, 0, i], turn[:, 1, i]
                vr, vi = (ps[:, 2 * (q % 2) + r].rearrange("p (i j) -> p i j", i=4) for r in range(2))
                dve.wait_ge(v_done, q + 2)
                tt(g_st[:, 0], vr, wr, ALU.mult)
                tt(g_tmp[:], vi, wi, ALU.mult)
                tt(g_st[:, 0], g_st[:, 0], g_tmp[:], ALU.add)
                tt(g_st[:, 1], vi, wr, ALU.mult)
                tt(g_tmp[:], vr, wi, ALU.mult, v_read)
                tt(g_st[:, 1], g_st[:, 1], g_tmp[:], ALU.subtract)
                for r in range(2):
                    for n in range(4):
                        c.after()
                        c(dve.tensor_tensor_scan(g_st[:, r, n], mag8[:, 4 * q + n:4 * q + n + 1].broadcast_to([P, NCH]),
                                                 g_st[:, r, n], 0.0, ALU.mult, ALU.add))
                tt(h_st[:, 0, i, 1:], g_st[:, 0], wr, ALU.mult)
                tt(g_tmp[:], g_st[:, 1], wi, ALU.mult)
                tt(h_st[:, 0, i, 1:], h_st[:, 0, i, 1:], g_tmp[:], ALU.subtract)
                tt(h_st[:, 1, i, 1:], g_st[:, 1], wr, ALU.mult)
                tt(g_tmp[:], g_st[:, 0], wi, ALU.mult)
                tt(h_st[:, 1, i, 1:], h_st[:, 1, i, 1:], g_tmp[:], ALU.add, h_ready)
            c.after(); c(dve.tensor_copy(h_end[:], h_st[:, :, :, NCH]), hs_ready)

        def channel_rows(scratch, j0, n):
            return scratch.rearrange("(g c) t -> c g t", c=SC)[:, :, j0:j0 + n]

        def feature_rows(scratch):
            return scratch.rearrange("(k p) t -> p k t", p=P)

        def act_s5(act):
            c = Chain(act, s5_act2)
            act.wait_ge(in_evac, LOOKBACK + 10)
            act.wait_ge(unit_done, LOOKBACK + FIRST_UNIT["in_even"] + 10)
            act.dma_start(feature_rows(io["u_scratch"]), u_p[:]).then_inc(u_out, 16)
            act.wait_ge(u_out, 16)
            for s in range(CH):
                act.dma_start(u_c[SC * s:SC * s + SC, :, 0:NCH], channel_rows(io["u_scratch"], s * NCH, NCH)
                              ).then_inc(u_in, 16)
            for s in range(CH):
                act.dma_start(u_c[SC * s:SC * s + SC, :, NCH:NU],
                              channel_rows(io["u_scratch"], SEQ + (s % DS) * DB, DB)).then_inc(u_in, 16)
            act.wait_ge(toep_zero, 1)
            act.wait_ge(lags_done, 1)
            c(act.activation(lags[:, 1].rearrange("p (a b) n -> p a (b n)", a=4), ps[0:SC, 4:8], ACT.Copy), lags_out)
            act.wait_ge(lags_ready, 1)
            for s in range(CH):
                act.dma_start(toep[SC * s:SC * s + SC, :, :, SC * s:P], lags[:, :, :, 0:P - SC * s]).then_inc(toep_in, 16)
            act.wait_ge(turned, 2)
            c(act.activation(in_ch[:, 1].rearrange("p (a b) n -> p a (b n)", a=4), ps[:, 4:8], ACT.Copy), turned_out_a)
            for q in range(4):
                act.wait_ge(y_done, q + 1)
                for par in range(2):
                    c(act.activation(u_c[:, 8 * q + par:8 * q + 8:2, 0:NCH],
                                     ps[:, 4 + 2 * (q % 2) + par].rearrange("p (i j) -> p i j", i=4),
                                     ACT.Gelu_apprx_tanh), y_read)
            act.wait_ge(y_done, 5)
            for par in range(2):
                c(act.activation(u_c[0:64, par:SG:2, NCH:NU],
                                 ps[0:64, par, 0:GP * DB].rearrange("p (i b) -> p i b", b=DB),
                                 ACT.Gelu_apprx_tanh), y_read)

            act.wait_ge(y_read, 10)
            for t in range(CH):
                act.dma_start(channel_rows(io["g_scratch"], t * NCH, NCH), u_c[SC * t:SC * t + SC, :, 0:NCH]
                              ).then_inc(g_out, 16)
            for t in range(DS):
                act.dma_start(channel_rows(io["g_scratch"], SEQ + t * DB, DB), u_c[SC * t:SC * t + SC, :, NCH:NU]
                              ).then_inc(g_out, 16)
            act.wait_ge(g_out, 16 * (CH + DS))
            act.dma_start(u_p[:], feature_rows(io["g_scratch"])).then_inc(g_in, 16)
            act.wait_ge(hs_ready, 1)
            act.dma_start(io["s5_prompt"], h_end[:]).then_inc(s5_out, 16)
            act.dma_start(io["s5_sample"], h_s[:]).then_inc(s5_out, 16)

        def act_s5_loads(act):
            for dst, name in ((lam, "s5_lam"), (b_in, "s5_b"), (c_in, "s5_c"), (kvec, "kvec"), (d_diag, "s5_d"), (h0, "s5_h0")):
                act.dma_start(dst[:], io[name]).then_inc(s5_in, 16)

        HD, NH, NKV = 64, 8, 2
        G = NH // NKV
        W = 128
        NB = SEQ // W
        RY = 3 * W
        ROW = 3200
        s2 = R1 + 76032
        bias_t = at("bias_t", [P, NH, 2 * W], s2)
        v_tok = at("v_tok", [P, NB + 1, P], s2 + 8192)
        prob = at("prob", [P, 2, NH, 2 * W], s2 + 12800)
        prob_t = at("prob_t", [P, NH, 2, W], s2 + 29184)
        prob_s = at("prob_s", [P, T], s2 + 12800)
        prob_st = at("prob_st", [P, NB + 1, P], s2 + 29184)
        st = s2 + 37376
        top = at("top", [P, 2, NH], st)
        den = at("den", [P, 2, NH], st + 64)
        sink_e = at("sink_e", [P, 2, NH], st + 128)
        sinks = at("sinks", [P, NH], st + 192)
        sinks_s = at("sinks_s", [P, NKV], st + 224)
        q_s = at("q_s", [P, G, NS], st + 256)
        own = at("own", [P, NKV, W + DS], A_LO + 4 * T * 4)
        c_k = at("c_k", [P, DB, W], A_LO + 4 * T * 4 + 2048)
        c_v = at("c_v", [P, DB, P], A_LO + 4 * T * 4 + 6144)
        other = at("other", [P, DB], A_LO + 4 * T * 4 + 10240)
        rel = at("rel", [P, NH, RY], R1 + 33792)
        buckets = at("buckets", [33, RY], R1 + 33792 + 12288)
        table = at("table", [33, NH], R1 + 33792 + 13824)
        rel_in, rel_done, rel_read, rel_out = sem("rel_in"), sem("rel_done"), sem("rel_read"), sem("rel_out")
        at_in, at_vec, at_act = sem("at_in"), sem("at_vec"), sem("at_act")
        sc_done, sc_read, top_ready, exp_done = sem("sc_done"), sem("sc_read"), sem("top_ready"), sem("exp_done")
        norm_done, pt_done, pt_read, o_done, o_read = (sem(n) for n in (
            "norm_done", "pt_done", "pt_read", "o_done", "o_read"))
        o_read_a, pt_read_s = sem("o_read_act"), sem("pt_read_sample")
        vt_done, vt_read, k_out = sem("vt_done"), sem("vt_read"), sem("k_out")
        skew = io["skew"]

        def act_bias_rows(act):
            act.dma_start(buckets[:], io["buckets"]).then_inc(rel_in, 16)
            act.dma_start(table[:], io["table"]).then_inc(rel_in, 16)
            act.wait_ge(rel_read, 1)
            act.dma_start(skew[0:P * ROW].rearrange("(p r) -> p r", r=ROW)[:, 0:NH * RY],
                          rel[:].rearrange("p h y -> p (h y)")).then_inc(rel_out, 16)

        def pe_bias_rows(pe):
            pe.wait_ge(rel_in, 32)
            for h in range(NH):
                mm = pe.matmul(ps[:, h, 0:RY], table[:, h:h + 1].broadcast_to([33, P]), buckets[:], start=True, stop=True)
            mm.then_inc(rel_done, 1)

        def vec_bias_rows(dve):
            dve.wait_ge(rel_done, 1)
            dve.tensor_copy(rel[:], ps[:, :, 0:RY]).then_inc(rel_read, 1)

        def skewed(n):
            return skew[W - 1:W - 1 + P * (ROW - 1)].rearrange("(p r) -> p r", r=ROW - 1)[:, 0:NH * RY].rearrange(
                "p (h y) -> p h y", y=RY)[:, :, 0:n]

        def act_at_loads(act):
            act.wait_ge(y_done, 5)
            act.wait_ge(rel_out, 16)
            act.dma_start(bias_t[:], skewed(2 * W)).then_inc(at_in, 16)
            act.dma_start(sinks[:], io["sinks"]).then_inc(at_in, 16)
            act.dma_start(sinks_s[:], io["sinks_s"]).then_inc(at_in, 16)
            act.dma_start(other[:], io["other"]).then_inc(at_in, 16)
            act.dma_start(c_k[:], io["c_k"]).then_inc(at_in, 16)
            act.dma_start(c_v[:], io["c_v"]).then_inc(at_in, 16)
            for kv in range(NKV):
                for hh in range(G):
                    for b in range(DB):
                        r = hh * NS + b * DS
                        act.dma_start(own[r:r + DS, kv], skewed(W + DS)[0:DS, kv * G + hh]).then_inc(at_in, 16)
            act.wait_ge(in_evac, LOOKBACK + 10)
            act.dma_start(io["k_prompt"], k_t[:, SEQ - W:SEQ]).then_inc(k_out, 16)
            act.dma_start(io["v_prompt"], v_t[:, SEQ - W:SEQ]).then_inc(k_out, 16)
            for out, cache, new in ((io["k_sample"], io["c_k"], k_t), (io["v_sample"], io["c_vt"], v_t)):
                act.dma_start(out[:, :, 0:W - DS], cache[:, :, DS:W]).then_inc(k_out, 16)
                act.dma_start(out[:, :, W - DS:W], new[:, SEQ:T].rearrange("p (b s) -> p b s", s=DS)).then_inc(k_out, 16)

        AT_LOADS = 6 + NKV * G * DB
        K_OUTS = 6

        def pe_attention(pe):
            pe.wait_ge(y_read, 10)
            for n in range(NB + 1):
                w = W if n < NB else NS
                mm = pe.transpose(ps[0:w, n // 4, (n % 4) * P:(n % 4 + 1) * P], v_t[:, n * W:n * W + w], ident[:])
            mm.then_inc(vt_done, 1)
            pe.wait_ge(at_in, 16 * AT_LOADS)
            pe.wait_ge(vt_read, 2)
            for kv in range(NKV):
                rows = slice(kv * HD, kv * HD + HD)
                q = q_s[rows].rearrange("p h t -> p (h t)")
                if kv:
                    pe.wait_ge(sc_read, kv)
                for n in range(2):
                    pe.matmul(ps[:, n], q, c_k[rows, 4 * n:4 * n + 4].rearrange("p b m -> p (b m)"), start=True, stop=True)
                pe.matmul(ps[:, 2, 0:NS], q, k_t[rows, SEQ:T], start=True, stop=True).then_inc(sc_done, 1)
                pe.wait_ge(norm_done, kv + 1)
                if kv:
                    pe.wait_ge(o_read, kv)
                for n in range(NB + 1):
                    w = W if n < NB else NS
                    mm = pe.transpose(ps[0:w, 4 + n // 4, (n % 4) * P:(n % 4 + 1) * P], prob_s[:, n * W:n * W + w], ident[:])
                mm.then_inc(pt_done, 1)
                pe.wait_ge(pt_read_s, kv + 1)
                for n in range(NB):
                    pe.matmul(ps[rows, 7, 0:P], c_v[:, n, rows], prob_st[:, n], start=(n == 0), stop=False)
                pe.matmul(ps[rows, 7, 0:P], v_tok[0:NS, NB, rows], prob_st[0:NS, NB], start=False, stop=True
                          ).then_inc(o_done, 1)

            def scores(n):
                pe.wait_ge(sc_read, NKV + n)
                k0 = max(n - 1, 0) * W
                for h in range(NH):
                    rows = slice((h // G) * HD, (h // G) * HD + HD)
                    c0 = (h % 2) * 2 * W + (W if n == 0 else 0)
                    mm = pe.matmul(ps[:, h // 2, c0:(h % 2 + 1) * 2 * W], q_t[rows, h % G, n * W:(n + 1) * W],
                                   k_t[rows, k0:(n + 1) * W], start=True, stop=True)
                mm.then_inc(sc_done, 1)

            scores(0)
            for n in range(NB):
                if n + 1 < NB:
                    scores(n + 1)
                pe.wait_ge(norm_done, NKV + n + 1)
                pe.wait_ge(o_read, NKV + n)
                if n:
                    pe.wait_ge(o_read_a, n)
                halves = (1,) if n == 0 else (0, 1)
                for h in range(NH):
                    for f in halves:
                        mm = pe.transpose(ps[:, 4 + h // 2, ((h % 2) * 2 + f) * W:((h % 2) * 2 + f + 1) * W],
                                          prob[:, n % 2, h, f * W:(f + 1) * W], ident[:])
                mm.then_inc(pt_done, 1)
                pe.wait_ge(pt_read, 2 * (n + 1))
                for kv in range(NKV):
                    rows = slice(kv * HD, kv * HD + HD)
                    for f in halves:
                        mm = pe.matmul(ps[rows, 4 + kv], v_tok[:, n - 1 + f, rows], prob_t[:, kv * G:kv * G + G, f],
                                       start=(f == halves[0]), stop=(f == 1))
                mm.then_inc(o_done, 1)

        def vec_attention(dve, c):
            TT_ = dve.tensor_tensor

            def tt(out, a, b, op, signal=None):
                c.after()
                c(TT_(out, a, b, op), signal)

            dve.wait_ge(vt_done, 1)
            c.after(); c(dve.tensor_copy(q_s[:], q_t[:, :, SEQ:T]))
            c.after(); c(dve.tensor_copy(v_tok[:, 0:NB].rearrange("p (a b) n -> p a (b n)", a=2), ps[:, 0:2]), vt_read)
            c.after(); c(dve.tensor_copy(v_tok[0:NS, NB], ps[0:NS, 2, 0:P]), vt_read)
            dve.wait_ge(at_in, 16 * AT_LOADS)
            for kv in range(NKV):
                dve.wait_ge(sc_done, kv + 1)
                old = prob_s[:, 0:SEQ].rearrange("p (b m) -> p b m", m=W)
                new = prob_s[:, SEQ:T].rearrange("p (b s) -> p b s", s=DS)
                tt(old, ps[:, 0:2].rearrange("p a (b m) -> p (a b) m", m=W), bc(own[:, kv, 0:W], 1, DB), ALU.add)
                tt(new, ps[:, 2, 0:NS].rearrange("p (b s) -> p b s", s=DS), bc(own[:, kv, W:W + DS], 1, DB), ALU.add, sc_read)
                tt(old, old, bc(other[:], 2, W), ALU.add)
                tt(new, new, bc(other[:], 2, DS), ALU.add)
                c.after(); c(dve.reduce_max(top[:, 0, kv:kv + 1], prob_s[:], AX_X))
                tt(top[:, 0, kv:kv + 1], top[:, 0, kv:kv + 1], sinks_s[:, kv:kv + 1], ALU.max)
                tt(sink_e[:, 0, kv:kv + 1], sinks_s[:, kv:kv + 1], top[:, 0, kv:kv + 1], ALU.subtract)
                c.after(); c(dve.tensor_scalar(top[:, 0, kv:kv + 1], top[:, 0, kv:kv + 1], -1.0, None, ALU.mult), top_ready)
                dve.wait_ge(exp_done, kv + 1)
                tt(den[:, 0, kv:kv + 1], den[:, 0, kv:kv + 1], sink_e[:, 0, kv:kv + 1], ALU.add)
                c.after(); c(dve.reciprocal(den[:, 0, kv:kv + 1], den[:, 0, kv:kv + 1]))
                c.after(); c(dve.tensor_scalar(prob_s[:], prob_s[:], den[:, 0, kv:kv + 1], None, ALU.mult), norm_done)
                dve.wait_ge(pt_done, kv + 1)
                c.after(); c(dve.tensor_copy(prob_st[:, 0:NB].rearrange("p (a b) n -> p a (b n)", a=2), ps[:, 4:6]))
                c.after(); c(dve.tensor_copy(prob_st[0:NS, NB], ps[0:NS, 6, 0:P]), pt_read_s)
                dve.wait_ge(o_done, kv + 1)
                rows = slice(kv * HD, kv * HD + HD)
                c.after(); c(dve.tensor_copy(q_t[rows, :, SEQ:T], ps[rows, 7, 0:P].rearrange("p (h t) -> p h t", h=G)), o_read)

            def soften(n):
                z = n % 2
                w0 = W if n == 0 else 0
                dve.wait_ge(sc_done, NKV + n + 1)
                if n >= 2:
                    dve.wait_ge(pt_done, NKV + n - 1)
                for f in range(2):
                    hs = slice(4 * f, 4 * f + 4)
                    tt(prob[:, z, hs, w0:], ps[:, 2 * f:2 * f + 2].rearrange("p a (h m) -> p (a h) m", h=2)[:, :, w0:],
                       bias_t[:, hs, w0:], ALU.add, sc_read if f else None)
                c.after(); c(dve.reduce_max(top[:, z], prob[:, z, :, w0:], AX_X))
                tt(top[:, z], top[:, z], sinks[:], ALU.max)
                tt(sink_e[:, z], sinks[:], top[:, z], ALU.subtract)
                c.after(); c(dve.tensor_scalar(top[:, z], top[:, z], -1.0, None, ALU.mult), top_ready)

            soften(0)
            for n in range(NB):
                z, w0 = n % 2, W if n == 0 else 0
                if n + 1 < NB:
                    soften(n + 1)
                dve.wait_ge(exp_done, NKV + n + 1)
                tt(den[:, z], den[:, z], sink_e[:, z], ALU.add)
                c.after(); c(dve.reciprocal(den[:, z], den[:, z]))
                tt(prob[:, z, :, w0:], prob[:, z, :, w0:], bc(den[:, z], 2, 2 * W - w0), ALU.mult, norm_done)
                dve.wait_ge(o_done, NKV + n + 1)
                rows = slice(0, HD)
                c.after(); c(dve.tensor_copy(q_t[rows, :, n * W:(n + 1) * W], ps[rows, 4].rearrange("p (h t) -> p h t", h=G)), o_read)

        def act_attention(act):
            c = Chain(act, at_act)
            for kv in range(NKV):
                act.wait_ge(top_ready, kv + 1)
                c(act.activation(sink_e[:, 0, kv:kv + 1], sink_e[:, 0, kv:kv + 1], ACT.Exp))
                c.after()
                c(act.activation(prob_s[:], prob_s[:], ACT.Exp, bias=top[:, 0, kv:kv + 1],
                                 accum_out=den[:, 0, kv:kv + 1]), exp_done)
            for n in range(NB):
                z, w0 = n % 2, W if n == 0 else 0
                act.wait_ge(top_ready, NKV + n + 1)
                c(act.activation(sink_e[:, z], sink_e[:, z], ACT.Exp))
                for h in range(NH):
                    c.after()
                    c(act.activation(prob[:, z, h, w0:], prob[:, z, h, w0:], ACT.Exp, bias=top[:, z, h:h + 1],
                                     accum_out=den[:, z, h:h + 1]), exp_done if h == NH - 1 else None)
                if n:
                    act_turn(act, c, n - 1)
            act_turn(act, c, NB - 1)

        def act_turn(act, c, n):
            act.wait_ge(pt_done, NKV + n + 1)
            f0 = 1 if n == 0 else 0
            for f in range(2):
                src = ps[:, 4 + 2 * f:6 + 2 * f].rearrange("p a (h f m) -> p (a h) f m", h=2, f=2)
                c(act.activation(prob_t[:, 4 * f:4 * f + 4, f0:], src[:, :, f0:], ACT.Copy), pt_read)
            act.wait_ge(o_done, NKV + n + 1)
            rows = slice(HD, P)
            c(act.activation(q_t[rows, :, n * W:(n + 1) * W], ps[rows, 5].rearrange("p (h t) -> p h t", h=G), ACT.Copy), o_read_a)

        glu_split, glu_done, sig_ready = sem("glu_split"), sem("glu_done"), sem("sig_ready")
        glu_act, glu_evac, mix_hi, mix_lo, glu_mul = (sem(n) for n in ("glu_act", "glu_evac", "mix_hi", "mix_lo", "glu_mul"))

        def natural(dst, src, k):
            return [(dst[:, k, 0:SEQ].rearrange("p (j s) -> p j s", s=CH), chunked(src[:, k])),
                    (dst[:, k, SEQ:T].rearrange("p (b s) -> p b s", s=DS), stepped(src[:, k]))]

        def act_glu(act):
            act.wait_ge(g_in, 16)
            act.wait_ge(o_read, NKV + NB)
            act.wait_ge(o_read_a, NB)
            for k in range(4):
                for d, s in natural(g_hi, u_p, k):
                    ins = act.activation(d, s, ACT.Copy)
                ins.then_inc(glu_act, 1)
            for k in range(4):
                act.activation(a_hi[:, 4 + k], q_t[:, k], ACT.Copy).then_inc(mix_hi, 1)
            for m in range(4):
                act.wait_ge(unit_done, LOOKBACK + FIRST_UNIT["glu"] + m + 1)
                if m:
                    act.wait_ge(glu_mul, m)
                act.activation(t3(sq[:, 0]), unit(m % 2), ACT.Sigmoid).then_inc(glu_evac, 1)
                act.wait_ge(glu_mul, m + 1)
                act.activation(a_hi[:, m], sq[:, 1], ACT.Copy).then_inc(mix_hi, 1)

        def vec_glu(dve, c):
            dve.wait_ge(g_in, 16)
            for k in range(4):
                dve.wait_ge(glu_act, k + 1)
                for (d, s), (hi, _) in zip(natural(g_lo, u_p, k), natural(g_hi, u_p, k)):
                    ins = dve.tensor_tensor(d, s, hi.bitcast(F32), ALU.subtract)
                ins.then_inc(glu_split, 1)
            for k in range(4):
                dve.wait_ge(mix_hi, k + 1)
                dve.tensor_tensor(a_lo[:, 4 + k], q_t[:, k], a_hi[:, 4 + k].bitcast(F32), ALU.subtract).then_inc(mix_lo, 1)
            for m in range(4):
                dve.wait_ge(glu_evac, LOOKBACK + m + 1)
                dve.wait_ge(mix_lo, 4 + m)
                sig, out = sq[:, 0], sq[:, 1]
                dve.tensor_tensor(out[:, 0:SEQ].rearrange("p (j s) -> p j s", s=CH), chunked(u_p[:, m]),
                                  sig[:, 0:SEQ].rearrange("p (j s) -> p j s", s=CH), ALU.mult)
                dve.tensor_tensor(out[:, SEQ:T].rearrange("p (b s) -> p b s", s=DS), stepped(u_p[:, m]),
                                  sig[:, SEQ:T].rearrange("p (b s) -> p b s", s=DS), ALU.mult).then_inc(glu_mul, 1)
                dve.wait_ge(mix_hi, 4 + m + 1)
                dve.tensor_tensor(a_lo[:, m], out, a_hi[:, m].bitcast(F32), ALU.subtract).then_inc(mix_lo, 1)

        def pe_glu(pe):
            pe.sem_inc(glu_evac, LOOKBACK)
            pe.wait_ge(glu_split, 4)
            for m in range(4):
                if m % 2 == 0:
                    pe.wait_ge(w_ready, LOOKBACK + FIRST_BLOCK["glu"] + m // 2 + 1)
                pe.wait_ge(glu_evac, m + 1)
                pe_unit(pe, m // 2, m % 2, range(4), (g_hi, g_lo), wk=4 * (m % 2))
            pe.wait_ge(mix_lo, 8)

        HH = 8
        LEVELS = range(1, 8)
        SAMPLE_LEVELS = (1, 2)
        NC = SEQ // P
        c_out = at("c_out", [P, KC, T], R1)
        raw = at("raw", [P, 2, 4, T], R1 + 33792)
        o0 = R1 + 67584
        cum = at("cum", [P, T], o0)
        key = at("key", [P, T], o0 + 4224)
        lev = at("lev", [P, 2, T], o0 + 8448)
        vtok = at("vtok", [P, NC + 1, P], o0 + 16896)
        ktok = at("ktok", [P, NC + 1, P], o0 + 21504)
        att = at("att", [P, NC + 1, P], o0 + 26112)
        reset = at("reset", [P, T], o0 + 30720, U8)
        state = at("state", [P, 2, P], o0 + 31776)
        lb = at("lb", [P, 6, HH], o0 + 32800)
        one_less, log_less, log_lb, log_gap = (lb[:, j] for j in range(4))
        last = at("last", [P, NC + DB], o0 + 32992)
        gnorm = at("gnorm", [P, 1], o0 + 33056)
        own_seq = at("own_seq", [NS, DB], o0 + 33088)
        vdiag = at("vdiag", [NS, DB, P], o0 + 8448)
        qdec, kdec = sq[:, 0], sq[:, 1]
        state_s = at("state_s", [P, DB, P], R1 + 105600)
        masks = at("masks", [P, 8, P], C2_END, U8)
        assert C2_END + 1024 <= nc.sbuf_usable_end
        masks_in = at("masks_in", [P, 8, P], R1 + 33792)
        reset_in = at("reset_in", [P, T], R1 + 33792 + 4096)

        V = ["query", "gate", "key", "logsig", "gap", "floor", "logf", "cum", "kd", "kds", "qdec", "kdec"]
        V += ["diff1"]
        for _l in LEVELS:
            V += ([f"diff{_l + 1}"] if _l < 7 else []) + [f"left{_l}", f"right{_l}"]
            if _l == 1:
                V += ["diag", "diag_s"]
            if _l > 1:
                V += [f"pick{_l - 1}"] + ([f"pick_s{_l - 1}"] if _l - 1 in SAMPLE_LEVELS else [])
        V += ["pick7", "vdiag"] + [f"state{_c}" for _c in range(1, NC + 1)]
        V += ["o_p", "o_s", "decay_s", "state_s", "mean_o", "scaled_o", "out"]
        A = ["sig_q", "sig_f", "sig_g", "abs1", "exp1", "ln1", "abs2", "exp2", "ln2", "vtok", "vtok_s",
             "ecum", "elast", "elast_s", "ekd"]
        for _l in LEVELS:
            A += [f"exp_l{_l}", f"exp_r{_l}"]
        A += ["ktok", "ktok_s", "square_o", "ln_o", "rstd_o"]
        T_ = ["vturn", "diag"] + [f"score{_l}" for _l in LEVELS] + ["kturn"]
        T_ += [f"add{_c}" for _c in range(NC)] + ["o", "add_s", "stat_o"]
        hv, ha, ht = Steps(sem("hgrn_vec"), V), Steps(sem("hgrn_act"), A), Steps(sem("hgrn_pe"), T_)
        he = Steps(sem("hgrn_evacuated"), ["e0", "e1", "e2", "e3"])
        hs_in, hs_out, hp_out, hc_in = sem("hs_in"), sem("hs_out"), sem("hp_out"), sem("hc_in")
        pick_turn = sem("pick_turn")
        lb_e, lb_s, lb_l, lb_r = sem("lb_e"), sem("lb_s"), sem("lb_l"), sem("lb_r")
        U_ODD = FIRST_UNIT["in_odd"]

        def head_row(dram, h):
            return dram[h] if isinstance(h, int) else dram[bass.ds(h, 1)].rearrange("a p n -> p (a n)")

        def blocks(ap, l, half, width=T):
            return ap[:, 0:width].rearrange("p (n f t) -> p n f t", f=2, t=1 << (l - 1))[:, :, half]

        def span(l):
            return T if l in SAMPLE_LEVELS else SEQ

        def pe_head_unit(pe, h, j, b):
            pe.wait_ge(w_ready, h * 4 + (FIRST_BLOCK["in_odd"] + j + 1 + LOOKBACK))
            if j:
                he.wait(pe, f"e{j - 1}", h)
            else:
                he.wait(pe, "e3", h - 1)
            pe_unit(pe, j % 2, 0, range(KC), (a_hi, a_lo))

        def vec_head_unit(dve, h, j, b):
            dve.wait_ge(unit_done, h * 4 + (LOOKBACK + U_ODD + j + 1))
            if not isinstance(h, int) or h > 0:
                hv.wait(dve, "out", h - 2)
            he.done(dve.tensor_tensor(t3(raw[:, b, j]), unit(0), t3(rstd[:]), ALU.mult), f"e{j}")

        CH0, CH1, CHS = 3, 4, 7

        def chunk_out(c, w=P):
            return ps[:, CH0 + c // 4, (c % 4) * P:(c % 4) * P + w] if c < NC else ps[:, CHS, 0:w]

        def pe_head(pe, h, piece, b):
            q, v = raw[:, b, 0], raw[:, b, 2]
            if piece == 0:
                he.wait(pe, "e2", h)
                hv.wait(pe, "out", h - 1)
                hv.wait(pe, "mean_o", h - 1)
                for c in range(NC + 1):
                    w = P if c < NC else NS
                    mm = pe.transpose(chunk_out(c)[0:w], v[:, c * P:c * P + w], ident[:])
                ht.done(mm, "vturn")
            if piece == 1:
                ha.wait(pe, "vtok_s", h)
                hv.wait(pe, "key", h)
                for c in range(NC + 1):
                    w = P if c < NC else NS
                    cols = slice(c * P, c * P + w)
                    mm = pe.matmul(chunk_out(c, w)[0:w], key[:, cols], q[:, cols], start=True, stop=True)
                ht.done(mm, "diag")
            for l in {1: (1, 2, 3), 2: (4, 5, 6, 7)}.get(piece, ()):
                x_ = lev[:, l % 2]
                hv.wait(pe, f"right{l}", h)
                if l > 2:
                    hv.wait(pe, f"pick{l - 2}", h)
                rt = blocks(x_, l, 1, span(l))
                per = 64 >> (l - 1)
                for c in range(NC):
                    mm = pe.matmul(ps[:, 5 + l % 2, c * 64:(c + 1) * 64], x_[:, c * P:(c + 1) * P],
                                   rt[:, c * per:(c + 1) * per], start=True, stop=True)
                if l in SAMPLE_LEVELS:
                    hv.wait(pe, "diag_s" if l == 1 else f"pick_s{l - 1}", h)
                    mm = pe.matmul(ps[0:NS, CHS, l * P:l * P + NS // 2], x_[:, SEQ:T], rt[:, NC * per:], start=True, stop=True)
                ht.done(mm, f"score{l}")
            if piece == 2:
                hv.wait(pe, "kdec", h)
                hv.wait(pe, "pick_s2", h)
                for c in range(NC + 1):
                    w = P if c < NC else NS
                    mm = pe.transpose(chunk_out(c)[0:w], kdec[:, c * P:c * P + w], ident[:])
                ht.done(mm, "kturn")
            if piece == 3:
                ha.wait(pe, "ktok_s", h)
                hv.wait(pe, "pick7", h)
                for c in range(NC):
                    pe.matmul(chunk_out(c), vtok[:, c], att[:, c], start=True, stop=(c == 0))
                    if c >= 2:
                        hv.wait(pe, f"state{c - 1}", h)
                    ht.done(pe.matmul(ps[:, 5 + c % 2, 0:P], ktok[:, c], vtok[:, c], start=True, stop=True), f"add{c}")
                    if c:
                        hv.wait(pe, f"state{c}", h)
                        pe.matmul(chunk_out(c), state[:, c % 2], qdec[:, c * P:(c + 1) * P], start=False, stop=True)
                pe.wait_ge(hs_in, h * 16 + 16)
                pe.matmul(ps[:, CHS, 0:NS], vtok[0:NS, NC], att[0:NS, NC, 0:NS], start=True, stop=True)
                for s in range(DB):
                    cols = slice(s * DS, (s + 1) * DS)
                    mm = pe.matmul(ps[:, CHS, cols], state_s[:, s], qdec[:, SEQ + s * DS:SEQ + (s + 1) * DS],
                                   start=False, stop=True, skip_group_check=True)
                ht.done(mm, "o")
                hv.wait(pe, "vdiag", h)
                hv.wait(pe, f"state{NC}", h)
                for f in range(2):
                    mm = pe.matmul(ps[:, 5 + f], ktok[0:NS, NC], vdiag[:, 4 * f:4 * f + 4].rearrange("p b v -> p (b v)"),
                                   start=True, stop=True)
                ht.done(mm, "add_s")
                ha.wait(pe, "square_o", h)
                for t, bank in enumerate((CH0, CH1, CHS)):
                    mm = pe.matmul(ps[:, bank, 0:TT], ones[:], cum[:, t * TT:(t + 1) * TT], start=True, stop=True)
                ht.done(mm, "stat_o")

        def vec_head(dve, h, piece, b):
            q, f, v, g = (raw[:, b, j] for j in range(4))
            TT_, STT = dve.tensor_tensor, dve.scalar_tensor_tensor

            def col(a):
                return a[:, bass.ds(h, 1)] if not isinstance(h, int) else a[:, h:h + 1]

            def step(name, fn, *args):
                hv.wait_last(dve, h)
                hv.done(fn(*args), name)

            def diff(l):
                if l > 2:
                    ht.wait(dve, f"score{l - 2}", h)
                n = span(l)
                whole = cum[:, 0:n].rearrange("p (n t) -> p n t", t=1 << l)
                ref = whole[:, :, (1 << (l - 1)) - 1:(1 << (l - 1))].broadcast_to(list(whole.shape))
                step(f"diff{l}", TT_, lev[:, l % 2, 0:n].rearrange("p (n t) -> p n t", t=1 << l), whole, ref, ALU.subtract)

            def pick(l):
                ht.wait(dve, f"score{l}", h)
                half = 1 << (l - 1)

                def right(ap):
                    return ap.rearrange("p c (n f t) -> p c n f t", f=2, t=half)[:, :, :, 1]

                n = 64 // half
                hv.wait_last(dve, h)
                out, m = right(att[:, 0:NC]), right(bc(masks[:, l], 1, NC))
                src = ps[:, 5 + l % 2].rearrange("p (c n t) -> p c n t", c=NC, n=n)
                if l == 1:
                    out, m, src = (z.rearrange("p c n t -> p c (n t)") for z in (out, m, src))
                dve.sem_inc(pick_turn, 1)
                hv.done(dve.copy_predicated(out, m, src), f"pick{l}")
                if l in SAMPLE_LEVELS:
                    out = att[0:NS, NC, 0:NS].rearrange("p (n f t) -> p n f t", f=2, t=half)[:, :, 1]
                    m = masks[0:NS, l, 0:NS].rearrange("p (n f t) -> p n f t", f=2, t=half)[:, :, 1]
                    src = ps[0:NS, CHS, l * P:l * P + NS // 2].rearrange("p (n t) -> p n t", t=half)
                    hv.wait_last(dve, h)
                    dve.sem_inc(pick_turn, 1)
                    hv.done(dve.copy_predicated(out, m, src), f"pick_s{l}")

            if piece == 0:
                ha.wait(dve, "sig_g", h)
                step("query", TT_, q, q, qdec, ALU.mult)
                step("gate", TT_, g, g, kdec, ALU.mult)
                step("key", dve.tensor_scalar, key[:], key[:], col(one_less), None, ALU.mult)
                ha.wait(dve, "ln1", h)
                step("logsig", STT, f, f, 0.0, qdec, ALU.min, ALU.subtract)
                step("gap", dve.tensor_scalar, qdec, f, col(log_gap), None, ALU.add)
                ha.wait(dve, "ln2", h)
                step("floor", dve.tensor_scalar, f, f, col(log_less), col(log_lb), ALU.add, ALU.max)
                step("logf", TT_, f, f, qdec, ALU.add)
                step("cum", dve.tensor_tensor_scan, cum[:], reset[:], f, 0.0, ALU.mult, ALU.add)
            if piece == 1:
                whole = cum[:, 0:SEQ].rearrange("p (c t) -> p c t", t=P)
                step("kd", TT_, kdec[:, 0:SEQ].rearrange("p (c t) -> p c t", t=P),
                     whole[:, :, P - 1:P].broadcast_to([P, NC, P]), whole, ALU.subtract)
                whole = cum[:, SEQ:T].rearrange("p (c t) -> p c t", t=DS)
                step("kds", TT_, kdec[:, SEQ:T].rearrange("p (c t) -> p c t", t=DS),
                     whole[:, :, DS - 1:DS].broadcast_to([P, DB, DS]), whole, ALU.subtract)
                ha.wait(dve, "ecum", h)
                step("qdec", TT_, qdec, qdec, q, ALU.mult)
                ha.wait(dve, "ekd", h)
                step("kdec", TT_, kdec, kdec, key[:], ALU.mult)
                diff(1)
            for l in {1: (1, 2, 3), 2: (4, 5, 6, 7)}.get(piece, ()):
                if l < 7:
                    diff(l + 1)
                n = span(l)
                ha.wait(dve, f"exp_r{l}", h)
                x_ = lev[:, l % 2]
                step(f"left{l}", TT_, blocks(x_, l, 0, n), blocks(x_, l, 0, n), blocks(key[:], l, 0, n), ALU.mult)
                step(f"right{l}", TT_, blocks(x_, l, 1, n), blocks(x_, l, 1, n), blocks(q, l, 1, n), ALU.mult)
                if l == 1:
                    ht.wait(dve, "diag", h)
                    step("diag", TT_, att[:, 0:NC], ps[:, CH0:CH1 + 1].rearrange("p a (c t) -> p (a c) t", t=P),
                         bc(ident[:], 1, NC), ALU.mult)
                    step("diag_s", TT_, att[0:NS, NC, 0:NS], ps[0:NS, CHS, 0:NS], ident[0:NS, 0:NS], ALU.mult)
                if l > 1:
                    pick(l - 1)
            if piece == 3:
                pick(7)
                ha.wait(dve, "ktok_s", h)
                step("vdiag", TT_, vdiag[:], bc(vtok[0:NS, NC], 1, DB), bc(own_seq[:], 2, P), ALU.mult)
                for c in range(NC):
                    ht.wait(dve, f"add{c}", h)
                    if c == 0:
                        step("state1", dve.tensor_copy, state[:, 1], ps[:, 5, 0:P])
                    else:
                        step(f"state{c + 1}", STT, state[:, (c + 1) % 2], state[:, c % 2], last[:, c:c + 1],
                             ps[:, 5 + c % 2, 0:P], ALU.mult, ALU.add)
                ht.wait(dve, "o", h)
                o = key
                step("o_p", dve.tensor_copy, o[:, 0:SEQ].rearrange("p (a n) -> p a n", a=2), ps[:, CH0:CH1 + 1])
                step("o_s", dve.tensor_copy, o[:, SEQ:T], ps[:, CHS, 0:NS])
                dve.wait_ge(hs_in, h * 16 + 16)
                step("decay_s", TT_, state_s[:], state_s[:], bc(last[:, NC:], 2, P), ALU.mult)
                ht.wait(dve, "add_s", h)
                step("state_s", TT_, state_s[:], state_s[:], ps[:, 5:7].rearrange("p a (b v) -> p (a b) v", v=P), ALU.add)
                ht.wait(dve, "stat_o", h)
                m = lev[:, 1]
                hv.wait_last(dve, h)
                dve.tensor_scalar(t3(m)[:, 0:2], ps[:, CH0:CH1 + 1, 0:TT], 1.0 / P, EPS, ALU.mult, ALU.add)
                hv.done(dve.tensor_scalar(t3(m)[:, 2], ps[:, CHS, 0:TT], 1.0 / P, EPS, ALU.mult, ALU.add), "mean_o")
                ha.wait(dve, "rstd_o", h)
                step("scaled_o", TT_, o[:], o[:], m, ALU.mult)
                step("out", STT, c_out[:, h] if isinstance(h, int) else c_out[:, bass.ds(h, 1)].rearrange("p a t -> p (a t)"), o[:], gnorm[:, 0:1], g, ALU.mult, ALU.mult)

        def act_head(act, h, piece, b):
            q, f, v, g = (raw[:, b, j] for j in range(4))

            def step(name, *args, **kw):
                ha.wait_last(act, h)
                ha.done(act.activation(*args, **kw), name)

            if piece == 0:
                he.wait(act, "e3", h)
                hv.wait(act, "out", h - 1)
                act.dma_start(state_s[:].rearrange("p b v -> p (b v)"), head_row(io["h_in"], h)).then_inc(hs_in, 16)
                step("sig_q", qdec, q, ACT.Sigmoid)
                step("sig_f", key[:], f, ACT.Sigmoid, scale=-1.0)
                step("sig_g", kdec, g, ACT.Sigmoid)
                hv.wait(act, "query", h)
                step("abs1", qdec, f, ACT.Abs)
                step("exp1", qdec, qdec, ACT.Exp, scale=-1.0)
                step("ln1", qdec, qdec, ACT.Ln, bias=1.0)
                hv.wait(act, "gap", h)
                step("abs2", qdec, qdec, ACT.Abs)
                step("exp2", qdec, qdec, ACT.Exp, scale=-1.0)
                step("ln2", qdec, qdec, ACT.Ln, bias=1.0)
                ht.wait(act, "vturn", h)
                step("vtok", vtok[:, 0:NC], ps[:, CH0:CH1 + 1].rearrange("p a (c t) -> p (a c) t", t=P), ACT.Copy)
                step("vtok_s", vtok[0:NS, NC], ps[0:NS, CHS, 0:P], ACT.Copy)
            if piece == 1:
                hv.wait(act, "cum", h)
                step("ecum", qdec, cum[:], ACT.Exp)
                step("elast", last[:, 0:NC], cum[:, P - 1:SEQ:P], ACT.Exp)
                step("elast_s", last[:, NC:], cum[:, SEQ + DS - 1:T:DS], ACT.Exp)
                hv.wait(act, "kds", h)
                step("ekd", kdec, kdec, ACT.Exp)
            for l in {1: (1, 2, 3), 2: (4, 5, 6, 7)}.get(piece, ()):
                n = span(l)
                x_ = lev[:, l % 2]
                hv.wait(act, f"diff{l}", h)
                step(f"exp_l{l}", blocks(x_, l, 0, n), blocks(x_, l, 0, n), ACT.Exp, scale=-1.0)
                step(f"exp_r{l}", blocks(x_, l, 1, n), blocks(x_, l, 1, n), ACT.Exp)
            if piece == 2:
                ht.wait(act, "kturn", h)
                step("ktok", ktok[:, 0:NC], ps[:, CH0:CH1 + 1].rearrange("p a (c t) -> p (a c) t", t=P), ACT.Copy)
                step("ktok_s", ktok[0:NS, NC], ps[0:NS, CHS, 0:P], ACT.Copy)
            if piece == 3:
                hv.wait(act, f"state{NC}", h)
                act.dma_start(head_row(io["h_prompt"], h), state[:, NC % 2]).then_inc(hp_out, 16)
                hv.wait(act, "o_s", h)
                step("square_o", cum[:], key[:], ACT.Square)
                hv.wait(act, "state_s", h)
                act.dma_start(head_row(io["h_sample"], h), state_s[:].rearrange("p b v -> p (b v)")).then_inc(hs_out, 16)
                hv.wait(act, "mean_o", h)
                step("ln_o", lev[:, 1], lev[:, 1], ACT.Ln)
                step("rstd_o", lev[:, 1], lev[:, 1], ACT.Exp, scale=-0.5)
                act.wait_ge(hs_out, h * 16 + 16)
                act.wait_ge(hp_out, h * 16 + 16)

        def heads(eng, unit_fn, head_fn):
            def both(h, b):
                for j in range(4):
                    if unit_fn:
                        unit_fn(eng, h + 1, j, 1 - b)
                    head_fn(eng, h, j, b)

            if unit_fn:
                for j in range(4):
                    unit_fn(eng, 0, j, 0)
            with eng.Fori(0, HH // 2 - 1) as i:
                for b in range(2):
                    both(i * 2 + b, b)
            both(HH - 2, 0)
            for j in range(4):
                head_fn(eng, HH - 1, j, 1)

        def act_lower_bound(act):
            act.wait_ge(lb_s, 1)
            act.activation(lb[:, 5], lb[:, 5], ACT.Exp).then_inc(lb_e, 1)
            act.wait_ge(lb_s, 2)
            act.activation(lb[:, 1], lb[:, 0], ACT.Ln).then_inc(lb_l, 1)
            act.activation(lb[:, 2], lb[:, 5], ACT.Ln).then_inc(lb_l, 1)

        def vec_lower_bound(dve):
            c = Chain(dve, lb_r)
            dve.wait_ge(hc_in, 16 * 5)
            c(dve.tensor_copy(masks[:], masks_in[:]))
            c.after(); c(dve.tensor_copy(reset[:], reset_in[:]))
            c.after(); c(dve.tensor_tensor(lb[:, 5], lb[:, 4], lb[:, 4], ALU.subtract), lb_s)
            dve.wait_ge(lb_e, 1)
            c.after(); c(dve.reciprocal(lb[:, 0], lb[:, 5]))
            c.after(); c(dve.tensor_tensor(lb[:, 5], lb[:, 5], lb[:, 0], ALU.mult))
            c.after(); c(dve.tensor_tensor(lb[:, 5], lb[:, 5], lb[:, 5], ALU.subtract))
            c.after(); c(dve.tensor_scalar(lb[:, 0], lb[:, 5], -1.0, 1.0, ALU.mult, ALU.add))
            c.after(); c(dve.tensor_scalar(lb[:, 5], lb[:, 5], LOG_FLOOR, 2.0 ** 50, ALU.max, ALU.mult), lb_s)
            dve.wait_ge(lb_l, 2)
            c.after(); c(dve.tensor_scalar(lb[:, 2], lb[:, 2], -50 * math.log(2.0), None, ALU.add))
            c.after(); c(dve.tensor_tensor(lb[:, 3], lb[:, 1], lb[:, 2], ALU.subtract))
            c.after()

        def act_hgrn_loads(act):
            for dst, name in ((reset_in[:], "reset"), (lb[:, 4], "lb"), (gnorm[:], "gnorm"), (own_seq[:], "own_seq"),
                              (masks_in[:], "masks")):
                act.dma_start(dst, io[name]).then_inc(hc_in, 16)

        out_hi, out_lo = sem("out_hi"), sem("out_lo")

        def act_out_split(act):
            act.wait_ge(unit_done, LOOKBACK + FIRST_UNIT["out_odd"])
            for k in range(KC):
                act.activation(a_hi[:, k], c_out[:, k], ACT.Copy).then_inc(out_hi, 1)

        def vec_out_split(dve):
            for k in range(KC):
                dve.wait_ge(out_hi, k + 1)
                dve.tensor_tensor(a_lo[:, k], c_out[:, k], a_hi[:, k].bitcast(F32), ALU.subtract).then_inc(out_lo, 1)

        load = Boundary("load", None, 0)
        mix0 = Boundary("mix0", 1, 2)
        end0 = Boundary("mlp0_end", 3, 4)
        mix1 = Boundary("mix1", 5, 6)
        end1 = Boundary("mlp1_end", 7, None)
        out_even, out_odd = OutProjection("out_even", mix0), OutProjection("out_odd", mix1)
        mlp0, mlp1 = Mlp("mlp0", mix0, end0), Mlp("mlp1", mix1, end1)
        ones_set = sem("ones_set")
        block = ctx.enter_context(nc.Block())

        def x_ready(n):
            return lambda eng, k: eng.wait_ge(x_in[k], 16 * n)

        @block.sync
        def _(sp):
            sp_weights(sp)

        @block.gpsimd
        def _(pool):
            pool.wait_ge(ones_set, 1)
            pool_weights(pool)

        @block.tensor
        def _(pe):
            pe.sem_inc(unit_done, LOOKBACK)
            pe.wait_ge(ones_set, 1)
            pe.wait_ge(consts_in, 32)
            pe_bias_rows(pe)
            pe.wait_ge(rel_read, 1)
            load.tensor(pe)
            pe.sem_inc(in_evac, LOOKBACK)
            pe_projection(pe, "in_even", in_evac)
            pe_s5(pe)
            pe_attention(pe)
            pe_glu(pe)
            out_even.tensor(pe)
            mix0.tensor(pe)
            mlp0.tensor(pe)
            end0.tensor(pe)
            ht.prime(pe)
            heads(pe, pe_head_unit, pe_head)
            pe.wait_ge(out_lo, KC)
            out_odd.tensor(pe)
            mix1.tensor(pe)
            mlp1.tensor(pe)
            end1.tensor(pe)

        @block.vector
        def _(dve):
            dve.memset(ones[:], 1.0).then_inc(ones_set, 1)
            vec_bias_rows(dve)
            dve.wait_ge(consts_in, 32)
            load.vector(dve, x_ready(1))
            c = vec_in_even(dve)
            vec_s5(dve, c)
            vec_attention(dve, c)
            vec_glu(dve, c)
            dve.wait_ge(k_out, 16 * K_OUTS)
            out_even.vector(dve)
            mix0.vector(dve, x_ready(2))
            mlp0.vector(dve)
            end0.vector(dve)
            dve.wait_ge(x_saved, 16 * KC)
            vec_lower_bound(dve)
            end0.act.wait(dve, "rstd_x")
            he.prime(dve)
            hv.prime(dve)
            heads(dve, vec_head_unit, vec_head)
            vec_out_split(dve)
            out_odd.vector(dve)
            mix1.vector(dve, x_ready(3))
            mlp1.vector(dve)
            end1.vector(dve)

        @block.scalar
        def _(act):
            act.dma_start(gains[:], io["gains"]).then_inc(consts_in, 16)
            act.dma_start(ident[:], io["ident"]).then_inc(consts_in, 16)
            for k in range(KC):
                act.dma_start(x[:, k], io["x"][k]).then_inc(x_in[k], 16)
            act_bias_rows(act)
            act.wait_ge(consts_in, 32)
            load.scalar(act, x_ready(1))
            load.act.wait(act, "rstd_x")
            act_s5_loads(act)
            act_prepare(act)
            act_s5(act)
            act_at_loads(act)
            act_attention(act)
            act_glu(act)
            act.wait_ge(mix_lo, 8)
            act.wait_ge(unit_done, LOOKBACK + FIRST_UNIT["out_even"])
            act.wait_ge(s5_out, 32)
            for k in range(KC):
                act.dma_start(x[:, k], io["x"][k]).then_inc(x_in[k], 16)
            out_even.scalar(act)
            mix0.scalar(act, x_ready(2))
            mlp0.scalar(act)
            end0.scalar(act, on_x=lambda e, k: e.dma_start(io["x_scratch"][k], x[:, k]).then_inc(x_saved, 16))
            act.wait_ge(x_saved, 16 * KC)
            end0.act.wait(act, "rstd_x")
            ha.prime(act)
            act_hgrn_loads(act)
            act_lower_bound(act)
            heads(act, None, act_head)
            hv.wait(act, "out", HH - 1)
            for k in range(KC):
                act.dma_start(x[:, k], io["x_scratch"][k]).then_inc(x_in[k], 16)
            act_out_split(act)
            out_odd.scalar(act)
            mix1.scalar(act, x_ready(3))
            mlp1.scalar(act)
            end1.scalar(act, on_x=lambda e, k: e.dma_start(io["y"][k], x[:, k]).then_inc(y_out, 16))
            act.wait_ge(y_out, 16 * KC)
            act.wait_ge(k_out, 16 * K_OUTS)
            act.wait_ge(s5_out, 32)
            act.wait_ge(hp_out, 16 * HH)
            act.wait_ge(hs_out, 16 * HH)


def relative_buckets():
    w = 128
    distance = 2 * w - 1 - np.arange(3 * w)
    inside = (distance >= 0) & (distance < w)
    n = np.maximum(distance, 0)
    large = 16 + (np.log(np.maximum(n, 16).astype(np.float32) / np.float32(16)) / np.float32(math.log(8))
                  * np.float32(16)).astype(np.int32)
    bucket = np.where(n < 16, n, np.minimum(large, 31))
    rows = np.zeros((33, 3 * w), np.float32)
    rows[bucket[inside], np.arange(3 * w)[inside]] = 1
    rows[32, ~inside] = -1e30
    return rows


def level_masks():
    s, t = np.arange(P)[:, None], np.arange(P)[None, :]
    out = np.zeros((P, 8, P), np.float32)
    for l in range(1, 8):
        h = 1 << (l - 1)
        out[:, l] = ((t & h) != 0) & ((s & h) == 0) & (s >> l == t >> l)
    return out


def weight_stream(w_in_even, w_glu, w_out_even, w_up, w_down, w_in_odd, w_out_odd, q_rows):
    def wide(w, c):
        return w[:, c:c + P].reshape(KC, P, P).transpose(1, 0, 2).reshape(P, KC * P)

    def halves(w, c):
        return np.concatenate([w[:, d:d + P].reshape(4, P, P).transpose(1, 0, 2) for d in (c, c + P)],
                              axis=1).reshape(P, KC * P)

    def mlp(up, down):
        out = []
        for g in range(GROUPS):
            out += [wide(up, (g * HID + j) * P) for j in range(HID)]
            out += [halves(down[g * HID * P:(g + 1) * HID * P], 2 * P * c) for c in range(4)]
        return out

    half = D // 2
    in_even = w_in_even[:, np.concatenate([np.arange(half), q_rows, np.arange(2 * half, 2 * half + 2 * P)])]
    out_even = w_out_even[np.concatenate([np.arange(half), q_rows])]
    blocks = [wide(in_even, n * P) for n in range(10)] + [halves(w_glu, 2 * P * c) for c in range(2)]
    blocks += [wide(out_even, n * P) for n in range(KC)] + mlp(w_up[0], w_down[0])
    blocks += [wide(w_in_odd, part * D + h * P) for h in range(KC) for part in range(4)]
    blocks += [wide(w_out_odd, n * P) for n in range(KC)] + mlp(w_up[1], w_down[1])
    assert len(blocks) == BLOCKS
    return np.stack(blocks)


def layout(i):
    def c(a):
        return np.ascontiguousarray(a)

    o = {}
    x = np.concatenate([i["x_prompt"].reshape(SEQ, D), i["x_sample"].reshape(NS, D)])
    o["x"] = c(x.T.reshape(KC, P, T))
    norms = [i[n][layer] for layer in range(2)
             for n in ("norm_mix_pre", "norm_mix_post", "norm_mlp_pre", "norm_mlp_post")]
    o["gains"] = c(np.stack(norms).reshape(8, KC, P).transpose(2, 0, 1))
    heads = np.array([[kv * 4 + hh for kv in range(2)] for hh in range(4)]).ravel()
    q_rows = (D // 2 + heads[:, None] * 64 + np.arange(64)).ravel()
    o["w"] = weight_stream(i["w_in_even"][0], i["s5_w_glu"][0], i["w_out_even"][0], i["w_up"], i["w_down"],
                           i["w_in_odd"][0], i["w_out_odd"][0], q_rows)
    step = np.broadcast_to(i["s5_log_step"][0][:, None], (32, 64))
    lam = np.stack([i["s5_lambda_re"][0], i["s5_lambda_im"][0], step])
    o["s5_lam"] = c(lam.reshape(3, 16, 2, 64).transpose(2, 3, 0, 1).reshape(P, 3, 16))
    b = np.stack([i["s5_b_re"][0], i["s5_b_im"][0]])
    o["s5_b"] = c(b.reshape(2, 16, 2, 64, 16).transpose(2, 3, 0, 1, 4).reshape(P, 2, 16, 16))
    cc = np.stack([i["s5_c_re"][0], i["s5_c_im"][0]]).transpose(0, 1, 3, 2)
    o["s5_c"] = c(cc.reshape(2, 16, 2, 64, 16).transpose(2, 3, 0, 1, 4).reshape(P, 2, 16, 16))
    d = i["s5_d"][0].reshape(16, 2, 16)
    diag = np.zeros((16, 32, 16), np.float32)
    for ch in range(16):
        diag[ch, :, ch] = d[:, :, ch].T.ravel()
    o["s5_d"] = diag
    h = np.stack([i["state_s5_re"][0], i["state_s5_im"][0]])
    o["s5_h0"] = c(h.reshape(2, DB, 16, 2, 64).transpose(3, 4, 0, 2, 1).reshape(P, 2, 16, DB))
    o["kvec"] = np.broadcast_to(np.array(list(range(9)) + list(range(7, -1, -1)), np.float32), (P, 17)).copy()
    o["ident"] = np.eye(P, dtype=np.float32)
    o["buckets"] = relative_buckets()
    o["table"] = np.concatenate([i["t5_bias_table"], np.ones((1, 8), np.float32)])
    sinks = i["swa_sinks"][0]
    o["sinks"] = np.broadcast_to(sinks, (P, 8)).copy()
    o["sinks_s"] = c(np.repeat(sinks.reshape(2, 4), NS, axis=1).T)
    other = np.full((4, DB, DS, DB), -1e30, np.float32)
    for s in range(DB):
        other[:, s, :, s] = 0
    o["other"] = other.reshape(P, DB)
    o["c_k"] = c(i["cache_swa_k"][0].transpose(2, 3, 0, 1).reshape(P, DB, P))
    o["c_vt"] = c(i["cache_swa_v"][0].transpose(2, 3, 0, 1).reshape(P, DB, P))
    o["c_v"] = c(i["cache_swa_v"][0].transpose(1, 0, 2, 3).reshape(P, DB, P))
    o["masks"] = level_masks()
    reset = np.ones((P, T), np.float32)
    reset[:, 0:SEQ:P] = 0
    reset[:, SEQ:T:DS] = 0
    o["reset"] = reset
    o["own_seq"] = (np.arange(NS)[:, None] // DS == np.arange(DB)).astype(np.float32)
    o["lb"] = c(i["hgrn_lb_param"][0].reshape(KC, P).T)
    o["gnorm"] = c(i["hgrn_gnorm"][0].reshape(P, 1))
    o["h_in"] = c(i["state_hgrn"][0].transpose(1, 2, 0, 3).reshape(KC, P, DB * P))
    return o


OUTPUTS = {"y": (KC, P, T), "s5_prompt": (P, 2, 16), "s5_sample": (P, 2, 16, DB),
           "k_prompt": (P, P), "v_prompt": (P, P), "k_sample": (P, DB, P), "v_sample": (P, DB, P),
           "h_prompt": (KC, P, P), "h_sample": (KC, P, DB * P)}
SCRATCH = {"skew": (P * 3200,), "u_scratch": (D // 2, T), "g_scratch": (D // 2, T), "x_scratch": (KC, P, T)}


def results(o):
    y = o["y"].reshape(D, T).T
    s5p = o["s5_prompt"].reshape(2, 64, 2, 16).transpose(2, 3, 0, 1).reshape(2, 1, 1, 32, 64)
    s5s = o["s5_sample"].reshape(2, 64, 2, 16, DB).transpose(2, 4, 3, 0, 1).reshape(2, 1, DB, 32, 64)
    kp, vp = (o[n].reshape(2, 64, P).transpose(2, 0, 1)[None, None] for n in ("k_prompt", "v_prompt"))
    ks, vs = (o[n].reshape(2, 64, DB, P).transpose(2, 3, 0, 1)[None] for n in ("k_sample", "v_sample"))
    hp = o["h_prompt"][None, None]
    hs = o["h_sample"].reshape(KC, P, DB, P).transpose(2, 0, 1, 3)[None]
    return tuple(np.ascontiguousarray(a) for a in (
        y[:SEQ].reshape(1, SEQ, D), y[SEQ:].reshape(DB, DS, D), kp, vp, ks, vs, s5p[0], s5p[1], s5s[0], s5s[1], hp, hs))


def kernel(**inputs):
    import concourse.bacc as bacc
    from concourse.bass_utils import run_bass_kernel_spmd

    nc = bacc.Bacc("TRN2", target_bir_lowering=False, num_devices=1)
    arrays = layout({name: np.asarray(a) for name, a in inputs.items()})
    io = {name: nc.dram_tensor(name, a.shape, mybir.dt.from_np(a.dtype), kind="ExternalInput").ap()
          for name, a in arrays.items()}
    for name, shape in OUTPUTS.items():
        io[name] = nc.dram_tensor(name, shape, F32, kind="ExternalOutput").ap()
    for name, shape in SCRATCH.items():
        io[name] = nc.dram_tensor(name, shape, F32, kind="Internal").ap()
    build_trunk(nc, io)
    run = run_bass_kernel_spmd(nc, [arrays], core_ids=[0])
    return results({name: run.results[0][name] for name in OUTPUTS})
```

```python
import math
from contextlib import ExitStack

import numpy as np

import concourse.bass as bass
from concourse import mybir

F32 = mybir.dt.float32
F32R = mybir.dt.float32r
I32 = mybir.dt.int32
U8 = mybir.dt.uint8
ALU = mybir.AluOpType
ACT = mybir.ActivationFunctionType
AX_X = mybir.AxisListType.X

P = 128
D = 1024
KC = D // P
SEQ = 1024
DB, DS = 8, 4
NS = DB * DS
T = SEQ + NS
TT = T // 3
FF = 4 * D
EPS = 1e-6
HID = 4
GROUPS = FF // (HID * P)
LOOKBACK = 2

STREAM = [("in_even", 10, 10), ("glu", 2, 4), ("out_even", 8, 8), ("mlp0", 64, 96),
          ("in_odd", 32, 32), ("out_odd", 8, 8), ("mlp1", 64, 96)]
FIRST_BLOCK, FIRST_UNIT = {}, {}
LOG_FLOOR = 1e-30
LOG_EXP_SET = 6
ROUND = 1.5 * 2.0 ** 23
TWO_PI = (6.28125, 0.0019350051879882812, 3.0199159819567e-07)
PI_BELOW = 3.14159250259
_b = _u = 0
for _name, _nb, _nu in STREAM:
    FIRST_BLOCK[_name], FIRST_UNIT[_name] = _b, _u
    _b, _u = _b + _nb, _u + _nu
BLOCKS = _b


class Steps:

    def __init__(self, sem, names):
        self.sem, self.names, self.next = sem, list(names), 0
        self.index = {n: i for i, n in enumerate(self.names)}
        assert len(self.index) == len(self.names)

    def prime(self, eng):
        eng.sem_inc(self.sem, len(self.names))

    def at(self, name, turn=0):
        return turn * len(self.names) + (len(self.names) + self.index[name] + 1)

    def done(self, ins, name):
        assert self.names[self.next] == name, (self.names[self.next], name)
        self.next = (self.next + 1) % len(self.names)
        return ins.then_inc(self.sem, 1)

    def wait(self, eng, name, turn=0):
        eng.wait_ge(self.sem, self.at(name, turn))

    def wait_last(self, eng, turn=0):
        eng.wait_ge(self.sem, turn * len(self.names) + (len(self.names) + self.next))


def t3(ap):
    return ap.rearrange("p (a t) -> p a t", a=3)


def build_trunk(nc, io):
    with ExitStack() as ctx:
        BASE = 16512
        W_RAW, W_HI, W_LO = BASE, BASE + 8192, BASE + 16384
        A_HI = BASE + 24576
        A_LO = A_HI + KC * T * 4
        R1 = A_LO + KC * T * 4

        def at(name, shape, offset, dt=F32):
            return nc.alloc_sbuf_tensor_at(name, shape, dt, offset=offset)

        w_raw = at("w_raw", [P, 2, KC * P], W_RAW)
        w_hi = at("w_hi", [P, 2, KC, P], W_HI, F32R)
        w_lo = at("w_lo", [P, 2, KC, P], W_LO, F32R)
        a_hi = at("a_hi", [P, KC, T], A_HI, F32R)
        a_lo = at("a_lo", [P, KC, T], A_LO, F32R)
        h_hi = at("h_hi", [P, HID, T], R1, F32R)
        h_lo = at("h_lo", [P, HID, T], R1 + 16896, F32R)
        y = at("y", [P, KC, T], R1 + 33792)
        x = at("x", [P, KC, T], R1 + 67584)
        rstd = at("rstd", [P, T], R1 + 101376)
        ssq = at("ssq", [P, T], R1 + 105600)
        sq = at("sq", [P, 2, T], R1 + 109824)
        gains = at("gains", [P, 8, KC], R1 + 118272)
        ones = at("ones", [P, P], R1 + 118528)
        CONST_END = R1 + 119040
        assert CONST_END <= nc.sbuf_usable_end

        ps = ctx.enter_context(nc.psum_tensor("ps", [P, 8, 512], F32))

        def sem(name):
            return ctx.enter_context(nc.semaphore(name))

        w_loaded = [sem("w_loaded0"), sem("w_loaded1")]
        hi_made = sem("w_hi_made")
        w_ready = sem("w_ready")
        unit_done = sem("unit_done")
        consts_in = sem("consts_in")
        x_in = [sem(f"x_in{k}") for k in range(KC)]
        x_saved = sem("x_saved")
        y_out = sem("y_out")

        def unit(slot):
            return ps[:, 3 * slot:3 * slot + 3, 0:TT]

        def load_log_exp(act):
            act.add_instruction(mybir.InstLoadActFuncSet(act_func_set_id=LOG_EXP_SET, engine=mybir.EngineType.Activation,
                                                         name=nc.get_next_instruction_name(), ins=[], outs=[]))

        def sp_weights(sp):
            with sp.Fori(0, BLOCKS // 2) as i:
                for b in range(2):
                    sp.wait_ge(w_ready, i * 2 + b + 1)
                    sp.dma_start(w_raw[:, b, :], io["w"][bass.ds(i * 2 + b, 1)].rearrange("a p n -> p (a n)")
                                 ).then_inc(w_loaded[b], 16)

        def pool_split(pool, count, b, turn_of_slot, free_at):
            pool.wait_ge(w_loaded[b], turn_of_slot)
            pool.wait_ge(unit_done, free_at)
            pool.wait_ge(w_ready, count + LOOKBACK)
            hi, lo = (w[:, b].rearrange("p k m -> p (k m)") for w in (w_hi, w_lo))
            pool.tensor_tensor(hi, w_raw[:, b, :], ones[:, 0:1].broadcast_to([P, KC * P]), ALU.mult).then_inc(hi_made, 1)
            pool.wait_ge(hi_made, count + 1)
            pool.tensor_tensor(lo, w_raw[:, b, :], hi.bitcast(F32), ALU.subtract).then_inc(w_ready, 1)

        def pool_weights(pool):
            pool.sem_inc(w_ready, LOOKBACK)
            for name, nb, nu in STREAM:
                n0, u0 = FIRST_BLOCK[name], FIRST_UNIT[name]
                if name.startswith("mlp"):
                    ahead = [-1, 0, 1, 2, 3, 4, 6, 8]
                    with pool.Fori(0, GROUPS) as g:
                        for j in range(8):
                            pool_split(pool, g * 8 + (n0 + j), j % 2, g * 64 + 16 * (n0 // 2 + j // 2 + 1),
                                       g * 12 + (LOOKBACK + u0 + ahead[j]))
                else:
                    per = nu // nb
                    with pool.Fori(0, nb // 2) as i:
                        for b in range(2):
                            pool_split(pool, i * 2 + (n0 + b), b, i * 16 + 16 * (n0 // 2 + 1),
                                       i * (2 * per) + (LOOKBACK + u0 - 1 + b))

        def pe_unit(pe, b, slot, ks, act, ready=None, wk=None):
            tiles = unit(slot)
            for n, k in enumerate(ks):
                if ready:
                    ready(k)
                w = n if wk is None else wk + n
                for t in range(3):
                    cols = slice(t * TT, (t + 1) * TT)
                    for i, (wt, at_) in enumerate(((w_hi, act[0]), (w_hi, act[1]), (w_lo, act[0]))):
                        mm = pe.matmul(tiles[:, t], wt[:, b, w], at_[:, k, cols],
                                       start=(n == 0 and i == 0), stop=(n == len(ks) - 1 and i == 2))
            mm.then_inc(unit_done, 1)

        def pe_first_unit(pe, name, tile_done=None):
            def part(k):
                if k == 0:
                    pe.wait_ge(w_ready, FIRST_BLOCK[name] + 1 + LOOKBACK)
                for t in range(3):
                    cols = slice(t * TT, (t + 1) * TT)
                    for i, (wt, at_) in enumerate(((w_hi, a_hi), (w_hi, a_lo), (w_lo, a_hi))):
                        mm = pe.matmul(unit(0)[:, t], wt[:, 0, k], at_[:, k, cols],
                                       start=(k == 0 and i == 0), stop=(k == KC - 1 and i == 2))
                    if k == KC - 1 and (tile_done or t == 2):
                        mm.then_inc(unit_done if t == 2 else tile_done, 1)
            return part

        def pe_projection(pe, name, evacuated, started=False):
            n0, nb = FIRST_BLOCK[name], dict((s[0], s[1]) for s in STREAM)[name]

            def one(i, b):
                pe.wait_ge(w_ready, i * 2 + (n0 + b + 1 + LOOKBACK))
                pe.wait_ge(evacuated, i * 2 + (b + 1))
                pe_unit(pe, b, b, range(KC), (a_hi, a_lo))

            if started:
                one(0, 1)
            with pe.Fori(1 if started else 0, nb // 2) as i:
                for b in range(2):
                    one(i, b)

        class Boundary:

            def __init__(self, tag, post, pre):
                self.tag, self.post, self.pre = tag, post, pre
                vec, act = [], []
                if post is not None:
                    vec.append("mean_y")
                    act += ["ln_y", "rstd_y"]
                for k in range(KC):
                    if post is not None:
                        vec += [f"scaled{k}", f"x{k}"]
                    if pre is not None:
                        if k > 0:
                            vec.append(f"lo{k - 1}")
                        act += [f"hi{k}", f"sq{k}"]
                if pre is not None:
                    vec += [f"lo{KC - 1}", "mean_x"]
                    act += ["ln_x", "rstd_x"]
                self.vec = Steps(sem(f"{tag}_vec"), vec)
                self.act = Steps(sem(f"{tag}_act"), act)
                if pre is not None:
                    self.stat_x = sem(f"{tag}_stat_x")
                if post is not None:
                    self.ssq_ready = sem(f"{tag}_ssq_ready")
                    self.stat_y = sem(f"{tag}_stat_y")

            def tensor(self, pe, first=None):
                if self.post is not None:
                    pe.wait_ge(self.ssq_ready, 1)
                    for t in range(3):
                        mm = pe.matmul(unit(0)[:, t], ones[:], ssq[:, t * TT:(t + 1) * TT], start=True, stop=True)
                    mm.then_inc(self.stat_y, 1)
                if self.pre is not None:
                    for k in range(KC):
                        self.act.wait(pe, f"sq{k}")
                        for t in range(3):
                            mm = pe.matmul(unit(1)[:, t], ones[:], sq[:, k % 2, t * TT:(t + 1) * TT],
                                           start=(k == 0), stop=(k == KC - 1))
                        mm.then_inc(self.stat_x, 1)
                        if k:
                            self.vec.wait(pe, f"lo{k - 1}")
                            if k == 1 and self.post is not None:
                                self.vec.wait(pe, "mean_y")
                            first(k - 1)
                    self.vec.wait(pe, f"lo{KC - 1}")
                    first(KC - 1)
                    self.vec.wait(pe, "mean_x")

            def vector(self, dve, x_ready=None):
                v = self.vec
                v.prime(dve)
                if self.post is not None:
                    dve.wait_ge(self.stat_y, 1)
                    v.done(dve.tensor_scalar(t3(ssq[:]), unit(0), 1.0 / D, EPS, ALU.mult, ALU.add), "mean_y")
                    self.act.wait(dve, "rstd_y")
                for k in range(KC):
                    if x_ready:
                        x_ready(dve, k)
                    if self.post is not None:
                        v.done(dve.tensor_tensor(y[:, k], y[:, k], rstd[:], ALU.mult), f"scaled{k}")
                        v.wait(dve, f"scaled{k}")
                        v.done(dve.scalar_tensor_tensor(x[:, k], y[:, k], gains[:, self.post, k:k + 1], x[:, k],
                                                        ALU.mult, ALU.add), f"x{k}")
                    if self.pre is not None and k > 0:
                        self.lo(dve, k - 1)
                if self.pre is not None:
                    self.lo(dve, KC - 1)
                    dve.wait_ge(self.stat_x, KC)
                    v.done(dve.tensor_scalar(t3(ssq[:]), unit(1), 1.0 / D, EPS, ALU.mult, ALU.add), "mean_x")

            def lo(self, dve, k):
                self.act.wait(dve, f"hi{k}")
                self.vec.done(dve.scalar_tensor_tensor(a_lo[:, k], x[:, k], gains[:, self.pre, k:k + 1],
                                                       a_hi[:, k].bitcast(F32), ALU.mult, ALU.subtract), f"lo{k}")

            def scalar(self, act, x_ready=None, on_x=None):
                a = self.act
                a.prime(act)
                if self.post is not None:
                    self.vec.wait(act, "mean_y")
                    self.rsqrt(act, "y")
                for k in range(KC):
                    if x_ready:
                        x_ready(act, k)
                    if self.post is not None:
                        self.vec.wait(act, f"x{k}")
                    if on_x:
                        on_x(act, k)
                    if self.pre is not None:
                        a.done(act.activation(a_hi[:, k], x[:, k], ACT.Copy, scale=gains[:, self.pre, k:k + 1]),
                               f"hi{k}")
                        if k >= 2:
                            act.wait_ge(self.stat_x, k - 1)
                        else:
                            a.wait_last(act)
                        a.done(act.activation(sq[:, k % 2], x[:, k], ACT.Square), f"sq{k}")
                if self.pre is not None:
                    self.vec.wait(act, "mean_x")
                    self.rsqrt(act, "x")

            def rsqrt(self, act, which):
                a = self.act
                load_log_exp(act)
                a.wait_last(act)
                a.done(act.activation(sq[:, 0], ssq[:], ACT.Ln), f"ln_{which}")
                a.wait_last(act)
                a.done(act.activation(rstd[:], sq[:, 0], ACT.Exp, scale=-0.5), f"rstd_{which}")

        class Mlp:
            def __init__(self, name, before, after):
                self.name, self.before, self.after = name, before, after
                vec = []
                for j in range(HID):
                    vec += [f"scaled{j}", f"squared{j}"] + ([f"lo{j - 1}"] if j else [])
                vec += [f"lo{HID - 1}"] + [f"sum{m}" for m in range(KC)]
                self.vec = Steps(sem(f"{name}_vec"), vec)
                self.act = Steps(sem(f"{name}_act"), [f"hi{j}" for j in range(HID)])
                self.sq_done = sem(f"{name}_squares")
                self.sums = sem(f"{name}_sums")
                self.u0, self.n0 = FIRST_UNIT[name], FIRST_BLOCK[name]

            def tensor(self, pe):
                v = self.vec

                def group(g, started=False):
                    for j in range(1 if started else 0, HID):
                        pe.wait_ge(w_ready, g * 8 + (self.n0 + j + 1 + LOOKBACK))
                        if j < 2:
                            v.wait(pe, f"sum{KC - 2 + j}", g - 1)
                        else:
                            v.wait(pe, f"scaled{j - 2}", g)
                        pe_unit(pe, j % 2, j % 2, range(KC), (a_hi, a_lo))
                    for m in range(KC):
                        if m % 2 == 0:
                            pe.wait_ge(w_ready, g * 8 + (self.n0 + 4 + m // 2 + 1 + LOOKBACK))
                        v.wait(pe, f"scaled{m + 2}" if m < 2 else f"sum{m - 2}", g)
                        pe_unit(pe, (m // 2) % 2, m % 2, range(HID), (h_hi, h_lo), wk=4 * (m % 2),
                                ready=(lambda k: v.wait(pe, f"lo{k}", g)) if m == 0 else None)

                group(0, started=True)
                with pe.Fori(1, GROUPS) as g:
                    group(g)

            def units(self, n, g):
                return g * 12 + (LOOKBACK + self.u0 + n + 1)

            def vec_group(self, dve, g, first, last):
                v, a = self.vec, self.act
                for j in range(HID):
                    dve.wait_ge(unit_done, self.units(j, g))
                    v.wait_last(dve, g)
                    v.done(dve.tensor_tensor(t3(ssq[:]), unit(j % 2), t3(rstd[:]), ALU.mult), f"scaled{j}")
                    v.wait_last(dve, g)
                    v.done(dve.scalar_tensor_tensor(sq[:, j % 2], ssq[:], 0.0, ssq[:], ALU.max, ALU.mult),
                           f"squared{j}")
                    if j:
                        self.lo(dve, g, j - 1)
                self.lo(dve, g, HID - 1)
                for m in range(KC):
                    dve.wait_ge(unit_done, self.units(HID + m, g))
                    v.wait_last(dve, g)
                    if first:
                        ins = dve.tensor_copy(t3(y[:, m]), unit(m % 2))
                    else:
                        ins = dve.tensor_tensor(t3(y[:, m]), unit(m % 2), t3(y[:, m]), ALU.add)
                    v.done(ins, f"sum{m}")
                    if last:
                        sum_squares(dve, m, self.sq_done, self.sums, self.after)

            def lo(self, dve, g, j):
                self.act.wait(dve, f"hi{j}", g)
                self.vec.done(dve.tensor_tensor(h_lo[:, j], sq[:, j % 2], h_hi[:, j].bitcast(F32), ALU.subtract),
                              f"lo{j}")

            def vector(self, dve):
                self.vec.prime(dve)
                self.before.act.wait(dve, "rstd_x")
                self.vec_group(dve, 0, True, False)
                with dve.Fori(1, GROUPS - 1) as g:
                    self.vec_group(dve, g, False, False)
                self.vec_group(dve, GROUPS - 1, False, True)

            def scalar(self, act):
                self.act.prime(act)
                with act.Fori(0, GROUPS) as g:
                    for j in range(HID):
                        self.vec.wait(act, f"squared{j}", g)
                        self.act.done(act.activation(h_hi[:, j], sq[:, j % 2], ACT.Copy), f"hi{j}")
                for m in range(KC):
                    self.vec.wait(act, f"sum{m}", GROUPS - 1)
                    square_y(act, m, self.sq_done, self.sums)

        def square_y(act, m, sq_done, sums):
            if m >= 2:
                act.wait_ge(sums, m - 1)
            act.activation(sq[:, m % 2], y[:, m], ACT.Square).then_inc(sq_done, 1)

        def sum_squares(dve, m, sq_done, sums, after):
            dve.wait_ge(sq_done, m + 1)
            if m == 0:
                ins = dve.tensor_copy(ssq[:], sq[:, 0])
            else:
                dve.wait_ge(sums, m)
                ins = dve.tensor_tensor(ssq[:], ssq[:], sq[:, m % 2], ALU.add)
            ins.then_inc(after.ssq_ready if m == KC - 1 else sums, 1)

        class OutProjection:

            def __init__(self, name, after):
                self.name, self.after = name, after
                self.evacuated = sem(f"{name}_evacuated")
                self.sq_done, self.sums = sem(f"{name}_squares"), sem(f"{name}_sums")

            def tensor(self, pe):
                pe.sem_inc(self.evacuated, LOOKBACK)
                pe_projection(pe, self.name, self.evacuated)

            def vector(self, dve):
                for m in range(KC):
                    dve.wait_ge(unit_done, LOOKBACK + FIRST_UNIT[self.name] + m + 1)
                    dve.tensor_copy(t3(y[:, m]), unit(m % 2)).then_inc(self.evacuated, 1)
                    sum_squares(dve, m, self.sq_done, self.sums, self.after)

            def scalar(self, act):
                for m in range(KC):
                    act.wait_ge(self.evacuated, LOOKBACK + m + 1)
                    square_y(act, m, self.sq_done, self.sums)

        CH = 8
        NCH = SEQ // CH
        SP_, SC, SG = 64, 16, 32
        GP = SG // 2
        L = CH + 1
        NU = NCH + DB
        NPOW = L + CH

        u_p = at("u_p", [P, 4, T], R1)
        q_t = at("q_t", [P, 4, T], R1 + 16896)
        k_t = at("k_t", [P, T], R1 + 33792)
        v_t = at("v_t", [P, T], R1 + 38016)
        in_st = at("in_st", [P, 2, GP, CH, SC], R1 + 42240)
        out_st = at("out_st", [P, 2, GP, L, SC], R1 + 58624)
        turn = at("turn", [P, 2, GP, NCH], R1 + 77056)
        prod = at("prod", [P, GP * L * SC], R1 + 77056)
        s0 = R1 + 93440
        bb = at("bb", [P, 2, GP, SC], s0)
        d_diag = at("d_diag", [SC, SG, SC], s0 + 2048)
        h0 = at("h0", [P, 2, GP, DB], s0 + 4096)
        pw = at("pw", [P, 2, NPOW, GP], s0 + 5120)
        mag8 = at("mag8", [P, GP], s0 + 7296)
        s1 = R1 + 105600
        lam = at("lam", [P, 3, GP], s1)
        b_in = at("b_in", [P, 2, GP, SC], s1 + 192)
        c_in = at("c_in", [P, 2, GP, SC], s1 + 2240)
        kvec = at("kvec", [P, NPOW], s1 + 4288)
        ang = at("ang", [P, NPOW, GP], s1 + 4416)
        rho = at("rho", [P, NPOW, GP], s1 + 5504)
        rnd = at("rnd", [P, NPOW, GP], s1 + 6592)
        sin_ = at("sin_", [P, NPOW, GP], s1 + 7680)
        cos_ = at("cos_", [P, NPOW, GP], s1 + 8768)
        sm = at("sm", [P, 12, GP], s1 + 9856)
        assert s1 + 9856 + 768 <= R1 + 118272
        rest = at("rest", [P, GP * NCH // 2], s1 + 192)
        assert 192 + GP * NCH * 2 <= 4288 + 192
        toep = at("toep", [P, 2, GP, P], R1 + 101376)
        A0 = A_HI
        u_c = at("u_c", [P, SG, NU], A0)
        h_st = at("h_st", [P, 2, GP, NCH + 1], A0 + 17408)
        lags = at("lags", [SC, 2, GP, P], A0 + 17408)
        g_st = at("g_st", [P, 2, 4, NCH], A0 + 33920)
        g_tmp = at("g_tmp", [P, 4, NCH], A0 + 38016)
        in_ch = at("in_ch", [P, 2, GP, P], A0 + 40064)
        h_s = at("h_s", [P, 2, GP, DB], A0 + 56448)
        h_s2 = at("h_s2", [P, 2, GP, DB], A0 + 62464)
        h_end = at("h_end", [P, 2, GP], A0 + 63488)
        g_hi = at("g_hi", [P, 4, T], R1 + 42240, F32R)
        g_lo = at("g_lo", [P, 4, T], R1 + 59136, F32R)
        ident = at("ident", [P, P], CONST_END)
        C2_END = CONST_END + 512
        assert C2_END <= nc.sbuf_usable_end

        s5_in, in_evac = sem("s5_in"), sem("in_even_evacuated")
        s5_vec, s5_act = sem("s5_vec"), sem("s5_act")
        u_out, g_out = sem("u_out"), sem("g_out")
        turned_out_a = sem("in_ch_out_act")
        s5_act2, lags_ready = sem("s5_act2"), sem("lags_ready")
        dt_ready, rates_ready, sines_ready = sem("dt_ready"), sem("rates_ready"), sem("sines_ready")
        prepared = sem("s5_prepared")
        lags_done, lags_out = sem("lags_done"), sem("lags_out")
        turned, turned_out = sem("in_ch_turned"), sem("in_ch_out")
        toep_zero, toep_in, u_in = sem("toep_zero"), sem("toep_in"), sem("u_in")
        v_done, v_read, h_ready, y_done, y_read = (sem(n) for n in ("v_done", "v_read", "h_ready", "y_done", "y_read"))
        g_in, s5_out, hs_ready = sem("g_in"), sem("s5_out"), sem("hs_ready")
        const_set, cin = sem("const_set"), sem("cin")

        class Chain:

            def __init__(self, eng, sem):
                self.eng, self.sem, self.count, self.tail = eng, sem, {}, None

            def __call__(self, ins, signal=None):
                s = signal or self.sem
                ins.then_inc(s, 1)
                self.count[id(s)] = self.count.get(id(s), 0) + 1
                self.tail = (s, self.count[id(s)])

            def after(self):
                if self.tail:
                    self.eng.wait_ge(*self.tail)
                return self.eng

        def bc(ap, axis, n):
            ap = ap.unsqueeze(axis)
            shape = list(ap.shape)
            shape[axis] = n
            return ap.broadcast_to(shape)

        def s5_prepare(dve, c):
            TT_, TS, STT = dve.tensor_tensor, dve.tensor_scalar, dve.scalar_tensor_tensor
            lr, li = lam[:, 0], lam[:, 1]

            def tt(out, a, b, op, signal=None):
                c.after()
                c(TT_(out, a, b, op), signal)

            dve.wait_ge(s5_in, 16 * 6)
            dve.wait_ge(dt_ready, 1)
            tt(sm[:, 1], lr, sm[:, 0], ALU.mult)
            tt(sm[:, 2], li, sm[:, 0], ALU.mult)
            tt(rho[:], bc(sm[:, 1], 1, NPOW), bc(kvec[:], 2, GP), ALU.mult)
            tt(ang[:], bc(sm[:, 2], 1, NPOW), bc(kvec[:], 2, GP), ALU.mult)
            c.after(); c(TS(rnd[:], ang[:], 1 / (2 * math.pi), ROUND, ALU.mult, ALU.add))
            c.after(); c(TS(rnd[:], rnd[:], -ROUND, None, ALU.add))
            for part in TWO_PI:
                c.after(); c(STT(ang[:], rnd[:], -part, ang[:], ALU.mult, ALU.add))
            c.after(); c(TS(ang[:], ang[:], PI_BELOW, -PI_BELOW, ALU.min, ALU.max), rates_ready)
            tt(sm[:, 3], lr, lr, ALU.mult)
            tt(sm[:, 4], li, li, ALU.mult)
            tt(sm[:, 3], sm[:, 3], sm[:, 4], ALU.add)
            c.after(); c(dve.reciprocal(sm[:, 3], sm[:, 3]))
            dve.wait_ge(sines_ready, 1)
            tt(cos_[:], cos_[:], cos_[:], ALU.mult)
            c.after(); c(TS(cos_[:], cos_[:], -2.0, 1.0, ALU.mult, ALU.add))
            tt(pw[:, 0], rho[:], cos_[:], ALU.mult)
            tt(pw[:, 1], rho[:], sin_[:], ALU.mult)
            c.after(); c(dve.tensor_copy(mag8[:], rho[:, CH]))
            c.after(); c(TS(sm[:, 4], pw[:, 0, 1], -1.0, None, ALU.add))
            tt(sm[:, 5], sm[:, 4], lr, ALU.mult)
            tt(sm[:, 6], pw[:, 1, 1], li, ALU.mult)
            tt(sm[:, 5], sm[:, 5], sm[:, 6], ALU.add)
            tt(sm[:, 5], sm[:, 5], sm[:, 3], ALU.mult)
            tt(sm[:, 6], pw[:, 1, 1], lr, ALU.mult)
            tt(sm[:, 7], sm[:, 4], li, ALU.mult)
            tt(sm[:, 6], sm[:, 6], sm[:, 7], ALU.subtract)
            tt(sm[:, 6], sm[:, 6], sm[:, 3], ALU.mult)
            cre, cim = bc(sm[:, 5], 2, SC), bc(sm[:, 6], 2, SC)
            pb = prod[:, 0:GP * SC].rearrange("p (i c) -> p i c", c=SC)
            tt(bb[:, 0], cre, b_in[:, 0], ALU.mult)
            tt(pb, cim, b_in[:, 1], ALU.mult)
            tt(bb[:, 0], bb[:, 0], pb, ALU.subtract)
            tt(bb[:, 1], cre, b_in[:, 1], ALU.mult)
            tt(pb, cim, b_in[:, 0], ALU.mult)
            tt(bb[:, 1], bb[:, 1], pb, ALU.add)
            yield
            pr, pi = (bc(pw[:, r, 0:L].rearrange("p k i -> p i k"), 3, SC) for r in range(2))
            cr, ci = (bc(c_in[:, r], 2, L) for r in range(2))
            po = prod[:].rearrange("p (i k c) -> p i k c", k=L, c=SC)
            tt(out_st[:, 0], cr, pr, ALU.mult)
            tt(po, ci, pi, ALU.mult)
            tt(out_st[:, 0], out_st[:, 0], po, ALU.subtract)
            yield
            tt(out_st[:, 1], cr, pi, ALU.mult)
            tt(po, ci, pr, ALU.mult)
            c.after(); c(STT(out_st[:, 1].rearrange("p i k c -> p (i k c)"),
                             out_st[:, 1].rearrange("p i k c -> p (i k c)"), -1.0, prod[:], ALU.mult, ALU.subtract))
            yield
            dve.wait_ge(rel_out, 16)
            pr, pi = (bc(pw[:, r, L:NPOW].rearrange("p k i -> p i k"), 3, SC) for r in range(2))
            br, bi = (bc(bb[:, r], 2, CH) for r in range(2))
            pn = prod[:, 0:GP * CH * SC].rearrange("p (i k c) -> p i k c", k=CH, c=SC)
            tt(in_st[:, 0], br, pr, ALU.mult)
            tt(pn, bi, pi, ALU.mult)
            tt(in_st[:, 0], in_st[:, 0], pn, ALU.subtract)
            yield
            tt(in_st[:, 1], br, pi, ALU.mult)
            tt(pn, bi, pr, ALU.mult)
            tt(in_st[:, 1], in_st[:, 1], pn, ALU.add)
            yield
            c.after(); c(dve.memset(turn[:, 0, :, 0:1], 1.0))
            c.after(); c(dve.memset(turn[:, 1, :, 0:1], 0.0))
            c.after(); c(dve.tensor_copy(sm[:, 8], cos_[:, CH]))
            c.after(); c(dve.tensor_copy(sm[:, 9], sin_[:, CH]))
            n = 1
            while n < NCH:
                wr, wi = bc(sm[:, 8], 2, n), bc(sm[:, 9], 2, n)
                old = [turn[:, r, :, 0:n] for r in range(2)]
                new = [turn[:, r, :, n:2 * n] for r in range(2)]
                tp = rest[:, 0:GP * n].rearrange("p (i j) -> p i j", i=GP)
                tt(new[0], old[0], wr, ALU.mult)
                tt(tp, old[1], wi, ALU.mult)
                tt(new[0], new[0], tp, ALU.subtract)
                tt(new[1], old[0], wi, ALU.mult)
                tt(tp, old[1], wr, ALU.mult)
                tt(new[1], new[1], tp, ALU.add, prepared if 2 * n == NCH else None)
                if 2 * n < NCH:
                    tt(sm[:, 10], sm[:, 8], sm[:, 8], ALU.mult)
                    tt(sm[:, 11], sm[:, 9], sm[:, 9], ALU.mult)
                    tt(sm[:, 9], sm[:, 8], sm[:, 9], ALU.mult)
                    c.after(); c(TS(sm[:, 9], sm[:, 9], 2.0, None, ALU.mult))
                    tt(sm[:, 8], sm[:, 10], sm[:, 11], ALU.subtract)
                n *= 2
                if n in (32, 64):
                    yield

        def chunked(ap):
            return ap[:, 0:SEQ].rearrange("p (s j) -> p j s", s=CH)

        def stepped(ap):
            return ap[:, SEQ:T].rearrange("p (s b) -> p b s", s=DS)

        def vec_in_even(dve):
            c = Chain(dve, s5_vec)
            pieces = s5_prepare(dve, c)
            dve.wait_ge(load.act.sem, load.act.at("rstd_x"))
            u0 = LOOKBACK + FIRST_UNIT["in_even"] + 1
            JT = TT // CH
            for u in range(10):
                dve.wait_ge(unit_done, u0 + u)
                un = unit(u % 2)
                if u < 4:
                    for t in range(3):
                        n = JT if t < 2 else NCH - 2 * JT
                        dve.tensor_tensor(chunked(u_p[:, u])[:, t * JT:t * JT + n],
                                          un[:, t, 0:n * CH].rearrange("p (j s) -> p j s", s=CH),
                                          rstd[:, t * TT:t * TT + n * CH].rearrange("p (j s) -> p j s", s=CH), ALU.mult)
                    dve.tensor_tensor(stepped(u_p[:, u]), un[:, 2, TT - NS:TT].rearrange("p (b s) -> p b s", s=DS),
                                      rstd[:, SEQ:T].rearrange("p (b s) -> p b s", s=DS), ALU.mult).then_inc(in_evac, 1)
                elif u < 8:
                    dve.scalar_tensor_tensor(t3(q_t[:, u - 4]), un, 0.125, t3(rstd[:]), ALU.mult, ALU.mult
                                             ).then_inc(in_evac, 1)
                else:
                    dve.wait_ge(rel_out, 16)
                    dve.tensor_tensor(t3((k_t, v_t)[u - 8][:]), un, t3(rstd[:]), ALU.mult).then_inc(in_evac, 1)
                next(pieces, None)
            for _ in pieces:
                pass
            dve.wait_ge(in_evac, LOOKBACK + 10)
            return c

        def act_prepare(act):
            act.wait_ge(s5_in, 16 * 6)
            act.activation(sm[:, 0], lam[:, 2], ACT.Exp).then_inc(dt_ready, 1)
            act.wait_ge(rates_ready, 1)
            act.activation(sin_[:], ang[:], ACT.Sin).then_inc(s5_act, 1)
            act.activation(cos_[:], ang[:], ACT.Sin, scale=0.5).then_inc(s5_act, 1)
            act.wait_ge(s5_act, 2)
            act.activation(rho[:], rho[:], ACT.Exp).then_inc(sines_ready, 1)

        def pe_s5(pe):
            pe.wait_ge(prepared, 1)
            pe.wait_ge(in_evac, LOOKBACK + 10)
            for i in range(GP):
                for par in range(2):
                    rows = slice(par * 64, par * 64 + 64)
                    out = ps[0:SC, par * 4 + i // 4, (i % 4) * P:(i % 4 + 1) * P]
                    for r in range(2):
                        mm = pe.matmul(out, bb[rows, r, i], out_st[rows, r, i, 0:CH].rearrange("p k c -> p (k c)"),
                                       start=(r == 0), stop=(r == 1))
            mm.then_inc(lags_done, 1)
            pe.wait_ge(lags_ready, 1)
            for r in range(2):
                for i in range(GP):
                    mm = pe.transpose(ps[:, r * 4 + i // 4, (i % 4) * P:(i % 4 + 1) * P],
                                      in_st[:, r, i].rearrange("p s c -> p (s c)"), ident[:])
                mm.then_inc(turned, 1)
            pe.wait_ge(turned_out, 1)
            pe.wait_ge(turned_out_a, 1)
            pe.wait_ge(u_in, 16 * 16)
            def state_in(bank, r, i0, n, rows, cols, w, width):
                for i in range(i0, i0 + n):
                    for par in range(2):
                        out = ps[par * 64:par * 64 + 64, bank, w + (i - i0) * width:w + (i - i0 + 1) * width]
                        mm = pe.matmul(out, in_ch[rows, r, i, par * 64:par * 64 + 64], u_c[rows, 2 * i + par, cols],
                                       start=True, stop=True)
                return mm
            for r in range(2):
                mm = state_in(4, r, 0, GP, slice(64, P), slice(NCH, NU), r * P, DB)
            mm.then_inc(v_done, 1)
            def y_of(out, i, par, m, urhs, hr, hi):
                rows = slice(par * 64, par * 64 + 64)
                pe.matmul(out, toep[:, par, i, 0:m], urhs, start=True, stop=False)
                pe.matmul(out, out_st[rows, 0, i, 1:L].rearrange("p k c -> p (k c)")[:, 0:m], hr[rows], start=False, stop=False)
                return pe.matmul(out, out_st[rows, 1, i, 1:L].rearrange("p k c -> p (k c)")[:, 0:m], hi[rows],
                                 start=False, stop=True)

            def quarter_in(q):
                if q >= 2:
                    pe.wait_ge(v_read, q)
                for r in range(2):
                    mm = state_in(2 * (q % 2) + r, r, 4 * q, 4, slice(0, P), slice(0, NCH), 0, NCH)
                mm.then_inc(v_done, 1)

            for q in range(3):
                quarter_in(q)
            pe.wait_ge(toep_in, 16 * CH)
            for i in range(GP):
                for par in range(2):
                    mm = y_of(ps[0:64, 6 + par, i * DB:(i + 1) * DB], i, par, 64, u_c[:, 2 * i + par, NCH:NU],
                              h0[:, 0, i], h0[:, 1, i])
            mm.then_inc(y_done, 1)
            quarter_in(3)
            pe.wait_ge(v_read, 1)
            for q in range(4):
                pe.wait_ge(h_ready, q + 1)
                if q:
                    pe.wait_ge(y_read, 2 * q)
                for n in range(4):
                    for par in range(2):
                        i = 4 * q + n
                        mm = y_of(ps[:, 4 + 2 * (q % 2) + par, n * NCH:(n + 1) * NCH], i, par, P,
                                  u_c[:, 2 * i + par, 0:NCH], h_st[:, 0, i, 0:NCH], h_st[:, 1, i, 0:NCH])
                mm.then_inc(y_done, 1)

        def vec_s5(dve, c):
            TT_ = dve.tensor_tensor

            def tt(out, a, b, op, signal=None):
                c.after()
                c(TT_(out, a, b, op), signal)

            c.after(); c(dve.memset(toep[:], 0.0), toep_zero)
            dve.wait_ge(lags_done, 1)
            c.after(); c(dve.tensor_copy(lags[:, 0].rearrange("p (a b) n -> p a (b n)", a=4), ps[0:SC, 0:4]))
            tt(lags[:, 0, :, 0:SC], lags[:, 0, :, 0:SC], d_diag[:, 0:GP], ALU.add)
            dve.wait_ge(lags_out, 1)
            tt(lags[:, 1, :, 0:SC], lags[:, 1, :, 0:SC], d_diag[:, GP:SG], ALU.add, lags_ready)
            dve.wait_ge(turned, 1)
            c.after(); c(dve.tensor_copy(in_ch[:, 0].rearrange("p (a b) n -> p a (b n)", a=4), ps[:, 0:4]), turned_out)
            dve.wait_ge(v_done, 1)
            p4 = [bc(pw[:, r, DS], 2, DB) for r in range(2)]
            add = ps[:, 4, 0:2 * P].rearrange("p (r i b) -> p r i b", r=2, b=DB)
            tt(h_s[:, 0], h0[:, 0], p4[0], ALU.mult)
            tt(h_s2[:, 0], h0[:, 1], p4[1], ALU.mult)
            tt(h_s[:, 1], h0[:, 0], p4[1], ALU.mult)
            tt(h_s2[:, 1], h0[:, 1], p4[0], ALU.mult)
            tt(h_s[:, 0], h_s[:, 0], h_s2[:, 0], ALU.subtract)
            tt(h_s[:, 1], h_s[:, 1], h_s2[:, 1], ALU.add)
            tt(h_s[:], h_s[:], add, ALU.add, v_read)
            dve.wait_ge(toep_in, 16 * CH)
            c.after(); c(dve.memset(h_st[:, :, :, 0:1], 0.0))
            for q in range(4):
                i = slice(4 * q, 4 * q + 4)
                wr, wi = turn[:, 0, i], turn[:, 1, i]
                vr, vi = (ps[:, 2 * (q % 2) + r].rearrange("p (i j) -> p i j", i=4) for r in range(2))
                dve.wait_ge(v_done, q + 2)
                tt(g_st[:, 0], vr, wr, ALU.mult)
                tt(g_tmp[:], vi, wi, ALU.mult)
                tt(g_st[:, 0], g_st[:, 0], g_tmp[:], ALU.add)
                tt(g_st[:, 1], vi, wr, ALU.mult)
                tt(g_tmp[:], vr, wi, ALU.mult, v_read)
                tt(g_st[:, 1], g_st[:, 1], g_tmp[:], ALU.subtract)
                for r in range(2):
                    for n in range(4):
                        c.after()
                        c(dve.tensor_tensor_scan(g_st[:, r, n], mag8[:, 4 * q + n:4 * q + n + 1].broadcast_to([P, NCH]),
                                                 g_st[:, r, n], 0.0, ALU.mult, ALU.add))
                tt(h_st[:, 0, i, 1:], g_st[:, 0], wr, ALU.mult)
                tt(g_tmp[:], g_st[:, 1], wi, ALU.mult)
                tt(h_st[:, 0, i, 1:], h_st[:, 0, i, 1:], g_tmp[:], ALU.subtract)
                tt(h_st[:, 1, i, 1:], g_st[:, 1], wr, ALU.mult)
                tt(g_tmp[:], g_st[:, 0], wi, ALU.mult)
                tt(h_st[:, 1, i, 1:], h_st[:, 1, i, 1:], g_tmp[:], ALU.add, h_ready)
            c.after(); c(dve.tensor_copy(h_end[:], h_st[:, :, :, NCH]), hs_ready)

        def channel_rows(scratch, j0, n):
            return scratch.rearrange("(g c) t -> c g t", c=SC)[:, :, j0:j0 + n]

        def feature_rows(scratch):
            return scratch.rearrange("(k p) t -> p k t", p=P)

        def act_s5(act):
            c = Chain(act, s5_act2)
            act.wait_ge(in_evac, LOOKBACK + 10)
            act.wait_ge(unit_done, LOOKBACK + FIRST_UNIT["in_even"] + 10)
            act.dma_start(feature_rows(io["u_scratch"]), u_p[:]).then_inc(u_out, 16)
            act.wait_ge(u_out, 16)
            for s in range(CH):
                act.dma_start(u_c[SC * s:SC * s + SC, :, 0:NCH], channel_rows(io["u_scratch"], s * NCH, NCH)
                              ).then_inc(u_in, 16)
            for s in range(CH):
                act.dma_start(u_c[SC * s:SC * s + SC, :, NCH:NU],
                              channel_rows(io["u_scratch"], SEQ + (s % DS) * DB, DB)).then_inc(u_in, 16)
            act.wait_ge(toep_zero, 1)
            act.wait_ge(lags_done, 1)
            c(act.activation(lags[:, 1].rearrange("p (a b) n -> p a (b n)", a=4), ps[0:SC, 4:8], ACT.Copy), lags_out)
            act.wait_ge(lags_ready, 1)
            for s in range(CH):
                act.dma_start(toep[SC * s:SC * s + SC, :, :, SC * s:P], lags[:, :, :, 0:P - SC * s]).then_inc(toep_in, 16)
            act.wait_ge(turned, 2)
            c(act.activation(in_ch[:, 1].rearrange("p (a b) n -> p a (b n)", a=4), ps[:, 4:8], ACT.Copy), turned_out_a)
            act.wait_ge(y_done, 1)
            for par in range(2):
                c(act.activation(u_c[0:64, par:SG:2, NCH:NU],
                                 ps[0:64, 6 + par, 0:GP * DB].rearrange("p (i b) -> p i b", b=DB),
                                 ACT.Gelu_apprx_tanh), y_read)
            act_at_loads(act)
            for q in range(4):
                act.wait_ge(y_done, q + 2)
                for par in range(2):
                    c(act.activation(u_c[:, 8 * q + par:8 * q + 8:2, 0:NCH],
                                     ps[:, 4 + 2 * (q % 2) + par].rearrange("p (i j) -> p i j", i=4),
                                     ACT.Gelu_apprx_tanh), y_read)

            act.wait_ge(y_read, 10)
            for t in range(CH):
                act.dma_start(channel_rows(io["g_scratch"], t * NCH, NCH), u_c[SC * t:SC * t + SC, :, 0:NCH]
                              ).then_inc(g_out, 16)
            for t in range(DS):
                act.dma_start(channel_rows(io["g_scratch"], SEQ + t * DB, DB), u_c[SC * t:SC * t + SC, :, NCH:NU]
                              ).then_inc(g_out, 16)
            act.wait_ge(g_out, 16 * (CH + DS))
            act.dma_start(u_p[:], feature_rows(io["g_scratch"])).then_inc(g_in, 16)
            act.wait_ge(hs_ready, 1)
            act.dma_start(io["s5_prompt"], h_end[:]).then_inc(s5_out, 16)
            act.dma_start(io["s5_sample"], h_s[:]).then_inc(s5_out, 16)

        def act_s5_loads(act):
            for dst, name in ((lam, "s5_lam"), (b_in, "s5_b"), (c_in, "s5_c"), (kvec, "kvec"), (d_diag, "s5_d"), (h0, "s5_h0")):
                act.dma_start(dst[:], io[name]).then_inc(s5_in, 16)

        HD, NH, NKV = 64, 8, 2
        G = NH // NKV
        W = 128
        NB = SEQ // W
        RY = 3 * W
        ROW = 3200
        s2 = R1 + 77056
        bias_t = at("bias_t", [P, NH, 2 * W], s2)
        v_tok = at("v_tok", [P, NB + 1, P], s2 + 8192)
        prob = at("prob", [P, 2, NH, 2 * W], s2 + 12800)
        prob_t = at("prob_t", [P, NH, 2, W], s2 + 29184)
        prob_s = at("prob_s", [P, T], s2 + 12800)
        prob_st = at("prob_st", [P, NB + 1, P], s2 + 29184)
        st = s2 + 37376
        top = at("top", [P, 2, NH], st)
        den = at("den", [P, 2, NH], st + 64)
        sink_e = at("sink_e", [P, 2, NH], st + 128)
        sinks = at("sinks", [P, NH], A0 + 58560)
        sinks_s = at("sinks_s", [P, NKV], A0 + 58624)
        q_s = at("q_s", [P, G, NS], st + 256)
        own = at("own", [P, NKV, W + DS], A0 + 57472)
        c_k = at("c_k", [P, DB, W], A0 + 40064)
        c_v = at("c_v", [P, DB, P], A0 + 44160)
        other = at("other", [P, DB], A0 + 58656)
        rel = at("rel", [P, NH, RY], R1 + 33792)
        buckets = at("buckets", [33, RY], R1 + 33792 + 12288)
        table = at("table", [33, NH], R1 + 33792 + 13824)
        rel_in, rel_done, rel_read, rel_out, own_out = (sem(n) for n in (
            "rel_in", "rel_done", "rel_read", "rel_out", "own_out"))
        at_in, at_vec, at_act = sem("at_in"), sem("at_vec"), sem("at_act")
        sc_done, sc_read, top_ready, exp_done = sem("sc_done"), sem("sc_read"), sem("top_ready"), sem("exp_done")
        norm_done, pt_done, pt_read, o_done, o_read = (sem(n) for n in (
            "norm_done", "pt_done", "pt_read", "o_done", "o_read"))
        o_read_a, pt_read_s = sem("o_read_act"), sem("pt_read_sample")
        vt_done, vt_read, k_out = sem("vt_done"), sem("vt_read"), sem("k_out")
        skew = io["skew"]

        def act_bias_rows(act):
            act.dma_start(buckets[:], io["buckets"]).then_inc(rel_in, 16)
            act.dma_start(table[:], io["table"]).then_inc(rel_in, 16)

        def act_skew(act):
            act.wait_ge(rel_read, 1)
            act.dma_start(skew[0:P * ROW].rearrange("(p r) -> p r", r=ROW)[:, 0:NH * RY],
                          rel[:].rearrange("p h y -> p (h y)")).then_inc(rel_out, 16)

        def act_own_rows(act):
            act.wait_ge(rel_out, 16)
            for kv in range(NKV):
                for hh in range(G):
                    rows = skewed(W + DS)[0:DS, kv * G + hh]
                    act.dma_start(io["own_scratch"][hh, :, :, kv], bc(rows, 0, DB)).then_inc(own_out, 16)

        def pe_bias_rows(pe):
            pe.wait_ge(rel_in, 32)
            for h in range(NH):
                mm = pe.matmul(ps[:, h, 0:RY], table[:, h:h + 1].broadcast_to([33, P]), buckets[:], start=True, stop=True)
            mm.then_inc(rel_done, 1)

        def vec_bias_rows(dve):
            dve.wait_ge(rel_done, 1)
            dve.tensor_copy(rel[:], ps[:, :, 0:RY]).then_inc(rel_read, 1)

        def skewed(n):
            return skew[W - 1:W - 1 + P * (ROW - 1)].rearrange("(p r) -> p r", r=ROW - 1)[:, 0:NH * RY].rearrange(
                "p (h y) -> p h y", y=RY)[:, :, 0:n]

        def act_at_loads(act):
            act.wait_ge(h_ready, 4)
            act.wait_ge(own_out, 16 * NKV * G)
            act.dma_start(bias_t[:], skewed(2 * W)).then_inc(at_in, 16)
            act.dma_start(sinks[:], io["sinks"]).then_inc(at_in, 16)
            act.dma_start(sinks_s[:], io["sinks_s"]).then_inc(at_in, 16)
            act.dma_start(other[:], io["other"]).then_inc(at_in, 16)
            act.dma_start(c_k[:], io["c_k"]).then_inc(at_in, 16)
            act.dma_start(c_v[:], io["c_v"]).then_inc(at_in, 16)
            act.dma_start(own[:], io["own_scratch"].rearrange("h b s k y -> (h b s) k y")).then_inc(at_in, 16)
            act.wait_ge(in_evac, LOOKBACK + 10)
            act.dma_start(io["k_prompt"], k_t[:, SEQ - W:SEQ]).then_inc(k_out, 16)
            act.dma_start(io["v_prompt"], v_t[:, SEQ - W:SEQ]).then_inc(k_out, 16)
            for out, cache, new in ((io["k_sample"], io["c_k"], k_t), (io["v_sample"], io["c_vt"], v_t)):
                act.dma_start(out[:, :, 0:W - DS], cache[:, :, DS:W]).then_inc(k_out, 16)
                act.dma_start(out[:, :, W - DS:W], new[:, SEQ:T].rearrange("p (b s) -> p b s", s=DS)).then_inc(k_out, 16)

        AT_LOADS = 7
        K_OUTS = 6

        def pe_attention(pe):
            pe.wait_ge(y_read, 10)
            for n in range(NB + 1):
                w = W if n < NB else NS
                mm = pe.transpose(ps[0:w, n // 4, (n % 4) * P:(n % 4 + 1) * P], v_t[:, n * W:n * W + w], ident[:])
            mm.then_inc(vt_done, 1)
            pe.wait_ge(at_in, 16 * AT_LOADS)
            pe.wait_ge(vt_read, 2)
            for kv in range(NKV):
                rows = slice(kv * HD, kv * HD + HD)
                q = q_s[rows].rearrange("p h t -> p (h t)")
                if kv:
                    pe.wait_ge(sc_read, kv)
                for n in range(2):
                    pe.matmul(ps[:, n], q, c_k[rows, 4 * n:4 * n + 4].rearrange("p b m -> p (b m)"), start=True, stop=True)
                pe.matmul(ps[:, 2, 0:NS], q, k_t[rows, SEQ:T], start=True, stop=True).then_inc(sc_done, 1)
                pe.wait_ge(norm_done, kv + 1)
                if kv:
                    pe.wait_ge(o_read, kv)
                for n in range(NB + 1):
                    w = W if n < NB else NS
                    mm = pe.transpose(ps[0:w, 4 + n // 4, (n % 4) * P:(n % 4 + 1) * P], prob_s[:, n * W:n * W + w], ident[:])
                mm.then_inc(pt_done, 1)
                pe.wait_ge(pt_read_s, kv + 1)
                for n in range(NB):
                    pe.matmul(ps[rows, 7, 0:P], c_v[:, n, rows], prob_st[:, n], start=(n == 0), stop=False)
                pe.matmul(ps[rows, 7, 0:P], v_tok[0:NS, NB, rows], prob_st[0:NS, NB], start=False, stop=True
                          ).then_inc(o_done, 1)

            def scores(n):
                pe.wait_ge(sc_read, NKV + n)
                k0 = max(n - 1, 0) * W
                for h in range(NH):
                    rows = slice((h // G) * HD, (h // G) * HD + HD)
                    c0 = (h % 2) * 2 * W + (W if n == 0 else 0)
                    mm = pe.matmul(ps[:, h // 2, c0:(h % 2 + 1) * 2 * W], q_t[rows, h % G, n * W:(n + 1) * W],
                                   k_t[rows, k0:(n + 1) * W], start=True, stop=True)
                mm.then_inc(sc_done, 1)

            scores(0)
            scores(1)
            for n in range(NB):
                if n + 2 < NB:
                    scores(n + 2)
                pe.wait_ge(norm_done, NKV + n + 1)
                pe.wait_ge(o_read, NKV + n)
                if n:
                    pe.wait_ge(o_read_a, n)
                halves = (1,) if n == 0 else (0, 1)
                for h in range(NH):
                    for f in halves:
                        mm = pe.transpose(ps[:, 4 + h // 2, ((h % 2) * 2 + f) * W:((h % 2) * 2 + f + 1) * W],
                                          prob[:, n % 2, h, f * W:(f + 1) * W], ident[:])
                mm.then_inc(pt_done, 1)
                pe.wait_ge(pt_read, 2 * (n + 1))
                for kv in range(NKV):
                    rows = slice(kv * HD, kv * HD + HD)
                    for f in halves:
                        mm = pe.matmul(ps[rows, 4 + kv], v_tok[:, n - 1 + f, rows], prob_t[:, kv * G:kv * G + G, f],
                                       start=(f == halves[0]), stop=(f == 1))
                mm.then_inc(o_done, 1)

        def vec_attention(dve, c):
            TT_ = dve.tensor_tensor

            def tt(out, a, b, op, signal=None):
                c.after()
                c(TT_(out, a, b, op), signal)

            dve.wait_ge(vt_done, 1)
            c.after(); c(dve.tensor_copy(q_s[:], q_t[:, :, SEQ:T]))
            c.after(); c(dve.tensor_copy(v_tok[:, 0:NB].rearrange("p (a b) n -> p a (b n)", a=2), ps[:, 0:2]), vt_read)
            c.after(); c(dve.tensor_copy(v_tok[0:NS, NB], ps[0:NS, 2, 0:P]), vt_read)
            dve.wait_ge(at_in, 16 * AT_LOADS)
            for kv in range(NKV):
                dve.wait_ge(sc_done, kv + 1)
                old = prob_s[:, 0:SEQ].rearrange("p (b m) -> p b m", m=W)
                new = prob_s[:, SEQ:T].rearrange("p (b s) -> p b s", s=DS)
                tt(old, ps[:, 0:2].rearrange("p a (b m) -> p (a b) m", m=W), bc(own[:, kv, 0:W], 1, DB), ALU.add)
                tt(new, ps[:, 2, 0:NS].rearrange("p (b s) -> p b s", s=DS), bc(own[:, kv, W:W + DS], 1, DB), ALU.add, sc_read)
                tt(old, old, bc(other[:], 2, W), ALU.add)
                tt(new, new, bc(other[:], 2, DS), ALU.add)
                c.after(); c(dve.reduce_max(top[:, 0, kv:kv + 1], prob_s[:], AX_X))
                tt(top[:, 0, kv:kv + 1], top[:, 0, kv:kv + 1], sinks_s[:, kv:kv + 1], ALU.max)
                tt(sink_e[:, 0, kv:kv + 1], sinks_s[:, kv:kv + 1], top[:, 0, kv:kv + 1], ALU.subtract)
                c.after(); c(dve.tensor_scalar(top[:, 0, kv:kv + 1], top[:, 0, kv:kv + 1], -1.0, None, ALU.mult), top_ready)
                dve.wait_ge(exp_done, kv + 1)
                tt(den[:, 0, kv:kv + 1], den[:, 0, kv:kv + 1], sink_e[:, 0, kv:kv + 1], ALU.add)
                c.after(); c(dve.reciprocal(den[:, 0, kv:kv + 1], den[:, 0, kv:kv + 1]))
                c.after(); c(dve.tensor_scalar(prob_s[:], prob_s[:], den[:, 0, kv:kv + 1], None, ALU.mult), norm_done)
                dve.wait_ge(pt_done, kv + 1)
                c.after(); c(dve.tensor_copy(prob_st[:, 0:NB].rearrange("p (a b) n -> p a (b n)", a=2), ps[:, 4:6]))
                c.after(); c(dve.tensor_copy(prob_st[0:NS, NB], ps[0:NS, 6, 0:P]), pt_read_s)
                dve.wait_ge(o_done, kv + 1)
                rows = slice(kv * HD, kv * HD + HD)
                c.after(); c(dve.tensor_copy(q_t[rows, :, SEQ:T], ps[rows, 7, 0:P].rearrange("p (h t) -> p h t", h=G)), o_read)

            def soften(n):
                z = n % 2
                w0 = W if n == 0 else 0
                dve.wait_ge(sc_done, NKV + n + 1)
                if n >= 2:
                    dve.wait_ge(pt_done, NKV + n - 1)
                for f in range(2):
                    hs = slice(4 * f, 4 * f + 4)
                    tt(prob[:, z, hs, w0:], ps[:, 2 * f:2 * f + 2].rearrange("p a (h m) -> p (a h) m", h=2)[:, :, w0:],
                       bias_t[:, hs, w0:], ALU.add, sc_read if f else None)
                c.after(); c(dve.reduce_max(top[:, z], prob[:, z, :, w0:], AX_X))
                tt(top[:, z], top[:, z], sinks[:], ALU.max)
                tt(sink_e[:, z], sinks[:], top[:, z], ALU.subtract)
                c.after(); c(dve.tensor_scalar(top[:, z], top[:, z], -1.0, None, ALU.mult), top_ready)

            def take(n):
                dve.wait_ge(o_done, NKV + n + 1)
                rows = slice(0, HD)
                c.after(); c(dve.tensor_copy(q_t[rows, :, n * W:(n + 1) * W], ps[rows, 4].rearrange("p (h t) -> p h t", h=G)), o_read)

            soften(0)
            for n in range(NB):
                z, w0 = n % 2, W if n == 0 else 0
                if n + 1 < NB:
                    soften(n + 1)
                if n:
                    take(n - 1)
                dve.wait_ge(exp_done, NKV + n + 1)
                tt(den[:, z], den[:, z], sink_e[:, z], ALU.add)
                c.after(); c(dve.reciprocal(den[:, z], den[:, z]))
                tt(prob[:, z, :, w0:], prob[:, z, :, w0:], bc(den[:, z], 2, 2 * W - w0), ALU.mult, norm_done)
            take(NB - 1)

        def act_attention(act):
            c = Chain(act, at_act)
            for kv in range(NKV):
                act.wait_ge(top_ready, kv + 1)
                c(act.activation(sink_e[:, 0, kv:kv + 1], sink_e[:, 0, kv:kv + 1], ACT.Exp))
                c.after()
                c(act.activation(prob_s[:], prob_s[:], ACT.Exp, bias=top[:, 0, kv:kv + 1],
                                 accum_out=den[:, 0, kv:kv + 1]), exp_done)
            def exps(n):
                z, w0 = n % 2, W if n == 0 else 0
                act.wait_ge(top_ready, NKV + n + 1)
                c.after(); c(act.activation(sink_e[:, z], sink_e[:, z], ACT.Exp))
                for h in range(NH):
                    c.after()
                    c(act.activation(prob[:, z, h, w0:], prob[:, z, h, w0:], ACT.Exp, bias=top[:, z, h:h + 1],
                                     accum_out=den[:, z, h:h + 1]), exp_done if h == NH - 1 else None)

            exps(0)
            for n in range(NB):
                if n + 1 < NB:
                    exps(n + 1)
                act.wait_ge(pt_done, NKV + n + 1)
                f0 = 1 if n == 0 else 0
                for f in range(2):
                    src = ps[:, 4 + 2 * f:6 + 2 * f].rearrange("p a (h f m) -> p (a h) f m", h=2, f=2)
                    c(act.activation(prob_t[:, 4 * f:4 * f + 4, f0:], src[:, :, f0:], ACT.Copy), pt_read)
                act.wait_ge(o_done, NKV + n + 1)
                rows = slice(HD, P)
                c(act.activation(q_t[rows, :, n * W:(n + 1) * W], ps[rows, 5].rearrange("p (h t) -> p h t", h=G), ACT.Copy), o_read_a)

        glu_split, glu_done, sig_ready = sem("glu_split"), sem("glu_done"), sem("sig_ready")
        glu_act, glu_evac, mix_hi, mix_lo, glu_mul = (sem(n) for n in ("glu_act", "glu_evac", "mix_hi", "mix_lo", "glu_mul"))

        def natural(dst, src, k):
            return [(dst[:, k, 0:SEQ].rearrange("p (j s) -> p j s", s=CH), chunked(src[:, k])),
                    (dst[:, k, SEQ:T].rearrange("p (b s) -> p b s", s=DS), stepped(src[:, k]))]

        def act_glu(act):
            act.wait_ge(g_in, 16)
            act.wait_ge(o_read, NKV + NB)
            act.wait_ge(o_read_a, NB)
            for k in range(4):
                for d, s in natural(g_hi, u_p, k):
                    ins = act.activation(d, s, ACT.Copy)
                ins.then_inc(glu_act, 1)
            for k in range(4):
                act.activation(a_hi[:, 4 + k], q_t[:, k], ACT.Copy).then_inc(mix_hi, 1)
            for m in range(4):
                act.wait_ge(unit_done, LOOKBACK + FIRST_UNIT["glu"] + m + 1)
                if m:
                    act.wait_ge(glu_mul, m)
                act.activation(t3(sq[:, 0]), unit(m % 2), ACT.Sigmoid).then_inc(glu_evac, 1)
                act.wait_ge(glu_mul, m + 1)
                act.activation(a_hi[:, m], sq[:, 1], ACT.Copy).then_inc(mix_hi, 1)

        def vec_glu(dve, c):
            dve.wait_ge(g_in, 16)
            dve.wait_ge(s5_out, 32)
            for k in range(4):
                dve.wait_ge(glu_act, k + 1)
                for (d, s), (hi, _) in zip(natural(g_lo, u_p, k), natural(g_hi, u_p, k)):
                    ins = dve.tensor_tensor(d, s, hi.bitcast(F32), ALU.subtract)
                ins.then_inc(glu_split, 1)
            for k in range(4):
                dve.wait_ge(mix_hi, k + 1)
                dve.tensor_tensor(a_lo[:, 4 + k], q_t[:, k], a_hi[:, 4 + k].bitcast(F32), ALU.subtract).then_inc(mix_lo, 1)
            for m in range(4):
                dve.wait_ge(glu_evac, LOOKBACK + m + 1)
                dve.wait_ge(mix_lo, 4 + m)
                sig, out = sq[:, 0], sq[:, 1]
                dve.tensor_tensor(out[:, 0:SEQ].rearrange("p (j s) -> p j s", s=CH), chunked(u_p[:, m]),
                                  sig[:, 0:SEQ].rearrange("p (j s) -> p j s", s=CH), ALU.mult)
                dve.tensor_tensor(out[:, SEQ:T].rearrange("p (b s) -> p b s", s=DS), stepped(u_p[:, m]),
                                  sig[:, SEQ:T].rearrange("p (b s) -> p b s", s=DS), ALU.mult).then_inc(glu_mul, 1)
                dve.wait_ge(mix_hi, 4 + m + 1)
                dve.tensor_tensor(a_lo[:, m], out, a_hi[:, m].bitcast(F32), ALU.subtract).then_inc(mix_lo, 1)

        def pe_glu(pe):
            pe.sem_inc(glu_evac, LOOKBACK)
            pe.wait_ge(glu_split, 4)
            for m in range(4):
                if m % 2 == 0:
                    pe.wait_ge(w_ready, LOOKBACK + FIRST_BLOCK["glu"] + m // 2 + 1)
                pe.wait_ge(glu_evac, m + 1)
                pe_unit(pe, m // 2, m % 2, range(4), (g_hi, g_lo), wk=4 * (m % 2))
            pe.wait_ge(mix_lo, 8)

        HH = 8
        LEVELS = range(1, 8)
        SAMPLE_LEVELS = (1, 2)
        NC = SEQ // P
        c_out = at("c_out", [P, KC, T], R1)
        raw = at("raw", [P, 2, 4, T], R1 + 33792)
        o0 = R1 + 67584
        cum = at("cum", [P, T], o0)
        key = at("key", [P, T], o0 + 4224)
        lev = at("lev", [P, 2, T], o0 + 8448)
        vtok = at("vtok", [P, NC + 1, P], o0 + 16896)
        ktok = at("ktok", [P, NC + 1, P], o0 + 21504)
        att = at("att", [P, NC + 1, P], o0 + 26112)
        reset = at("reset", [P, T], o0 + 30720, U8)
        state = at("state", [P, 2, P], o0 + 31776)
        lb = at("lb", [P, 6, HH], o0 + 32800)
        one_less, log_less, log_lb, log_gap = (lb[:, j] for j in range(4))
        last = at("last", [P, NC + DB], o0 + 32992)
        gnorm = at("gnorm", [P, 1], o0 + 33056)
        own_seq = at("own_seq", [NS, DB], o0 + 33088)
        vdiag = at("vdiag", [NS, DB, P], o0 + 8448)
        qdec, kdec = sq[:, 0], sq[:, 1]
        state_s = at("state_s", [P, DB, P], R1 + 105600)
        masks = at("masks", [P, 8, P], C2_END, U8)
        assert C2_END + 1024 <= nc.sbuf_usable_end
        masks_in = at("masks_in", [P, 8, P], R1 + 33792)
        reset_in = at("reset_in", [P, T], R1 + 33792 + 4096)

        V = ["logsig", "gap", "query", "floor", "key", "logf", "cum", "diff1"]
        for _l in LEVELS:
            V += ([f"diff{_l + 1}"] if _l < 7 else []) + [f"left{_l}", f"right{_l}"]
            if _l == 1:
                V += ["diag", "diag_s"]
            if _l > 1:
                V += [f"pick{_l - 1}"] + ([f"pick_s{_l - 1}"] if _l - 1 in SAMPLE_LEVELS else [])
            V += {2: ["gate", "kd", "kds"], 3: ["qdec", "kdec"]}.get(_l, [])
        V += ["pick7", "vdiag"] + [f"state{_c}" for _c in range(1, NC + 1)]
        V += ["o_p", "o_s", "decay_s", "state_s", "mean_o", "scaled_o", "out"]
        A = ["abs1", "exp1", "ln1", "sig_q", "sig_g", "sig_f", "vtok", "vtok_s", "abs2", "exp2", "ln2"]
        for _l in LEVELS:
            A += [f"exp_l{_l}", f"exp_r{_l}"] + {1: ["ecum", "elast", "elast_s"], 3: ["ekd"], 5: ["ktok", "ktok_s"]}.get(_l, [])
        A += ["square_o", "ln_o", "rstd_o"]
        PE_ORDER = ("g0 vturn g1 g2 g3 g4 diag score1 g5 score2 g6 score3 g7 score4 kturn g8a score5 g8b score6 g9a "
                    "score7 g9b add0 add1 chunk0 chunk1 add2 chunk2 add3 chunk3 add4 chunk4 add5 chunk5 add6 chunk6 add7 "
                    "chunk7 sample g10 stat g11").split()
        VEC_ORDER = ("t0 floor t1 decay t2 level1 t3 t4 level2 gates t5 level3 decays t6 level4 t7 level5 level6 t8 level7 "
                     "last t9 states result t10 mean t11 out").split()
        T_ = []
        for _n in PE_ORDER:
            if _n == "sample":
                T_ += ["o", "add_s"]
            elif _n == "stat":
                T_ += ["stat_o"]
            elif not _n.startswith(("g", "chunk")):
                T_ += [_n]
        hv, ha, ht = Steps(sem("hgrn_vec"), V), Steps(sem("hgrn_act"), A), Steps(sem("hgrn_pe"), T_)
        he = Steps(sem("hgrn_evacuated"), [f"t{_n}" for _n in range(12)])
        hs_in, hs_out, hp_out, hc_in = sem("hs_in"), sem("hs_out"), sem("hp_out"), sem("hc_in")
        pick_turn, tile_done = sem("pick_turn"), sem("tile_done")
        lb_e, lb_s, lb_l, lb_r = sem("lb_e"), sem("lb_s"), sem("lb_l"), sem("lb_r")
        U_ODD = FIRST_UNIT["in_odd"]

        def head_row(dram, h):
            return dram[h] if isinstance(h, int) else dram[bass.ds(h, 1)].rearrange("a p n -> p (a n)")

        def blocks(ap, l, half, width=T):
            return ap[:, 0:width].rearrange("p (n f t) -> p n f t", f=2, t=1 << (l - 1))[:, :, half]

        def span(l):
            return T if l in SAMPLE_LEVELS else SEQ

        def pe_head_tile(pe, h, n, half=""):
            j, t = n // 3, n % 3
            ks = {"": range(KC), "a": range(KC // 2), "b": range(KC // 2, KC)}[half]
            if t == 0 and half != "b":
                pe.wait_ge(w_ready, h * 4 + (FIRST_BLOCK["in_odd"] + j + 1 + LOOKBACK))
            if half != "b":
                he.wait(pe, f"t{(n - 3) % 12}", h if n >= 3 else h - 1)
            cols = slice(t * TT, (t + 1) * TT)
            for k in ks:
                for i, (w, a) in enumerate(((w_hi, a_hi), (w_hi, a_lo), (w_lo, a_hi))):
                    mm = pe.matmul(ps[:, t, 0:TT], w[:, j % 2, k], a[:, k, cols], start=(k == 0 and i == 0),
                                   stop=(k == KC - 1 and i == 2))
            if half != "a":
                mm.then_inc(tile_done if t < 2 else unit_done, 1)

        def vec_head_tile(dve, h, n, b):
            j, t = n // 3, n % 3
            if t < 2:
                dve.wait_ge(tile_done, h * 8 + (2 * j + t + 1))
            else:
                dve.wait_ge(unit_done, h * 4 + (LOOKBACK + U_ODD + j + 1))
            cols = slice(t * TT, (t + 1) * TT)
            he.done(dve.tensor_tensor(raw[:, b, j, cols], ps[:, t, 0:TT], rstd[:, cols], ALU.mult), f"t{n}")

        CHS = 7

        def chunk_out(pair, c, w=P):
            return ps[:, pair + c // 4, (c % 4) * P:(c % 4) * P + w] if c < NC else ps[:, CHS, 0:w]

        def chunks_of(pair):
            return ps[:, pair:pair + 2].rearrange("p a (c t) -> p (a c) t", t=P)

        PAIR_OF = {1: 3, 2: 5, 3: 3, 4: 3, 5: 5, 6: 3, 7: 5}

        def pe_head(pe, h, b):
            q, v = raw[:, b, 0], raw[:, b, 2]
            free_of = {1: (ha, "vtok_s"), 2: (hv, "diag_s"), 3: (hv, "pick1"), 4: (hv, "pick3"), 5: (ha, "ktok_s"),
                       6: (hv, "pick4"), 7: (hv, "pick5")}

            def turn_all(src, pair, name):
                for c in range(NC + 1):
                    w = P if c < NC else NS
                    mm = pe.transpose(chunk_out(pair, c)[0:w], src[:, c * P:c * P + w], ident[:])
                ht.done(mm, name)

            def vturn():
                he.wait(pe, "t8", h)
                hv.wait(pe, "mean_o", h - 1)
                turn_all(v, 3, "vturn")

            def diag():
                hv.wait(pe, "key", h)
                ha.wait(pe, "vtok_s", h)
                for c in range(NC + 1):
                    w = P if c < NC else NS
                    cols = slice(c * P, c * P + w)
                    mm = pe.matmul(chunk_out(5, c, w)[0:w], key[:, cols], q[:, cols], start=True, stop=True)
                ht.done(mm, "diag")

            def score(l):
                x_ = lev[:, l % 2]
                hv.wait(pe, f"right{l}", h)
                steps, name = free_of[l]
                steps.wait(pe, name, h)
                for c in range(NC):
                    cols = slice(c * P, (c + 1) * P)
                    mm = pe.matmul(chunk_out(PAIR_OF[l], c), x_[:, cols], x_[:, cols], start=True, stop=True)
                if l in SAMPLE_LEVELS:
                    hv.wait(pe, "diag_s" if l == 1 else f"pick_s{l - 1}", h)
                    mm = pe.matmul(ps[0:NS, CHS, 0:NS], x_[:, SEQ:T], x_[:, SEQ:T], start=True, stop=True)
                ht.done(mm, f"score{l}")

            def kturn():
                hv.wait(pe, "kdec", h)
                hv.wait(pe, "pick_s2", h)
                turn_all(kdec, 5, "kturn")

            def chunk(c):
                if c == 0:
                    ha.wait(pe, "ktok_s", h)
                    hv.wait(pe, "pick7", h)
                pe.matmul(chunk_out(3, c), vtok[:, c], att[:, c], start=True, stop=(c == 0))
                if c:
                    hv.wait(pe, f"state{c}", h)
                    pe.matmul(chunk_out(3, c), state[:, c % 2], qdec[:, c * P:(c + 1) * P], start=False, stop=True)

            def add(c):
                if c == 0:
                    ha.wait(pe, "ktok_s", h)
                    hv.wait(pe, "pick7", h)
                if c >= 2:
                    hv.wait(pe, f"state{c - 1}", h)
                ht.done(pe.matmul(ps[:, 5 + c % 2, 0:P], ktok[:, c], vtok[:, c], start=True, stop=True), f"add{c}")

            def sample():
                pe.wait_ge(hs_in, h * 16 + 16)
                pe.matmul(ps[:, CHS, 0:NS], vtok[0:NS, NC], att[0:NS, NC, 0:NS], start=True, stop=True)
                for s in range(DB):
                    cols = slice(s * DS, (s + 1) * DS)
                    mm = pe.matmul(ps[:, CHS, cols], state_s[:, s], qdec[:, SEQ + s * DS:SEQ + (s + 1) * DS],
                                   start=False, stop=True, skip_group_check=True)
                ht.done(mm, "o")
                hv.wait(pe, "vdiag", h)
                hv.wait(pe, f"state{NC}", h)
                for f in range(2):
                    mm = pe.matmul(ps[:, 5 + f], ktok[0:NS, NC], vdiag[:, 4 * f:4 * f + 4].rearrange("p b v -> p (b v)"),
                                   start=True, stop=True)
                ht.done(mm, "add_s")

            def stat():
                ha.wait(pe, "square_o", h)
                for t, bank in enumerate((3, 4, CHS)):
                    mm = pe.matmul(ps[:, bank, 0:TT], ones[:], cum[:, t * TT:(t + 1) * TT], start=True, stop=True)
                ht.done(mm, "stat_o")

            pieces = dict(vturn=vturn, diag=diag, kturn=kturn, sample=sample, stat=stat)
            for l in LEVELS:
                pieces[f"score{l}"] = lambda l=l: score(l)
            for c in range(NC):
                pieces[f"add{c}"], pieces[f"chunk{c}"] = (lambda c=c: add(c)), (lambda c=c: chunk(c))
            return pieces

        def vec_head(dve, h, b):
            q, f, v, g = (raw[:, b, j] for j in range(4))
            TT_, STT = dve.tensor_tensor, dve.scalar_tensor_tensor

            def col(a):
                return a[:, bass.ds(h, 1)] if not isinstance(h, int) else a[:, h:h + 1]

            def step(name, fn, *args):
                hv.wait_last(dve, h)
                hv.done(fn(*args), name)

            def diff(l):
                if l > 2:
                    ht.wait(dve, f"score{l - 2}", h)
                n = span(l)
                whole = cum[:, 0:n].rearrange("p (n t) -> p n t", t=1 << l)
                ref = whole[:, :, (1 << (l - 1)) - 1:(1 << (l - 1))].broadcast_to(list(whole.shape))
                step(f"diff{l}", TT_, lev[:, l % 2, 0:n].rearrange("p (n t) -> p n t", t=1 << l), whole, ref, ALU.subtract)

            def pick(l):
                ht.wait(dve, f"score{l}", h)
                half = 1 << (l - 1)

                def right(ap):
                    return ap.rearrange("p c (n f t) -> p c n f t", f=2, t=half)[:, :, :, 1]

                hv.wait_last(dve, h)
                out, m = right(att[:, 0:NC]), right(bc(masks[:, l], 1, NC))
                src = right(chunks_of(PAIR_OF[l]))
                dve.sem_inc(pick_turn, 1)
                hv.done(dve.copy_predicated(out, m, src), f"pick{l}")
                if l in SAMPLE_LEVELS:
                    out = att[0:NS, NC, 0:NS].rearrange("p (n f t) -> p n f t", f=2, t=half)[:, :, 1]
                    m = masks[0:NS, l, 0:NS].rearrange("p (n f t) -> p n f t", f=2, t=half)[:, :, 1]
                    src = ps[0:NS, CHS, 0:NS].rearrange("p (n f t) -> p n f t", f=2, t=half)[:, :, 1]
                    hv.wait_last(dve, h)
                    dve.sem_inc(pick_turn, 1)
                    hv.done(dve.copy_predicated(out, m, src), f"pick_s{l}")

            soft = lev[:, 0]

            def floor():
                ha.wait(dve, "sig_f", h)
                step("logsig", STT, f, f, 0.0, soft, ALU.min, ALU.subtract)
                step("gap", dve.tensor_scalar, soft, f, col(log_gap), None, ALU.add)
                ha.wait(dve, "sig_q", h)
                step("query", TT_, q, q, qdec, ALU.mult)
                step("floor", dve.tensor_scalar, f, f, col(log_less), col(log_lb), ALU.add, ALU.max)
                step("key", dve.tensor_scalar, key[:], key[:], col(one_less), None, ALU.mult)

            def decay():
                ha.wait(dve, "ln2", h)
                step("logf", TT_, f, f, soft, ALU.add)
                step("cum", dve.tensor_tensor_scan, cum[:], reset[:], f, 0.0, ALU.mult, ALU.add)
                diff(1)

            def gates():
                ha.wait(dve, "sig_g", h)
                step("gate", TT_, g, g, kdec, ALU.mult)
                whole = cum[:, 0:SEQ].rearrange("p (c t) -> p c t", t=P)
                step("kd", TT_, kdec[:, 0:SEQ].rearrange("p (c t) -> p c t", t=P),
                     whole[:, :, P - 1:P].broadcast_to([P, NC, P]), whole, ALU.subtract)
                whole = cum[:, SEQ:T].rearrange("p (c t) -> p c t", t=DS)
                step("kds", TT_, kdec[:, SEQ:T].rearrange("p (c t) -> p c t", t=DS),
                     whole[:, :, DS - 1:DS].broadcast_to([P, DB, DS]), whole, ALU.subtract)

            def decays():
                ha.wait(dve, "ecum", h)
                step("qdec", TT_, qdec, qdec, q, ALU.mult)
                ha.wait(dve, "ekd", h)
                step("kdec", TT_, kdec, kdec, key[:], ALU.mult)

            def level(l):
                if l < 7:
                    diff(l + 1)
                n = span(l)
                ha.wait(dve, f"exp_r{l}", h)
                x_ = lev[:, l % 2]
                step(f"left{l}", TT_, blocks(x_, l, 0, n), blocks(x_, l, 0, n), blocks(key[:], l, 0, n), ALU.mult)
                step(f"right{l}", TT_, blocks(x_, l, 1, n), blocks(x_, l, 1, n), blocks(q, l, 1, n), ALU.mult)
                if l == 1:
                    ht.wait(dve, "diag", h)
                    step("diag", TT_, att[:, 0:NC], chunks_of(5), bc(ident[:], 1, NC), ALU.mult)
                    step("diag_s", TT_, att[0:NS, NC, 0:NS], ps[0:NS, CHS, 0:NS], ident[0:NS, 0:NS], ALU.mult)
                if l > 1:
                    pick(l - 1)

            def last_():
                pick(7)
                ha.wait(dve, "ktok_s", h)
                step("vdiag", TT_, vdiag[:], bc(vtok[0:NS, NC], 1, DB), bc(own_seq[:], 2, P), ALU.mult)

            def states():
                for c in range(NC):
                    ht.wait(dve, f"add{c}", h)
                    if c == 0:
                        step("state1", dve.tensor_copy, state[:, 1], ps[:, 5, 0:P])
                    else:
                        step(f"state{c + 1}", STT, state[:, (c + 1) % 2], state[:, c % 2], last[:, c:c + 1],
                             ps[:, 5 + c % 2, 0:P], ALU.mult, ALU.add)

            o, m = key, lev[:, 1]

            def result():
                ht.wait(dve, "o", h)
                step("o_p", dve.tensor_copy, o[:, 0:SEQ].rearrange("p (a n) -> p a n", a=2), ps[:, 3:5])
                step("o_s", dve.tensor_copy, o[:, SEQ:T], ps[:, CHS, 0:NS])
                dve.wait_ge(hs_in, h * 16 + 16)
                step("decay_s", TT_, state_s[:], state_s[:], bc(last[:, NC:], 2, P), ALU.mult)
                ht.wait(dve, "add_s", h)
                step("state_s", TT_, state_s[:], state_s[:], ps[:, 5:7].rearrange("p a (b v) -> p (a b) v", v=P), ALU.add)

            def mean():
                ht.wait(dve, "stat_o", h)
                hv.wait_last(dve, h)
                dve.tensor_scalar(t3(m)[:, 0:2], ps[:, 3:5, 0:TT], 1.0 / P, EPS, ALU.mult, ALU.add)
                hv.done(dve.tensor_scalar(t3(m)[:, 2], ps[:, CHS, 0:TT], 1.0 / P, EPS, ALU.mult, ALU.add), "mean_o")

            def out():
                ha.wait(dve, "rstd_o", h)
                step("scaled_o", TT_, o[:], o[:], m, ALU.mult)
                step("out", STT, c_out[:, h] if isinstance(h, int) else c_out[:, bass.ds(h, 1)].rearrange("p a t -> p (a t)"),
                     o[:], gnorm[:, 0:1], g, ALU.mult, ALU.mult)

            pieces = dict(floor=floor, decay=decay, gates=gates, decays=decays, last=last_, states=states, result=result, mean=mean, out=out)
            for l in LEVELS:
                pieces[f"level{l}"] = lambda l=l: level(l)
            return pieces

        def act_head(act, h, b):
            q, f, v, g = (raw[:, b, j] for j in range(4))
            soft = lev[:, 0]

            def step(name, *args, **kw):
                ha.wait_last(act, h)
                ha.done(act.activation(*args, **kw), name)

            he.wait(act, "t11", h)
            hv.wait(act, "mean_o", h - 1)
            step("abs1", soft, f, ACT.Abs)
            step("exp1", soft, soft, ACT.Exp, scale=-1.0)
            step("ln1", soft, soft, ACT.Ln, bias=1.0)
            step("sig_q", qdec, q, ACT.Sigmoid)
            step("sig_g", kdec, g, ACT.Sigmoid)
            hv.wait(act, "out", h - 1)
            step("sig_f", key[:], f, ACT.Sigmoid, scale=-1.0)
            ht.wait(act, "vturn", h)
            step("vtok", vtok[:, 0:NC], chunks_of(3), ACT.Copy)
            step("vtok_s", vtok[0:NS, NC], ps[0:NS, CHS, 0:P], ACT.Copy)
            load_log_exp(act)
            hv.wait(act, "gap", h)
            step("abs2", soft, soft, ACT.Abs)
            step("exp2", soft, soft, ACT.Exp, scale=-1.0)
            step("ln2", soft, soft, ACT.Ln, bias=1.0)
            if not isinstance(h, int) or h:
                act.wait_ge(hs_out, h * 16)
                act.wait_ge(hp_out, h * 16)
            act.dma_start(state_s[:].rearrange("p b v -> p (b v)"), head_row(io["h_in"], h)).then_inc(hs_in, 16)
            hv.wait(act, "query", h)
            hv.wait(act, "cum", h)
            for l in LEVELS:
                n = span(l)
                x_ = lev[:, l % 2]
                hv.wait(act, f"diff{l}", h)
                step(f"exp_l{l}", blocks(x_, l, 0, n), blocks(x_, l, 0, n), ACT.Exp, scale=-1.0)
                step(f"exp_r{l}", blocks(x_, l, 1, n), blocks(x_, l, 1, n), ACT.Exp)
                if l == 1:
                    step("ecum", qdec, cum[:], ACT.Exp)
                    step("elast", last[:, 0:NC], cum[:, P - 1:SEQ:P], ACT.Exp)
                    step("elast_s", last[:, NC:], cum[:, SEQ + DS - 1:T:DS], ACT.Exp)
                if l == 3:
                    hv.wait(act, "kds", h)
                    step("ekd", kdec, kdec, ACT.Exp)
                if l == 5:
                    ht.wait(act, "kturn", h)
                    step("ktok", ktok[:, 0:NC], chunks_of(5), ACT.Copy)
                    step("ktok_s", ktok[0:NS, NC], ps[0:NS, CHS, 0:P], ACT.Copy)
            hv.wait(act, f"state{NC}", h)
            act.dma_start(head_row(io["h_prompt"], h), state[:, NC % 2]).then_inc(hp_out, 16)
            hv.wait(act, "o_s", h)
            step("square_o", cum[:], key[:], ACT.Square)
            hv.wait(act, "state_s", h)
            act.dma_start(head_row(io["h_sample"], h), state_s[:].rearrange("p b v -> p (b v)")).then_inc(hs_out, 16)
            hv.wait(act, "mean_o", h)
            step("ln_o", lev[:, 1], lev[:, 1], ACT.Ln)
            step("rstd_o", lev[:, 1], lev[:, 1], ACT.Exp, scale=-0.5)

        def heads(turn):
            def run(eng):
                with eng.Fori(0, HH // 2 - 1) as i:
                    for b in range(2):
                        turn(eng, i * 2 + b, b, True)
                turn(eng, HH - 2, 0, True)
                turn(eng, HH - 1, 1, False)
            return run

        def pe_turn(pe, h, b, following):
            pieces = pe_head(pe, h, b)
            for name in PE_ORDER:
                if name in pieces:
                    pieces[name]()
                elif following:
                    pe_head_tile(pe, h + 1, int(name[1:].rstrip("ab")), name[1:].lstrip("0123456789"))

        def vec_turn(dve, h, b, following):
            pieces = vec_head(dve, h, b)
            for name in VEC_ORDER:
                if name in pieces:
                    pieces[name]()
                elif following:
                    vec_head_tile(dve, h + 1, int(name[1:]), 1 - b)

        def pe_heads(pe):
            for n in range(3, 12):
                pe_head_tile(pe, 0, n)
            heads(pe_turn)(pe)

        def vec_heads(dve):
            for n in range(12):
                vec_head_tile(dve, 0, n, 0)
            heads(vec_turn)(dve)

        def act_heads(act):
            heads(lambda act, h, b, following: act_head(act, h, b))(act)

        def act_lower_bound(act):
            act.wait_ge(lb_s, 1)
            act.activation(lb[:, 5], lb[:, 5], ACT.Exp).then_inc(lb_e, 1)
            act.wait_ge(lb_s, 2)
            act.activation(lb[:, 1], lb[:, 0], ACT.Ln).then_inc(lb_l, 1)
            act.activation(lb[:, 2], lb[:, 5], ACT.Ln).then_inc(lb_l, 1)

        def vec_lower_bound(dve):
            c = Chain(dve, lb_r)
            dve.wait_ge(hc_in, 16 * 5)
            c(dve.tensor_copy(masks[:], masks_in[:]))
            c.after(); c(dve.tensor_copy(reset[:], reset_in[:]))
            c.after(); c(dve.tensor_tensor(lb[:, 5], lb[:, 4], lb[:, 4], ALU.subtract), lb_s)
            dve.wait_ge(lb_e, 1)
            c.after(); c(dve.reciprocal(lb[:, 0], lb[:, 5]))
            c.after(); c(dve.tensor_tensor(lb[:, 5], lb[:, 5], lb[:, 0], ALU.mult))
            c.after(); c(dve.tensor_tensor(lb[:, 5], lb[:, 5], lb[:, 5], ALU.subtract))
            c.after(); c(dve.tensor_scalar(lb[:, 0], lb[:, 5], -1.0, 1.0, ALU.mult, ALU.add))
            c.after(); c(dve.tensor_scalar(lb[:, 5], lb[:, 5], LOG_FLOOR, 2.0 ** 50, ALU.max, ALU.mult), lb_s)
            dve.wait_ge(lb_l, 2)
            c.after(); c(dve.tensor_scalar(lb[:, 2], lb[:, 2], -50 * math.log(2.0), None, ALU.add))
            c.after(); c(dve.tensor_tensor(lb[:, 3], lb[:, 1], lb[:, 2], ALU.subtract))
            c.after()

        def act_hgrn_loads(act):
            for dst, name in ((reset_in[:], "reset"), (lb[:, 4], "lb"), (gnorm[:], "gnorm"), (own_seq[:], "own_seq"),
                              (masks_in[:], "masks")):
                act.dma_start(dst, io[name]).then_inc(hc_in, 16)

        out_hi, out_lo = sem("out_hi"), sem("out_lo")

        def act_out_split(act):
            act.wait_ge(unit_done, LOOKBACK + FIRST_UNIT["out_odd"])
            for k in range(KC):
                act.activation(a_hi[:, k], c_out[:, k], ACT.Copy).then_inc(out_hi, 1)

        def vec_out_split(dve):
            for k in range(KC):
                dve.wait_ge(out_hi, k + 1)
                dve.tensor_tensor(a_lo[:, k], c_out[:, k], a_hi[:, k].bitcast(F32), ALU.subtract).then_inc(out_lo, 1)

        load = Boundary("load", None, 0)
        mix0 = Boundary("mix0", 1, 2)
        end0 = Boundary("mlp0_end", 3, 4)
        mix1 = Boundary("mix1", 5, 6)
        end1 = Boundary("mlp1_end", 7, None)
        out_even, out_odd = OutProjection("out_even", mix0), OutProjection("out_odd", mix1)
        mlp0, mlp1 = Mlp("mlp0", mix0, end0), Mlp("mlp1", mix1, end1)
        ones_set = sem("ones_set")
        block = ctx.enter_context(nc.Block())

        def x_ready(n):
            return lambda eng, k: eng.wait_ge(x_in[k], 16 * n)

        @block.sync
        def _(sp):
            sp_weights(sp)

        @block.gpsimd
        def _(pool):
            pool.wait_ge(ones_set, 1)
            pool_weights(pool)

        @block.tensor
        def _(pe):
            pe.sem_inc(unit_done, LOOKBACK)
            pe.wait_ge(ones_set, 1)
            pe.wait_ge(consts_in, 32)
            pe_bias_rows(pe)
            pe.wait_ge(rel_read, 1)
            pe.sem_inc(in_evac, LOOKBACK)
            load.tensor(pe, pe_first_unit(pe, "in_even"))
            pe_projection(pe, "in_even", in_evac, started=True)
            pe_s5(pe)
            pe_attention(pe)
            pe_glu(pe)
            out_even.tensor(pe)
            mix0.tensor(pe, pe_first_unit(pe, "mlp0"))
            mlp0.tensor(pe)
            end0.tensor(pe, pe_first_unit(pe, "in_odd", tile_done))
            ht.prime(pe)
            pe_heads(pe)
            pe.wait_ge(out_lo, KC)
            out_odd.tensor(pe)
            mix1.tensor(pe, pe_first_unit(pe, "mlp1"))
            mlp1.tensor(pe)
            end1.tensor(pe)

        @block.vector
        def _(dve):
            dve.memset(ones[:], 1.0).then_inc(ones_set, 1)
            vec_bias_rows(dve)
            dve.wait_ge(consts_in, 32)
            load.vector(dve, x_ready(1))
            c = vec_in_even(dve)
            vec_s5(dve, c)
            vec_attention(dve, c)
            vec_glu(dve, c)
            dve.wait_ge(k_out, 16 * K_OUTS)
            out_even.vector(dve)
            mix0.vector(dve, x_ready(2))
            mlp0.vector(dve)
            end0.vector(dve)
            dve.wait_ge(x_saved, 16 * KC)
            vec_lower_bound(dve)
            end0.act.wait(dve, "rstd_x")
            he.prime(dve)
            hv.prime(dve)
            vec_heads(dve)
            vec_out_split(dve)
            out_odd.vector(dve)
            mix1.vector(dve, x_ready(3))
            mlp1.vector(dve)
            end1.vector(dve)

        @block.scalar
        def _(act):
            act.dma_start(gains[:], io["gains"]).then_inc(consts_in, 16)
            act.dma_start(ident[:], io["ident"]).then_inc(consts_in, 16)
            act_bias_rows(act)
            for k in range(KC):
                act.dma_start(x[:, k], io["x"][k]).then_inc(x_in[k], 16)
            act.wait_ge(consts_in, 32)
            load.scalar(act, x_ready(1))
            load.act.wait(act, "rstd_x")
            act_s5_loads(act)
            act_skew(act)
            act_prepare(act)
            act_own_rows(act)
            act_s5(act)
            act_attention(act)
            act_glu(act)
            act.wait_ge(mix_lo, 8)
            act.wait_ge(unit_done, LOOKBACK + FIRST_UNIT["out_even"])
            act.wait_ge(s5_out, 32)
            for k in range(KC):
                act.dma_start(x[:, k], io["x"][k]).then_inc(x_in[k], 16)
            out_even.scalar(act)
            mix0.scalar(act, x_ready(2))
            mlp0.scalar(act)
            end0.scalar(act, on_x=lambda e, k: e.dma_start(io["x_scratch"][k], x[:, k]).then_inc(x_saved, 16))
            act.wait_ge(x_saved, 16 * KC)
            end0.act.wait(act, "rstd_x")
            ha.prime(act)
            act_hgrn_loads(act)
            act_lower_bound(act)
            act_heads(act)
            hv.wait(act, "out", HH - 1)
            act.wait_ge(hs_out, 16 * HH)
            act.wait_ge(hp_out, 16 * HH)
            for k in range(KC):
                act.dma_start(x[:, k], io["x_scratch"][k]).then_inc(x_in[k], 16)
            act_out_split(act)
            out_odd.scalar(act)
            mix1.scalar(act, x_ready(3))
            mlp1.scalar(act)
            end1.scalar(act, on_x=lambda e, k: e.dma_start(io["y"][k], x[:, k]).then_inc(y_out, 16))
            act.wait_ge(y_out, 16 * KC)
            act.wait_ge(k_out, 16 * K_OUTS)
            act.wait_ge(s5_out, 32)
            act.wait_ge(hp_out, 16 * HH)
            act.wait_ge(hs_out, 16 * HH)


def relative_buckets():
    w = 128
    distance = 2 * w - 1 - np.arange(3 * w)
    inside = (distance >= 0) & (distance < w)
    n = np.maximum(distance, 0)
    large = 16 + (np.log(np.maximum(n, 16).astype(np.float32) / np.float32(16)) / np.float32(math.log(8))
                  * np.float32(16)).astype(np.int32)
    bucket = np.where(n < 16, n, np.minimum(large, 31))
    rows = np.zeros((33, 3 * w), np.float32)
    rows[bucket[inside], np.arange(3 * w)[inside]] = 1
    rows[32, ~inside] = -1e30
    return rows


def level_masks():
    s, t = np.arange(P)[:, None], np.arange(P)[None, :]
    out = np.zeros((P, 8, P), np.float32)
    for l in range(1, 8):
        h = 1 << (l - 1)
        out[:, l] = ((t & h) != 0) & ((s & h) == 0) & (s >> l == t >> l)
    return out


def weight_stream(w_in_even, w_glu, w_out_even, w_up, w_down, w_in_odd, w_out_odd, q_rows):
    def wide(w, c):
        return w[:, c:c + P].reshape(KC, P, P).transpose(1, 0, 2).reshape(P, KC * P)

    def halves(w, c):
        return np.concatenate([w[:, d:d + P].reshape(4, P, P).transpose(1, 0, 2) for d in (c, c + P)],
                              axis=1).reshape(P, KC * P)

    def mlp(up, down):
        out = []
        for g in range(GROUPS):
            out += [wide(up, (g * HID + j) * P) for j in range(HID)]
            out += [halves(down[g * HID * P:(g + 1) * HID * P], 2 * P * c) for c in range(4)]
        return out

    half = D // 2
    in_even = w_in_even[:, np.concatenate([np.arange(half), q_rows, np.arange(2 * half, 2 * half + 2 * P)])]
    out_even = w_out_even[np.concatenate([np.arange(half), q_rows])]
    blocks = [wide(in_even, n * P) for n in range(10)] + [halves(w_glu, 2 * P * c) for c in range(2)]
    blocks += [wide(out_even, n * P) for n in range(KC)] + mlp(w_up[0], w_down[0])
    blocks += [wide(w_in_odd, part * D + h * P) for h in range(KC) for part in range(4)]
    blocks += [wide(w_out_odd, n * P) for n in range(KC)] + mlp(w_up[1], w_down[1])
    assert len(blocks) == BLOCKS
    return np.stack(blocks)


def layout(i):
    def c(a):
        return np.ascontiguousarray(a)

    o = {}
    x = np.concatenate([i["x_prompt"].reshape(SEQ, D), i["x_sample"].reshape(NS, D)])
    o["x"] = c(x.T.reshape(KC, P, T))
    norms = [i[n][layer] for layer in range(2)
             for n in ("norm_mix_pre", "norm_mix_post", "norm_mlp_pre", "norm_mlp_post")]
    o["gains"] = c(np.stack(norms).reshape(8, KC, P).transpose(2, 0, 1))
    heads = np.array([[kv * 4 + hh for kv in range(2)] for hh in range(4)]).ravel()
    q_rows = (D // 2 + heads[:, None] * 64 + np.arange(64)).ravel()
    o["w"] = weight_stream(i["w_in_even"][0], i["s5_w_glu"][0], i["w_out_even"][0], i["w_up"], i["w_down"],
                           i["w_in_odd"][0], i["w_out_odd"][0], q_rows)
    step = np.broadcast_to(i["s5_log_step"][0][:, None], (32, 64))
    lam = np.stack([i["s5_lambda_re"][0], i["s5_lambda_im"][0], step])
    o["s5_lam"] = c(lam.reshape(3, 16, 2, 64).transpose(2, 3, 0, 1).reshape(P, 3, 16))
    b = np.stack([i["s5_b_re"][0], i["s5_b_im"][0]])
    o["s5_b"] = c(b.reshape(2, 16, 2, 64, 16).transpose(2, 3, 0, 1, 4).reshape(P, 2, 16, 16))
    cc = np.stack([i["s5_c_re"][0], i["s5_c_im"][0]]).transpose(0, 1, 3, 2)
    o["s5_c"] = c(cc.reshape(2, 16, 2, 64, 16).transpose(2, 3, 0, 1, 4).reshape(P, 2, 16, 16))
    d = i["s5_d"][0].reshape(16, 2, 16)
    diag = np.zeros((16, 32, 16), np.float32)
    for ch in range(16):
        diag[ch, :, ch] = d[:, :, ch].T.ravel()
    o["s5_d"] = diag
    h = np.stack([i["state_s5_re"][0], i["state_s5_im"][0]])
    o["s5_h0"] = c(h.reshape(2, DB, 16, 2, 64).transpose(3, 4, 0, 2, 1).reshape(P, 2, 16, DB))
    o["kvec"] = np.broadcast_to(np.array(list(range(9)) + list(range(7, -1, -1)), np.float32), (P, 17)).copy()
    o["ident"] = np.eye(P, dtype=np.float32)
    o["buckets"] = relative_buckets()
    o["table"] = np.concatenate([i["t5_bias_table"], np.ones((1, 8), np.float32)])
    sinks = i["swa_sinks"][0]
    o["sinks"] = np.broadcast_to(sinks, (P, 8)).copy()
    o["sinks_s"] = c(np.repeat(sinks.reshape(2, 4), NS, axis=1).T)
    other = np.full((4, DB, DS, DB), -1e30, np.float32)
    for s in range(DB):
        other[:, s, :, s] = 0
    o["other"] = other.reshape(P, DB)
    o["c_k"] = c(i["cache_swa_k"][0].transpose(2, 3, 0, 1).reshape(P, DB, P))
    o["c_vt"] = c(i["cache_swa_v"][0].transpose(2, 3, 0, 1).reshape(P, DB, P))
    o["c_v"] = c(i["cache_swa_v"][0].transpose(1, 0, 2, 3).reshape(P, DB, P))
    o["masks"] = level_masks()
    reset = np.ones((P, T), np.float32)
    reset[:, 0:SEQ:P] = 0
    reset[:, SEQ:T:DS] = 0
    o["reset"] = reset
    o["own_seq"] = (np.arange(NS)[:, None] // DS == np.arange(DB)).astype(np.float32)
    o["lb"] = c(i["hgrn_lb_param"][0].reshape(KC, P).T)
    o["gnorm"] = c(i["hgrn_gnorm"][0].reshape(P, 1))
    o["h_in"] = c(i["state_hgrn"][0].transpose(1, 2, 0, 3).reshape(KC, P, DB * P))
    return o


OUTPUTS = {"y": (KC, P, T), "s5_prompt": (P, 2, 16), "s5_sample": (P, 2, 16, DB),
           "k_prompt": (P, P), "v_prompt": (P, P), "k_sample": (P, DB, P), "v_sample": (P, DB, P),
           "h_prompt": (KC, P, P), "h_sample": (KC, P, DB * P)}
SCRATCH = {"skew": (P * 3200,), "own_scratch": (4, DB, DS, 2, P + DS), "u_scratch": (D // 2, T), "g_scratch": (D // 2, T), "x_scratch": (KC, P, T)}


def results(o):
    y = o["y"].reshape(D, T).T
    s5p = o["s5_prompt"].reshape(2, 64, 2, 16).transpose(2, 3, 0, 1).reshape(2, 1, 1, 32, 64)
    s5s = o["s5_sample"].reshape(2, 64, 2, 16, DB).transpose(2, 4, 3, 0, 1).reshape(2, 1, DB, 32, 64)
    kp, vp = (o[n].reshape(2, 64, P).transpose(2, 0, 1)[None, None] for n in ("k_prompt", "v_prompt"))
    ks, vs = (o[n].reshape(2, 64, DB, P).transpose(2, 3, 0, 1)[None] for n in ("k_sample", "v_sample"))
    hp = o["h_prompt"][None, None]
    hs = o["h_sample"].reshape(KC, P, DB, P).transpose(2, 0, 1, 3)[None]
    return tuple(np.ascontiguousarray(a) for a in (
        y[:SEQ].reshape(1, SEQ, D), y[SEQ:].reshape(DB, DS, D), kp, vp, ks, vs, s5p[0], s5p[1], s5s[0], s5s[1], hp, hs))


def kernel(**inputs):
    import concourse.bacc as bacc
    from concourse.bass_utils import run_bass_kernel_spmd

    nc = bacc.Bacc("TRN2", target_bir_lowering=False, num_devices=1)
    arrays = layout({name: np.asarray(a) for name, a in inputs.items()})
    io = {name: nc.dram_tensor(name, a.shape, mybir.dt.from_np(a.dtype), kind="ExternalInput").ap()
          for name, a in arrays.items()}
    for name, shape in OUTPUTS.items():
        io[name] = nc.dram_tensor(name, shape, F32, kind="ExternalOutput").ap()
    for name, shape in SCRATCH.items():
        io[name] = nc.dram_tensor(name, shape, F32, kind="Internal").ap()
    build_trunk(nc, io)
    run = run_bass_kernel_spmd(nc, [arrays], core_ids=[0])
    return results({name: run.results[0][name] for name in OUTPUTS})
```
